# Optimizing a Trainium2 kernel written in Bass

```python
import jax, jax.numpy as jnp
from jax import lax
import numpy as np

D_MODEL = 1024
BATCH = 1
SEQ = 512
DEPTH = 2

GRID_W = 64
CTX_LEN = 256
N_MIXERS = 2
N_A_LAYERS = (DEPTH + N_MIXERS - 1) // N_MIXERS
N_B_LAYERS = DEPTH // N_MIXERS

D_RNN = D_MODEL
CONV_W = 4
LRU_BLOCKS = 8
LRU_BLOCK = D_RNN // LRU_BLOCKS
LRU_C = 8.0

MLA_HEADS = 16
QK_NOPE = 64
QK_ROPE = 32
QK_DIM = QK_NOPE + QK_ROPE
V_DIM = 64
Q_LORA = 384
KV_LORA = 256
ROPE_FREQS = QK_ROPE // 4
ROPE_BASE = 10000.0
Q_BLOCK = 128
ATTN_SCALE = QK_DIM ** -0.5

N_EXPERTS = 16
D_EXPERT = 1024
CAPACITY_FACTOR = 2

EPS = 1e-6

kernel_name = "hybrid_rglru_mla_ecmoe_dit"

def rmsnorm(x, g):
    xf = x.astype(jnp.float32)
    y = xf * lax.rsqrt(jnp.mean(xf * xf, axis=-1, keepdims=True) + EPS)
    return (y * g.astype(jnp.float32)).astype(x.dtype)

def adaln(cvec, w, b):
    m = jax.nn.silu(cvec) @ w + b
    return jnp.split(m[..., None, :], 6, axis=-1)

def modulate(h, shift, scale):
    return h * (1 + scale) + shift

def axial_rope(rows):
    row = jnp.broadcast_to(jnp.arange(rows)[:, None], (rows, GRID_W)).reshape(-1)
    col = jnp.broadcast_to(jnp.arange(GRID_W)[None, :], (rows, GRID_W)).reshape(-1)
    pos = jnp.stack([row, col], axis=-1).astype(jnp.float32)
    freq = ROPE_BASE ** (-jnp.arange(ROPE_FREQS, dtype=jnp.float32) / ROPE_FREQS)
    ang = pos[:, :, None] * freq
    return jnp.cos(ang), jnp.sin(ang)

def apply_rope(x, cos, sin):
    xr = x.reshape(x.shape[:-1] + (2, 2, ROPE_FREQS))
    x1 = xr[..., 0, :]
    x2 = xr[..., 1, :]
    out = jnp.stack([x1 * cos - x2 * sin, x1 * sin + x2 * cos], axis=-2)
    return out.reshape(x.shape).astype(x.dtype)

def dwconv_centred(x, w, b):
    T = x.shape[1]
    xp = jnp.pad(x, ((0, 0), (CONV_W // 2, CONV_W - 1 - CONV_W // 2), (0, 0)))
    y = xp[:, 0:T] * w[0]
    for k in range(1, CONV_W):
        y = y + xp[:, k:k + T] * w[k]
    return y + b

def rglru_direction(xc, w_g, b_g, lam, h0, reverse):
    B, T, _ = xc.shape
    xb = xc.reshape(B, T, LRU_BLOCKS, LRU_BLOCK)
    g = jnp.einsum('btnk,gnkj->gbtnj', xb, w_g).reshape(2, B, T, D_RNN) + b_g[:, None, None, :]
    r = jax.nn.sigmoid(g[0].astype(jnp.float32))
    ig = jax.nn.sigmoid(g[1].astype(jnp.float32))
    log_a = -LRU_C * r * jax.nn.softplus(-lam.astype(jnp.float32))
    a = jnp.exp(log_a)
    u = jnp.sqrt(-jnp.expm1(2.0 * log_a)) * (ig * xc.astype(jnp.float32))

    def step(h, au):
        at, ut = au
        h = at * h + ut
        return h, h

    h_last, hs = lax.scan(step, h0, (jnp.moveaxis(a, 1, 0), jnp.moveaxis(u, 1, 0)), reverse=reverse)
    return jnp.moveaxis(hs, 0, 1), h_last

def rglru_mixer(h_lat, h_ctx, w_in, conv_w, conv_b, gate_w, gate_b, lam, w_out, need_ctx):
    def branches(h):
        z = h @ w_in
        return jax.nn.gelu(z[..., :D_RNN]), dwconv_centred(z[..., D_RNN:], conv_w, conv_b)

    B = h_lat.shape[0]
    g_ctx, xc_ctx = branches(h_ctx)
    g_lat, xc_lat = branches(h_lat)
    y_lat = 0.0
    y_ctx = 0.0
    for d in range(2):
        h0 = jnp.zeros((B, D_RNN), jnp.float32)
        yc, hc = rglru_direction(xc_ctx, gate_w[d], gate_b[d], lam[d], h0, reverse=(d == 1))
        yl, _ = rglru_direction(xc_lat, gate_w[d], gate_b[d], lam[d], hc, reverse=(d == 1))
        y_lat = y_lat + yl
        y_ctx = y_ctx + yc
    out_lat = (y_lat.astype(h_lat.dtype) * g_lat) @ w_out
    out_ctx = (y_ctx.astype(h_ctx.dtype) * g_ctx) @ w_out if need_ctx else None
    return out_lat, out_ctx

def mla_qkv(h, w_in, q_norm, kv_norm, w_uq, w_ukv, cos, sin):
    B, L, _ = h.shape
    z = h @ w_in
    cq = z[..., :Q_LORA]
    ckv = z[..., Q_LORA:Q_LORA + KV_LORA]
    kr = z[..., Q_LORA + KV_LORA:]
    q = (rmsnorm(cq, q_norm) @ w_uq).reshape(B, L, MLA_HEADS, QK_DIM)
    kv = (rmsnorm(ckv, kv_norm) @ w_ukv).reshape(B, L, MLA_HEADS, QK_NOPE + V_DIM)
    q_nope, q_rope = q[..., :QK_NOPE], q[..., QK_NOPE:]
    k_nope, v = kv[..., :QK_NOPE], kv[..., QK_NOPE:]
    if cos is not None:
        q_rope = apply_rope(q_rope, cos[:, None], sin[:, None])
        kr = apply_rope(kr, cos, sin)
    k_rope = jnp.broadcast_to(kr[:, :, None, :], (B, L, MLA_HEADS, QK_ROPE))
    return (jnp.concatenate([q_nope, q_rope], axis=-1),
            jnp.concatenate([k_nope, k_rope], axis=-1), v)

def attend(q, k, v):
    s = jnp.einsum('bqhd,bkhd->bhqk', q, k).astype(jnp.float32) * ATTN_SCALE
    p = jax.nn.softmax(s, axis=-1).astype(v.dtype)
    return jnp.einsum('bhqk,bkhd->bqhd', p, v)

def mla_mixer(h_lat, h_ctx, w_in, q_norm, kv_norm, w_uq, w_ukv, w_o, cos, sin, need_ctx):
    B, T, _ = h_lat.shape
    q_lat, k_lat, v_lat = mla_qkv(h_lat, w_in, q_norm, kv_norm, w_uq, w_ukv, cos, sin)
    q_ctx, k_ctx, v_ctx = mla_qkv(h_ctx, w_in, q_norm, kv_norm, w_uq, w_ukv, None, None)
    k_all = jnp.concatenate([k_lat, k_ctx], axis=1)
    v_all = jnp.concatenate([v_lat, v_ctx], axis=1)
    nb = T // Q_BLOCK
    qb = q_lat.reshape(B, nb, Q_BLOCK, MLA_HEADS, QK_DIM).swapaxes(0, 1)
    o = lax.map(lambda qq: attend(qq, k_all, v_all), qb)
    out_lat = o.swapaxes(0, 1).reshape(B, T, MLA_HEADS * V_DIM) @ w_o
    out_ctx = None
    if need_ctx:
        Lc = h_ctx.shape[1]
        out_ctx = attend(q_ctx, k_ctx, v_ctx).reshape(B, Lc, MLA_HEADS * V_DIM) @ w_o
    return out_lat, out_ctx

def ec_moe(h, router, w_up, w_down):
    B, T, _ = h.shape
    cap = CAPACITY_FACTOR * T // N_EXPERTS
    aff = jax.nn.softmax((h @ router).astype(jnp.float32), axis=-1)
    gate, idx = lax.top_k(jnp.swapaxes(aff, 1, 2), cap)
    bidx = jnp.arange(B)[:, None, None]
    xg = h[bidx, idx]
    up = jnp.einsum('becd,edf->becf', xg, w_up)
    hid = jax.nn.silu(up[..., :D_EXPERT]) * up[..., D_EXPERT:]
    y = jnp.einsum('becf,efd->becd', hid, w_down) * gate[..., None].astype(h.dtype)
    return jnp.zeros_like(h).at[bidx, idx].add(y)

def setup_inputs(seed: int = 0) -> dict:
    key = jax.random.key(seed)
    ks = jax.random.split(key, 32)
    f32 = jnp.float32
    nrm = lambda k, shape, s: jax.random.normal(k, shape, f32) * s
    a0 = jax.random.uniform(ks[12], (N_A_LAYERS, 2, D_RNN), f32, 0.9, 0.999)
    return {
        "x": nrm(ks[0], (BATCH, SEQ, D_MODEL), 1.0),
        "c": nrm(ks[1], (BATCH, D_MODEL), 1.0),
        "ctx": nrm(ks[2], (BATCH, CTX_LEN, D_MODEL), 1.0),
        "c_ctx": nrm(ks[3], (D_MODEL,), 1.0),
        "ada_w": nrm(ks[4], (DEPTH, D_MODEL, 6 * D_MODEL), 0.5 * D_MODEL ** -0.5),
        "ada_b": nrm(ks[5], (DEPTH, 6 * D_MODEL), 0.01),
        "norm_mix": 1.0 + nrm(ks[6], (DEPTH, D_MODEL), 0.01),
        "norm_ffn": 1.0 + nrm(ks[7], (DEPTH, D_MODEL), 0.01),
        "norm_final": 1.0 + nrm(ks[8], (D_MODEL,), 0.01),
        "lru_w_in": nrm(ks[9], (N_A_LAYERS, D_MODEL, 2 * D_RNN), D_MODEL ** -0.5),
        "lru_conv_w": nrm(ks[10], (N_A_LAYERS, CONV_W, D_RNN), CONV_W ** -0.5),
        "lru_conv_b": nrm(ks[11], (N_A_LAYERS, D_RNN), 0.01),
        "lru_gate_w": nrm(ks[13], (N_A_LAYERS, 2, 2, LRU_BLOCKS, LRU_BLOCK, LRU_BLOCK), LRU_BLOCK ** -0.5),
        "lru_gate_b": nrm(ks[14], (N_A_LAYERS, 2, 2, D_RNN), 0.01),
        "lru_lambda": jnp.log(a0) - jnp.log1p(-a0),
        "lru_w_out": nrm(ks[15], (N_A_LAYERS, D_RNN, D_MODEL), D_RNN ** -0.5),
        "mla_w_in": nrm(ks[16], (N_B_LAYERS, D_MODEL, Q_LORA + KV_LORA + QK_ROPE), D_MODEL ** -0.5),
        "mla_q_norm": 1.0 + nrm(ks[17], (N_B_LAYERS, Q_LORA), 0.01),
        "mla_kv_norm": 1.0 + nrm(ks[18], (N_B_LAYERS, KV_LORA), 0.01),
        "mla_w_uq": nrm(ks[19], (N_B_LAYERS, Q_LORA, MLA_HEADS * QK_DIM), Q_LORA ** -0.5),
        "mla_w_ukv": nrm(ks[20], (N_B_LAYERS, KV_LORA, MLA_HEADS * (QK_NOPE + V_DIM)), KV_LORA ** -0.5),
        "mla_w_o": nrm(ks[21], (N_B_LAYERS, MLA_HEADS * V_DIM, D_MODEL), (MLA_HEADS * V_DIM) ** -0.5),
        "moe_router": nrm(ks[22], (DEPTH, D_MODEL, N_EXPERTS), D_MODEL ** -0.5),
        "moe_w_up": nrm(ks[23], (DEPTH, N_EXPERTS, D_MODEL, 2 * D_EXPERT), D_MODEL ** -0.5),
        "moe_w_down": nrm(ks[24], (DEPTH, N_EXPERTS, D_EXPERT, D_MODEL), D_EXPERT ** -0.5),
    }

def reference(x, c, ctx, c_ctx, ada_w, ada_b, norm_mix, norm_ffn, norm_final,
              lru_w_in, lru_conv_w, lru_conv_b, lru_gate_w, lru_gate_b, lru_lambda, lru_w_out,
              mla_w_in, mla_q_norm, mla_kv_norm, mla_w_uq, mla_w_ukv, mla_w_o,
              moe_router, moe_w_up, moe_w_down):
    T = x.shape[1]
    ROWS = T // GRID_W
    cos, sin = axial_rope(ROWS)
    for i in range(DEPTH):
        need_ctx = i < DEPTH - 1
        s1, sc1, g1, s2, sc2, g2 = adaln(c, ada_w[i], ada_b[i])
        s1c, sc1c, g1c, s2c, sc2c, g2c = adaln(c_ctx, ada_w[i], ada_b[i])
        h_lat = modulate(rmsnorm(x, norm_mix[i]), s1, sc1)
        h_ctx = modulate(rmsnorm(ctx, norm_mix[i]), s1c, sc1c)
        j = i // N_MIXERS
        if i % N_MIXERS == 0:
            o_lat, o_ctx = rglru_mixer(h_lat, h_ctx, lru_w_in[j], lru_conv_w[j], lru_conv_b[j],
                                       lru_gate_w[j], lru_gate_b[j], lru_lambda[j], lru_w_out[j], need_ctx)
        else:
            o_lat, o_ctx = mla_mixer(h_lat, h_ctx, mla_w_in[j], mla_q_norm[j], mla_kv_norm[j],
                                     mla_w_uq[j], mla_w_ukv[j], mla_w_o[j], cos, sin, need_ctx)
        x = x + g1 * o_lat
        x = x + g2 * ec_moe(modulate(rmsnorm(x, norm_ffn[i]), s2, sc2),
                            moe_router[i], moe_w_up[i], moe_w_down[i])
        if need_ctx:
            ctx = ctx + g1c * o_ctx
            ctx = ctx + g2c * ec_moe(modulate(rmsnorm(ctx, norm_ffn[i]), s2c, sc2c),
                                     moe_router[i], moe_w_up[i], moe_w_down[i])
    return rmsnorm(x, norm_final)


_drawn_inputs = setup_inputs


def setup_inputs(seed=0):
    import zlib

    import numpy as np

    out = dict(_drawn_inputs(seed))
    spreads = {}
    factors = {'ctx': 2.748,
     'ada_b': 3.467,
     'norm_mix': 8.0,
     'norm_ffn': 8.0,
     'norm_final': 36.629,
     'lru_conv_b': 5.348,
     'lru_gate_b': 8.0,
     'mla_q_norm': 22.359,
     'mla_kv_norm': 24.216}
    for name, (base, spread) in spreads.items():
        noise = np.random.default_rng([zlib.crc32(name.encode()), seed]).standard_normal(out[name].shape)
        drawn = base * np.exp(spread * noise) if base else spread * noise
        out[name] = __import__('jax').numpy.asarray(drawn.astype(out[name].dtype))
    for name, factor in factors.items():
        out[name] = (out[name] * factor).astype(out[name].dtype)
    return out
```

```python
from contextlib import ExitStack

import numpy as np

import concourse.bass as bass
from concourse import mybir

ALU = mybir.AluOpType
ACT = mybir.ActivationFunctionType
F32 = mybir.dt.float32
U32 = mybir.dt.uint32
AX_X = mybir.AxisListType.X

P = 128
RING = 8
BANK = 512
EPS = 1e-6
LRU_C = 8.0
GRID_W = 64
ROPE_BASE = 10000.0


class Chain:

    def __init__(self, eng, sem):
        self.eng, self.sem, self.n = eng, sem, 0

    def step(self, ins):
        self.n = self.n + 1
        ins.then_inc(self.sem, 1)
        self.eng.wait_ge(self.sem, self.n)


def build(nc, x, c, ctx, c_ctx, ada_w, ada_b, norm_mix, norm_ffn, norm_final, lru_w_in, lru_conv_w, lru_conv_b,
          lru_gate_w, lru_gate_b, lru_lambda, lru_w_out, mla_w_in, mla_q_norm, mla_kv_norm, mla_w_uq, mla_w_ukv,
          mla_w_o, moe_router, moe_w_up, moe_w_down, rope, out):
    TL, D = x.shape[1], x.shape[2]
    TC = ctx.shape[1]
    T = TL + TC
    KD = D // P
    TLT, TT = TL // P, T // P
    L, E = moe_router.shape[0], moe_router.shape[2]
    F = moe_w_down.shape[2]
    CAPL, CAPC = 2 * TL // E, 2 * TC // E
    CAP = [CAPL + CAPC, CAPL]
    FFT = [TT, TLT]
    QL, KVL = mla_q_norm.shape[1], mla_kv_norm.shape[1]
    ROPE = mla_w_in.shape[2] - QL - KVL
    H = 16
    NOPE = mla_w_uq.shape[2] // H - ROPE
    QK = NOPE + ROPE
    VD = mla_w_ukv.shape[2] // H - NOPE
    HG = 4
    NG = H // HG
    KQ, KKV = QL // P, KVL // P
    FQ = ROPE // 4
    SCALE = float(QK) ** -0.5
    CONV = lru_conv_w.shape[1]
    PADL, PADR = CONV // 2, CONV - 1 - CONV // 2
    CX = TL + PADL + PADR
    W = CX + TC
    WP = W + 1
    MODW = 2 * D
    MZ = QL + KVL + ROPE
    MLA_K = [(0, 3), (3, 6), (6, 8)]
    assert (D, TL, TC, T, F) == (1024, 512, 256, 768, 1024) and CAPL % 8 == 0 and CAPC % 8 == 0 and WP == 772

    mods = nc.dram_tensor("mods", [L, 2, 6 * D], F32).ap()
    stream = nc.dram_tensor("stream", [T, D], F32).ap()
    normed = nc.dram_tensor("normed", [T, D], F32).ap()

    chunks, slot_loads = [], [0] * RING
    place = {}

    def chunk(name, slot):
        place[name] = (slot, slot_loads[slot] + 1)
        chunks.append((name, slot, slot_loads[slot]))
        slot_loads[slot] += 1

    free6 = [2, 3, 4, 5, 6, 7]
    turn = 0
    for k in range(KD):
        chunk(("ada", 0, k), k)
    for m in range(KD):
        chunk(("lru_in", (m + KD // 2) % KD), m)
    chunk(("gate", 0), 0)
    chunk(("gate", 1), 1)
    for g in range(1, 6):
        for k in range(KD):
            chunk(("ada", g, k), free6[turn % 6])
            turn += 1
    for j in range(4):
        chunk(("lru_out", j), free6[turn % 6])
        turn += 1
    head_chunks = list(chunks)
    moe_base = [None, None]
    NCH = 12
    LOOPS = E // 2
    moe_base[0] = list(slot_loads)
    slot_loads = [n + 3 * LOOPS for n in slot_loads]
    chunks = []
    for j in range(3):
        chunk(("mla_in", j), j)
    for j in range(KQ):
        chunk(("uq", j), 3 + j)
    for j in range(KKV):
        chunk(("ukv", j), 6 + j)
    for j in range(3):
        chunk(("w_o", j), j)
    chunk(("w_o", 3), 3)
    mla_chunks = list(chunks)
    moe_base[1] = list(slot_loads)

    with ExitStack() as es:
        def sb(name, shape, dt=F32, st=es):
            return st.enter_context(nc.sbuf_tensor("sb_" + name, shape, dt))

        def sem(name):
            return es.enter_context(nc.semaphore(name))

        wide = es.enter_context(nc.psum_tensor("wide", [P, 4, BANK], F32))
        duo = es.enter_context(nc.psum_tensor("duo", [P, 2, BANK], F32))
        turned = es.enter_context(nc.psum_tensor("turned", [P, 2, BANK], F32))

        ring = sb("ring", [P, RING, 2048])
        ident = sb("ident", [P, P])
        eps = sb("eps", [P, 1])
        rowsA = sb("rowsA", [P, P])
        rowsB = sb("rowsB", [P, P])
        pA = sb("pA", [P, 48])
        pB = sb("pB", [P, 96])
        modc = [sb("modc0", [P, 96]), sb("modc1", [P, 96])]
        cols = sb("cols", [P, 14, KD])
        router = sb("router", [P, L, KD, E])
        silu_c = sb("silu_c", [P, KD, 2])
        stat = sb("stat", [P, 3, TT])
        lam = sb("lam", [P, 8, 16])
        idx_t = sb("idx_t", [P, E], U32)
        gate_t = sb("gate_t", [P, E])
        mx = sb("mx", [P, 4, TT])
        marks = sb("marks", [P, 32])
        aff = sb("aff", [P, TT, E])
        aff2 = sb("aff2", [P, TLT, 48])
        affT = sb("affT", [48, TL])
        top_v = sb("top_v", [48, CAPL])
        top_i = sb("top_i", [48, CAPL], U32)
        top_f = sb("top_f", [48, CAPL])
        turn_in = sb("turn_in", [E, 2, CAP[0]])

        def phase(*tensors):
            st = ExitStack()
            made = [sb(n, s, d, st) for n, s, d in tensors]
            return st, made

        st, (areaA, areaB, areaC, areaD, areaE, gmix, rows0, rows1, modbias) = phase(
            ("areaA", [P, 8, WP], F32), ("areaB", [P, 8, WP], F32), ("areaC", [P, 8, WP], F32),
            ("areaD", [P, 8, WP], F32), ("areaE", [P, 4, WP], F32), ("gmix", [P, 2, D], F32),
            ("rows0", [P, P], F32), ("rows1", [P, P], F32), ("modbias", [2, MODW], F32))
        st.close()

        def flat(a, n, w):
            return a[:].rearrange("p a b -> p (a b)")[:, 0:n * w].rearrange("p (n w) -> p n w", n=n)

        st, (x_b, gmix1) = phase(("x_b", [P, TT, D], F32), ("gmix1", [P, D], F32))
        mla_keep = ExitStack()
        cqT, ckvT, krr, ropes, cqn, kraw, rtmp = [sb(n, s, F32, mla_keep) for n, s in (
            ("cqT", [P, KQ, TL]), ("ckvT", [P, KKV, T]), ("krr", [P, TT, ROPE]), ("ropes", [P, TLT, 2, 2 * FQ]),
            ("cqn", [P, 2, QL + KVL]), ("kraw", [P, 2, ROPE]), ("rtmp", [P, 4, HG * 2 * FQ]))]
        sub, (xn2, hT2) = phase(("xn2", [P, TT, D], F32), ("hT2", [P, KD, T], F32))
        sub.close()
        sub, (OT, qT, kT, V, qtok, ktok, prob, PT, asum) = phase(
            ("OT", [P, KD, TL], F32), ("qT", [QK, HG, TL], F32), ("kT", [QK, HG, T], F32),
            ("V", [P, TT, HG, VD], F32), ("qtok", [P, 2, HG, QK], F32), ("ktok", [P, 2, HG, QK], F32),
            ("prob", [P, 2, T], F32), ("PT", [P, 2, TT, TL], F32), ("asum", [P, 3, 8], F32))
        sub.close()
        sub, (_, xn3, hT3) = phase(("OTkeep", [P, KD, TL], F32), ("xn3", [P, TLT, D], F32), ("hT3", [P, KD, TL], F32))
        sub.close()
        mla_keep.close()
        st.close()

        st, (x_f, xo_f) = phase(("x_f", [P, TLT, D], F32), ("xo_f", [P, TLT, D], F32))
        xg, xgT, sg, hid, hidT, ye, mod_a, mod_b, gffn, idx_c, gate_c = [sb(n, s, d, st) for n, s, d in (
            ("xg", [P, 2, D], F32), ("xgT", [P, 2, KD, CAP[0]], F32), ("sg", [P, 2, BANK], F32),
            ("hid", [P, 2, BANK], F32), ("hidT", [P, 2, 4, CAP[0]], F32), ("ye", [P, 2, D], F32),
            ("mod_a", [P, KD, CAP[0]], F32), ("mod_b", [P, KD, CAP[0]], F32), ("gffn", [P, D], F32),
            ("idx_c", [P, 2], U32), ("gate_c", [P, 2], F32))]
        nf = sb("nf", [P, D], F32, st)
        st.close()

        landed = [sem(f"landed{s}") for s in range(RING)]
        used = [sem(f"used{s}") for s in range(RING)]
        s_const, s_parA, s_parB, s_rope, s_router = [sem(n) for n in ("s_const", "s_parA", "s_parB", "s_rope", "s_router")]
        s_partr, s_pcol, s_silu_c, s_lam, s_lamE = [sem(n) for n in ("s_partr", "s_pcol", "s_silu_c", "s_lam", "s_lamE")]
        s_ada, s_modev, s_modst, s_bias, s_modrow, s_modtr, s_modcol = [sem(n) for n in (
            "s_ada", "s_modev", "s_modst", "s_bias", "s_modrow", "s_modtr", "s_modcol")]
        s_x0 = [sem(f"s_x0{t}") for t in range(TT)]
        s_x = [sem(f"s_x{t}") for t in range(TT)]
        s_rms, s_xn, s_xtr, s_hTa, s_hTd = [sem(n) for n in ("s_rms", "s_xn", "s_xtr", "s_hTa", "s_hTd")]
        N0 = [0, TT, 2 * TT, 3 * TT, 3 * TT + TLT]
        s_z, s_gelu, s_ucopy, s_xc = [sem(n) for n in ("s_z", "s_gelu", "s_ucopy", "s_xc")]
        s_gmm, s_sig, s_ix, s_tanh, s_v, s_sqrt, s_scan, s_ysum, s_yg = [sem(n) for n in (
            "s_gmm", "s_sig", "s_ix", "s_tanh", "s_v", "s_sqrt", "s_scan", "s_ysum", "s_yg")]
        s_gmix = [sem("s_gmix0"), sem("s_gmix1")]
        s_o = [sem("s_o0"), sem("s_o1")]
        s_x1 = [sem("s_x1_0"), sem("s_x1_1")]
        s_st = [sem("s_st0"), sem("s_st1")]
        s_nst = [sem("s_nst0"), sem("s_nst1")]
        s_log = [sem("s_log0"), sem("s_log1")]
        s_sub = [sem("s_sub0"), sem("s_sub1")]
        s_aexp = [sem("s_aexp0"), sem("s_aexp1")]
        s_aff = [sem("s_aff0"), sem("s_aff1")]
        s_afft = [sem("s_afft0"), sem("s_afft1")]
        s_top = [sem("s_top0"), sem("s_top1")]
        s_topt = [sem("s_topt0"), sem("s_topt1")]
        s_sel = [sem("s_sel0"), sem("s_sel1")]
        s_idxc = [sem("s_idxc0"), sem("s_idxc1")]
        s_gath = [[sem(f"s_gath{i}{b}") for b in range(2)] for i in range(L)]
        s_xgtr = [sem("s_xgtr0"), sem("s_xgtr1")]
        s_xgT = [sem("s_xgT0"), sem("s_xgT1")]
        s_up = [sem("s_up0"), sem("s_up1")]
        s_silu = [sem("s_silu0"), sem("s_silu1")]
        s_hid = [sem("s_hid0"), sem("s_hid1")]
        s_hidtr = [sem("s_hidtr0"), sem("s_hidtr1")]
        s_hidT = [sem("s_hidT0"), sem("s_hidT1")]
        s_down = [sem("s_down0"), sem("s_down1")]
        s_gatec = [sem("s_gatec0"), sem("s_gatec1")]
        s_ye = [sem("s_ye0"), sem("s_ye1")]
        s_scat = [sem("s_scat0"), sem("s_scat1")]
        s_mz, s_mzs, s_cqn, s_cqtr, s_cqT, s_krr = [sem(n) for n in ("s_mz", "s_mzs", "s_cqn", "s_cqtr", "s_cqT", "s_krr")]
        s_q, s_qtok, s_qtr, s_qT, s_kv, s_V, s_ktok, s_ktr, s_kT = [sem(n) for n in (
            "s_q", "s_qtok", "s_qtr", "s_qT", "s_kv", "s_V", "s_ktok", "s_ktr", "s_kT")]
        s_S, s_max, s_exp, s_pn, s_ptr, s_PTd, s_PTa, s_av, s_OT, s_rs = [sem(n) for n in (
            "s_S", "s_max", "s_exp", "s_pn", "s_ptr", "s_PTd", "s_PTa", "s_av", "s_OT", "s_rs")]
        s_fin, s_out, s_nf = sem("s_fin"), sem("s_out"), sem("s_nf")
        s_dve, s_act, s_pool = sem("s_dve"), sem("s_act"), sem("s_pool")
        s_dloop = [sem("s_dloop0"), sem("s_dloop1"), sem("s_dloop2")]
        NCONST = 9

        def ring_at(name):
            return ring[:, place[name][0], :]

        def col(layer, v, what, k):
            return v * 48 + what * 8 + k

        B_CONV, B_CB, B_GB, B_LAM = 0, CONV * KD, CONV * KD + KD, CONV * KD + KD + 4 * KD
        B_QN = B_LAM + 2 * KD
        B_KVN = B_QN + KQ
        NB = B_KVN + KKV
        N_COL = [[0, 1], [2, 3], [4, 5], [6, None]]

        x_d = x.rearrange("b t d -> (b t) d")
        ctx_d = ctx.rearrange("b t d -> (b t) d")
        out_d = out.rearrange("b t d -> (b t) d")
        stages = [
            dict(x=flat(areaD, TT, D), xn=flat(areaA, TT, D), hT=flat(areaB, KD, T), n=TT, lay=0, sc=1, sh=0),
            dict(x=flat(areaD, TT, D), xn=flat(areaC, TT, D), hT=flat(areaA, KD, T), n=TT, lay=0, sc=4, sh=3),
            dict(x=x_b[:], xn=xn2[:], hT=hT2[:], n=TT, lay=1, sc=1, sh=0),
            dict(x=x_b[:], xn=xn3[:], hT=hT3[:], n=TLT, lay=1, sc=4, sh=3),
        ]
        XC, G, Y = areaD, areaC, areaB
        RT, IT, A = areaA[:, 0:4, :], areaA[:, 4:8, :], areaE[:]
        rounds = [(0, 0), (1, 0), (0, 1), (1, 1)]

        def seg(a, i):
            return a[:, 0:TL] if i == 0 else a[:, CX:CX + TC]

        block = es.enter_context(nc.Block())

        @block.sync
        def _(sp):
            for dst, src in (
                (rowsA[0:8], c.rearrange("b (k q) -> (b k) q", q=P)), (rowsA[8:16], c_ctx.rearrange("(k q) -> k q", q=P)),
                (rowsA[16:32], norm_mix.rearrange("l (k q) -> (l k) q", q=P)),
                (rowsA[32:48], norm_ffn.rearrange("l (k q) -> (l k) q", q=P)),
            ):
                sp.dma_start(dst, src).then_inc(s_parA, 16)
            for t in range(TT):
                src = x_d[t * P:(t + 1) * P, :] if t < TLT else ctx_d[(t - TLT) * P:(t - TLT + 1) * P, :]
                sp.dma_start(stages[0]["x"][:, t, :], src).then_inc(s_x0[t], 16)

            def load(name, slot, before):
                if before >= 1:
                    sp.wait_ge(used[slot], before)
                dst = ring[:, slot, :]
                if name[0] == "ada":
                    lay, g = divmod(name[1], 3)
                    src = ada_w[lay, name[2] * P:(name[2] + 1) * P, g * MODW:(g + 1) * MODW]
                elif name[0] == "lru_in":
                    dst = dst.rearrange("p (k n) -> p k n", k=KD)
                    src = lru_w_in[0].rearrange("(k p) n -> p k n", p=P)[:, :, name[1] * 256:(name[1] + 1) * 256]
                elif name[0] == "gate":
                    dst = dst.rearrange("p (n j) -> p n j", j=P)
                    src = lru_gate_w[0, name[1]].rearrange("g n k j -> k (g n) j")
                elif name[0] in ("lru_out", "w_o"):
                    dst = dst.rearrange("p (k n) -> p k n", k=2)
                    src = (lru_w_out if name[0] == "lru_out" else mla_w_o)[0]
                    src = src.rearrange("(k p) n -> p k n", p=P)[:, 2 * name[1]:2 * name[1] + 2, :]
                elif name[0] == "mla_in":
                    k0, k1 = MLA_K[name[1]]
                    dst = dst[:, 0:(k1 - k0) * MZ].rearrange("p (k n) -> p k n", n=MZ)
                    src = mla_w_in[0].rearrange("(k p) n -> p k n", p=P)[:, k0:k1, :]
                elif name[0] == "uq":
                    dst, src = dst[:, 0:H * QK], mla_w_uq[0, name[1] * P:(name[1] + 1) * P, :]
                elif name[0] == "ukv":
                    src = mla_w_ukv[0, name[1] * P:(name[1] + 1) * P, :]
                sp.dma_start(dst, src).then_inc(landed[slot], 16)

            def experts(lay):
                base = moe_base[lay]
                up = moe_w_up[lay].rearrange("e (k p) (s h n) -> e p k s h n", p=P, s=2, h=2)
                down = moe_w_down[lay].rearrange("e (k p) n -> e p k n", p=P)
                with sp.Fori(0, LOOPS) as i:
                    for n in range(2 * NCH):
                        b, j, slot, lap = n // NCH, n % NCH, n % RING, n // RING
                        sp.wait_ge(used[slot], i * 3 + (base[slot] + lap))
                        e = i * 2 + b
                        if j < 8:
                            h, s, q = j // 4, j % 4 // 2, j % 2
                            dst = ring[:, slot, :].rearrange("p (k n) -> p k n", k=4)
                            sp.dma_start(dst, up[e, :, 4 * q:4 * q + 4, s, h, :]).then_inc(landed[slot], 16)
                        else:
                            dst = ring[:, slot, :].rearrange("p (k n) -> p k n", k=2)
                            sp.dma_start(dst, down[e, :, (j - 8) * 2:(j - 8) * 2 + 2, :]).then_inc(landed[slot], 16)

            for n, (name, slot, before) in enumerate(head_chunks):
                load(name, slot, before)
                if n == 7:
                    for dst, src in (
                        (rowsB[B_CONV:B_CB], lru_conv_w.rearrange("a w (k q) -> (a w k) q", q=P)),
                        (rowsB[B_CB:B_GB], lru_conv_b.rearrange("a (k q) -> (a k) q", q=P)),
                        (rowsB[B_GB:B_LAM], lru_gate_b.rearrange("a d g (k q) -> (a d g k) q", q=P)),
                        (rowsB[B_LAM:B_QN], lru_lambda.rearrange("a d (k q) -> (a d k) q", q=P)),
                        (rowsB[B_QN:B_KVN], mla_q_norm.rearrange("a (k q) -> (a k) q", q=P)),
                        (rowsB[B_KVN:NB], mla_kv_norm.rearrange("a (k q) -> (a k) q", q=P)),
                    ):
                        sp.dma_start(dst, src).then_inc(s_parB, 16)
                    for lay in range(L):
                        sp.dma_start(router[:, lay], moe_router[lay].rearrange("(k p) e -> p k e", p=P)).then_inc(s_router, 16)
            experts(0)
            for name, slot, before in mla_chunks:
                load(name, slot, before)
            experts(1)

        @block.tensor
        def _(pe):
            mm = nc.tensor.matmul

            def arrived(name):
                slot, n = place[name]
                pe.wait_ge(landed[slot], 16 * n)

            def turn(dst, src, plain=False):
                n = src.shape[0]
                if plain:
                    return mm(dst, src, ident[0:n, 0:n], start=True, stop=True)
                return nc.tensor.transpose(dst, src, ident[0:n, 0:n])

            def ada(i, owed=None):
                if i >= 1:
                    pe.wait_ge(s_modev, i)
                for k in range(KD):
                    arrived(("ada", i, k))
                    w = ring_at(("ada", i, k))
                    for n in range(4):
                        ins = mm(wide[0:2, n, :], silu_c[:, k, :], w[:, n * BANK:(n + 1) * BANK],
                                 start=k == 0, stop=k == KD - 1)
                        if owed and n == 0:
                            ins.then_inc(owed, 1)
                            owed = None
                    ins.then_inc(used[place[("ada", i, k)][0]], 1)

            def turn_mods(i, n):
                pe.wait_ge(s_modrow, 32 * (i + 1))
                rows = (rows0, rows0, rows1)[i]
                turn(duo[:, 0, 0:n], rows[0:n, :]).then_inc(s_modtr, 1)

            def turn_tile(s, t, owed=None):
                pe.wait_ge(s_xn, N0[s] + t + 1)
                for half, s_ev in ((0, s_hTa), (1, s_hTd)):
                    if t >= 1:
                        pe.wait_ge(s_ev, N0[s] + t)
                    for k in range(4):
                        f = (4 * half + k) * P
                        ins = turn(turned[:, half, k * P:(k + 1) * P], stages[s]["xn"][:, t, f:f + P])
                        if owed:
                            ins.then_inc(owed, 1)
                            owed = None
                    ins.then_inc(s_xtr, 1)

            pe.wait_ge(s_const, NCONST)
            pe.wait_ge(s_parA, 64)
            turn(turned[:, 0, 0:48], rowsA[0:48, :]).then_inc(s_partr, 1)
            pe.wait_ge(s_silu_c, 1)
            ada(0)
            pe.wait_ge(s_parB, 96)
            turn(turned[:, 1, 0:NB], rowsB[0:NB, :]).then_inc(s_partr, 1)
            turn_mods(0, 32)
            pe.wait_ge(s_pcol, 2)
            for t in range(TT):
                turn_tile(0, t)

            pe.wait_ge(s_hTa, TT)
            pe.wait_ge(s_hTd, TT)
            pe.wait_ge(s_modev, 1)
            hT = stages[0]["hT"]
            owed = None
            for q in range(2 * KD):
                name = ("lru_in", (q // 2 + KD // 2) % KD)
                arrived(name)
                w = ring_at(name).rearrange("p (k n) -> p k n", k=KD)[:, :, (q % 2) * P:(q % 2 + 1) * P]
                if q >= 2:
                    if q - 2 < KD:
                        pe.wait_ge(s_ucopy, q - 1)
                    else:
                        pe.wait_ge(s_gelu, q - 1 - KD)
                b = 2 * (q % 2)
                for k in range(KD):
                    first = mm(wide[:, b, :], w[:, k, :], hT[:, k, 0:TL], start=k == 0, stop=k == KD - 1)
                    if owed and k == 0:
                        first.then_inc(owed, 1)
                        owed = None
                    ins = mm(wide[:, b + 1, 0:TC], w[:, k, :], hT[:, k, TL:T], start=k == 0, stop=k == KD - 1)
                ins.then_inc(s_z, 1)
                if q % 2:
                    owed = used[place[name][0]]

            def gates(r, owed=None):
                d, half = rounds[r]
                arrived(("gate", d))
                w = ring_at(("gate", d)).rearrange("p (n j) -> p n j", j=P)
                for jj in range(4):
                    n, u = 4 * half + jj, 4 * r + jj
                    pe.wait_ge(s_xc, n + 1)
                    for g, banks in ((0, turned), (1, duo)):
                        if u >= 1:
                            pe.wait_ge(s_sig, 2 * (u - 1) + g + 1)
                        ins = mm(banks[:, 0, :], w[:, g * KD + n, :], seg(XC[:, n, :], 0), start=True, stop=True)
                        if owed:
                            ins.then_inc(owed, 1)
                            owed = None
                        mm(banks[:, 1, 0:TC], w[:, g * KD + n, :], seg(XC[:, n, :], 1), start=True, stop=True).then_inc(s_gmm, 1)

            gates(0, owed)
            pe.wait_ge(s_gelu, KD)
            ada(1)
            gates(1)
            ada(2)
            gates(2)
            ada(3, used[place[("gate", 0)][0]])
            gates(3)
            ada(4, used[place[("gate", 1)][0]])
            ada(5)
            pe.wait_ge(s_sig, 32)
            turn_mods(1, 96)
            pe.wait_ge(s_modcol, 2)
            turn_mods(2, 96)

            def out_project(lay, s, lhs, names):
                n_t = FFT[lay]
                for step in range(n_t + 2):
                    if step < n_t:
                        t = step
                        if t >= 2:
                            pe.wait_ge(s_x1[lay], t - 1)
                        b = 2 * (t % 2)
                        for k in range(KD):
                            if t == 0 and k % 2 == 0:
                                arrived(names[k // 2])
                            w = ring_at(names[k // 2]).rearrange("p (k n) -> p k n", k=2)[:, k % 2, :]
                            for n in range(2):
                                ins = mm(wide[:, b + n, :], lhs(k, t), w[:, n * BANK:(n + 1) * BANK],
                                         start=k == 0, stop=k == KD - 1)
                            if t == n_t - 1 and k % 2 and k < KD - 1:
                                ins.then_inc(used[place[names[k // 2]][0]], 1)
                        ins.then_inc(s_o[lay], 1)
                    if 1 <= step <= n_t:
                        turn_tile(s, step - 1, used[place[names[3]][0]] if step == n_t else None)
                    if step >= 2:
                        t = step - 2
                        pe.wait_ge(s_hTa, N0[s] + t + 1)
                        pe.wait_ge(s_hTd, N0[s] + t + 1)
                        for k in range(KD):
                            ins = mm(duo[:, 0, t * E:(t + 1) * E], stages[s]["hT"][:, k, t * P:(t + 1) * P],
                                     router[:, lay, k, :], start=k == 0, stop=k == KD - 1)
                        ins.then_inc(s_log[lay], 1)

            def turn_choice(lay):
                pe.wait_ge(s_aff[lay], 1)
                for t in range(TLT):
                    ins = turn(turned[0:48, 0, t * P:(t + 1) * P], aff2[:, t, :])
                ins.then_inc(s_afft[lay], 1)
                pe.wait_ge(s_top[lay], 1)
                for i in range(2):
                    ins = turn(duo[0:CAP[lay], 1, i * E:(i + 1) * E], turn_in[:, i, 0:CAP[lay]])
                ins.then_inc(s_topt[lay], 1)

            def experts(lay):
                M = CAP[lay]
                base = moe_base[lay]

                def turn_rows(e, pair, b, part):
                    if part == 0:
                        pe.wait_ge(s_gath[lay][b], pair * 16 + 16)
                    pe.wait_ge(s_hidT[lay], e * 2 + (1 + part))
                    for k in range(4):
                        ins = turn(turned[:, part, k * M:(k + 1) * M], xg[0:M, b, (4 * part + k) * P:(4 * part + k + 1) * P],
                                   plain=k == 0 and M <= 64)
                    ins.then_inc(s_xgtr[lay], 1)

                def body(i, last):
                    for b in range(2):
                        e = i * 2 + b

                        def slot_of(j):
                            n = b * NCH + j
                            return n % RING, n // RING

                        def here(j):
                            slot, lap = slot_of(j)
                            pe.wait_ge(landed[slot], i * 48 + 16 * (base[slot] + lap + 1))
                            return ring[:, slot, :]

                        def half(h):
                            for s in range(2):
                                if s == 0:
                                    pe.wait_ge(s_hid[lay], e * 2 + (h + 1))
                                for q in range(2):
                                    j = 4 * h + 2 * s + q
                                    w = here(j).rearrange("p (k n) -> p k n", k=4)
                                    if h == 0 and s == 0:
                                        pe.wait_ge(s_xgT[lay], e * 2 + (q + 1))
                                    for k in range(4):
                                        kk = 4 * q + k
                                        ins = mm(wide[0:M, 2 * h + s, :], xgT[:, b, kk, 0:M], w[:, k, :],
                                                 start=kk == 0, stop=kk == KD - 1)
                                    ins.then_inc(used[slot_of(j)[0]], 1)
                                if h == 1 and s == 0:
                                    turn_hid(0)

                        def turn_hid(h):
                            pe.wait_ge(s_hid[lay], e * 2 + (h + 3))
                            pe.wait_ge(s_xgT[lay], e * 2 + (h + 1))
                            for k in range(4):
                                ins = turn(turned[:, h, k * M:(k + 1) * M], hid[0:M, h, k * P:(k + 1) * P], plain=k == 0 and M <= 64)
                            ins.then_inc(s_hidtr[lay], 1)

                        def down(h):
                            pe.wait_ge(s_hidT[lay], e * 2 + (h + 3))
                            for j in (8 + 2 * h, 9 + 2 * h):
                                w = here(j).rearrange("p (k n) -> p k n", k=2)
                                for k in range(2):
                                    kk = (j - 8) * 2 + k
                                    for n in range(2):
                                        ins = mm(duo[0:M, n, :], hidT[:, h, kk % 4, 0:M], w[:, k, n * BANK:(n + 1) * BANK],
                                                 start=kk == 0, stop=kk == KD - 1)
                                ins.then_inc(used[slot_of(j)[0]], 1)

                        half(0)
                        half(1)
                        pe.wait_ge(s_ye[lay], e + 1)
                        down(0)
                        turn_hid(1)
                        more = not (last and b == 1)
                        if more:
                            turn_rows(e + 1, i + b, 1 - b, 0)
                        down(1)
                        if more:
                            turn_rows(e + 1, i + b, 1 - b, 1)

                turn_rows(0, 0, 0, 0)
                turn_rows(0, 0, 0, 1)
                with pe.Fori(0, LOOPS - 1) as i:
                    body(i, False)
                body(LOOPS - 1, True)

            pe.wait_ge(s_yg, KD)
            pe.wait_ge(s_modev, 6)
            pe.wait_ge(s_modcol, 3)

            def lru_lhs(k, t):
                at = t * P if t < TLT else CX + (t - TLT) * P
                return Y[:, k, at:at + P]

            out_project(0, 1, lru_lhs, [("lru_out", j) for j in range(4)])
            turn_choice(0)
            experts(0)

            for t in range(TT):
                turn_tile(2, t)
            hT = stages[2]["hT"]
            pe.wait_ge(s_hTa, N0[2] + TT)
            pe.wait_ge(s_hTd, N0[2] + TT)
            for j in range(3):
                arrived(("mla_in", j))

            def mla_w(k):
                j = [n for n, (a, b) in enumerate(MLA_K) if a <= k < b][0]
                return ring_at(("mla_in", j))[:, (k - MLA_K[j][0]) * MZ:(k - MLA_K[j][0] + 1) * MZ]

            for step in range(TT + 1):
                if step < TT:
                    t = step
                    if t >= 2:
                        pe.wait_ge(s_cqn, t - 1)
                    else:
                        pe.wait_ge(s_hid[0], 2 * E + 2)
                    b = 2 * (t % 2)
                    for k in range(KD):
                        lhs = hT[:, k, t * P:(t + 1) * P]
                        if t < TLT:
                            mm(wide[:, b, 0:QL], lhs, mla_w(k)[:, 0:QL], start=k == 0, stop=k == KD - 1)
                        ins = mm(wide[:, b + 1, 0:MZ - QL], lhs, mla_w(k)[:, QL:MZ], start=k == 0, stop=k == KD - 1)
                        if t == TT - 1 and k in (2, 5):
                            ins.then_inc(used[place[("mla_in", k // 3)][0]], 1)
                    ins.then_inc(s_mz, 1)
                if step >= 1:
                    t = step - 1
                    pe.wait_ge(s_cqn, t + 1)
                    if t >= 1:
                        pe.wait_ge(s_cqT, t)
                    for k in range(KQ if t < TLT else 0):
                        turn(duo[:, 0, k * P:(k + 1) * P], cqn[:, t % 2, k * P:(k + 1) * P])
                    for k in range(KKV):
                        ins = turn(duo[:, 1, k * P:(k + 1) * P], cqn[:, t % 2, QL + k * P:QL + (k + 1) * P])
                        if step == TT and k == 0:
                            ins.then_inc(used[place[("mla_in", 2)][0]], 1)
                    ins.then_inc(s_cqtr, 1)
            for j in range(KQ):
                arrived(("uq", j))
            for j in range(KKV):
                arrived(("ukv", j))
            pe.wait_ge(s_cqT, TT)
            with pe.Fori(0, NG) as g:
                pe.wait_ge(s_OT, g * 2 + 1)
                for step in range(TLT + 1):
                    if step < TLT:
                        t = step
                        pe.wait_ge(s_qtok, g * 4 + (t + 1))
                        for k in range(KQ):
                            ins = mm(duo[:, t % 2, 0:HG * QK], cqT[:, k, t * P:(t + 1) * P],
                                     ring_at(("uq", k))[:, bass.ds(g * (HG * QK), HG * QK)], start=k == 0, stop=k == KQ - 1)
                        ins.then_inc(s_q, 1)
                    if step >= 1:
                        t = step - 1
                        pe.wait_ge(s_qtok, g * 4 + (t + 3))
                        pe.wait_ge(s_qT, g * 4 + (t + 1))
                        for h in range(HG):
                            ins = turn(turned[0:QK, 0, h * P:(h + 1) * P], qtok[:, t % 2, h, :])
                        ins.then_inc(s_qtr, 1)
                for step in range(TT + 1):
                    if step < TT:
                        t = step
                        pe.wait_ge(s_ktok, g * 6 + (t + 1))
                        if t < 2:
                            pe.wait_ge(s_qtok, g * 4 + (t + 5))
                        for k in range(KKV):
                            ins = mm(duo[:, t % 2, :], ckvT[:, k, t * P:(t + 1) * P],
                                     ring_at(("ukv", k))[:, bass.ds(g * BANK, BANK)], start=k == 0, stop=k == KKV - 1)
                        ins.then_inc(s_kv, 1)
                    if step >= 1:
                        t = step - 1
                        pe.wait_ge(s_ktok, g * 6 + (t + 3))
                        pe.wait_ge(s_kT, g * 6 + (t + 1))
                        for h in range(HG):
                            ins = turn(turned[0:QK, 1, h * P:(h + 1) * P], ktok[:, t % 2, h, :])
                        ins.then_inc(s_ktr, 1)
                pe.wait_ge(s_qT, g * 4 + 5)
                pe.wait_ge(s_kT, g * 6 + 7)

                def scores(u):
                    h, t = divmod(u, TLT)
                    pe.wait_ge(s_exp, g * 16 + (u + 1))
                    b = 2 * (u % 2)
                    q = qT[:, h, t * P:(t + 1) * P]
                    mm(wide[:, b, :], q, kT[:, h, 0:TL], start=True, stop=True)
                    mm(wide[:, b + 1, 0:TC], q, kT[:, h, TL:T], start=True, stop=True).then_inc(s_S, 1)

                def turn_probs(u):
                    h, t = divmod(u, TLT)
                    pe.wait_ge(s_pn, g * 16 + (u + 1))
                    pe.wait_ge(s_PTa, g * 16 + (u + 1))
                    for k in range(4):
                        ins = turn(turned[:, 0, k * P:(k + 1) * P], prob[:, u % 2, k * P:(k + 1) * P])
                    ins.then_inc(s_ptr, 1)
                    pe.wait_ge(s_PTd, g * 16 + (u + 1))
                    for k in range(4, TT):
                        ins = turn(turned[:, 1, (k - 4) * P:(k - 3) * P], prob[:, u % 2, k * P:(k + 1) * P])
                    ins.then_inc(s_ptr, 1)

                def values(h):
                    pe.wait_ge(s_PTa, g * 16 + (4 * h + 5))
                    pe.wait_ge(s_PTd, g * 16 + (4 * h + 5))
                    if h % 2 == 0:
                        pe.wait_ge(s_OT, g * 2 + (h // 2 + 1))
                    r = (h % 2) * VD
                    for k in range(TT):
                        ins = mm(duo[r:r + VD, 0, :], V[:, k, h, :], PT[:, h % 2, k, :], start=k == 0, stop=k == TT - 1)
                    ins.then_inc(s_av, 1)

                U = HG * TLT
                for u in range(U + 2):
                    if u < U:
                        scores(u)
                    if u >= 2:
                        turn_probs(u - 2)
                        if (u - 2) % TLT == TLT - 1 and u - 2 >= TLT:
                            values((u - 2) // TLT - 1)
                values(HG - 1)
            for n, name in enumerate([("uq", j) for j in range(KQ)] + [("ukv", j) for j in range(KKV)]):
                turn(duo[0:32, 1, 32 * n:32 * n + 32], ident[0:32, 0:32]).then_inc(used[place[name][0]], 1)
            pe.wait_ge(s_OT, 2 * NG + 1)
            out_project(1, 3, lambda k, t: OT[:, k, t * P:(t + 1) * P], [("w_o", j) for j in range(4)])
            turn_choice(1)
            experts(1)

        @block.scalar
        def _(act):
            fn = nc.scalar.activation
            chain = Chain(act, s_act)

            def x_ready(eng, s, t):
                if s == 0:
                    eng.wait_ge(s_x0[t], 16)
                elif s == 2:
                    eng.wait_ge(s_x[t], 32)
                else:
                    eng.wait_ge(s_x1[s // 2], t + 1)

            def squares(s, t):
                x_ready(act, s, t)
                chain.step(fn(stages[s]["xn"][:, t, :], stages[s]["x"][:, t, :], ACT.Square, accum_out=stat[:, 0, t:t + 1]))
                fn(stat[:, 1, t:t + 1], stat[:, 0, t:t + 1], ACT.Sqrt, bias=eps[:, 0:1], scale=1.0 / D).then_inc(s_rms, 1)

            def modulate(s, t):
                a = 2 * s + (0 if t < TLT else 1)
                if t == 0:
                    act.wait_ge(s_modcol, (1, 2, 3, 3)[s])
                act.wait_ge(s_xtr, 2 * (N0[s] + t) + 1)
                for k in range(4):
                    ins = fn(stages[s]["hT"][:, k, t * P:(t + 1) * P], turned[:, 0, k * P:(k + 1) * P], ACT.Identity,
                             bias=cols[:, 7 + a, k:k + 1], scale=cols[:, a, k:k + 1])
                ins.then_inc(s_hTa, 1)

            def norm(s):
                n = stages[s]["n"]
                for step in range(n + 1):
                    if step < n:
                        squares(s, step)
                    if step >= 1:
                        modulate(s, step - 1)

            act.wait_ge(s_const, NCONST)
            act.wait_ge(s_pcol, 1)
            fn(silu_c[:].rearrange("p k v -> p v k"), pA[:, 0:16].rearrange("p (v k) -> p v k", v=2), ACT.Silu).then_inc(s_silu_c, 1)
            norm(0)
            act.wait_ge(s_lam, 1)
            fn(lam[:, 1, :], lam[:, 0, :], ACT.Exp, scale=-1.0).then_inc(s_lamE, 1)
            for q in range(KD, 2 * KD):
                act.wait_ge(s_z, q + 1)
                b = 2 * (q % 2)
                fn(seg(G[:, q - KD, :], 0), wide[:, b, :], ACT.Gelu_apprx_tanh)
                fn(seg(G[:, q - KD, :], 1), wide[:, b + 1, 0:TC], ACT.Gelu_apprx_tanh).then_inc(s_gelu, 1)
            for r, (d, half) in enumerate(rounds):
                for jj in range(4):
                    n, u = 4 * half + jj, 4 * r + jj
                    if r >= 1:
                        act.wait_ge(s_scan, u - 3)
                    elif jj == 0:
                        act.wait_ge(s_lam, 3)
                    for g, banks, dst in ((0, turned, RT), (1, duo, IT)):
                        act.wait_ge(s_gmm, 2 * u + g + 1)
                        bias = pB[:, B_GB + (2 * d + g) * KD + n:B_GB + (2 * d + g) * KD + n + 1]
                        fn(seg(dst[:, jj, :], 0), banks[:, 0, :], ACT.Sigmoid, bias=bias)
                        fn(seg(dst[:, jj, :], 1), banks[:, 1, 0:TC], ACT.Sigmoid, bias=bias).then_inc(s_sig, 1)
                act.wait_ge(s_lam, 2)
                for jj in range(4):
                    n, u = 4 * half + jj, 4 * r + jj
                    act.wait_ge(s_sig, 2 * u + 2)
                    at = d * KD + n
                    chain.step(fn(A[:, jj, 0:W], RT[:, jj, 0:W], ACT.Exp, scale=lam[:, 2, at:at + 1]))
                    fn(RT[:, jj, 0:W], RT[:, jj, 0:W], ACT.Tanh, scale=lam[:, 3, at:at + 1]).then_inc(s_tanh, 1)
                for jj in range(4):
                    u = 4 * r + jj
                    act.wait_ge(s_v, u + 1)
                    fn(RT[:, jj, 0:W], RT[:, jj, 0:W], ACT.Sqrt).then_inc(s_sqrt, 1)

            def affinities(lay):
                act.wait_ge(s_sub[lay], 1)
                fn(aff[:, 0:FFT[lay], :], aff[:, 0:FFT[lay], :], ACT.Exp).then_inc(s_aexp[lay], 1)

            def experts(lay):
                M, base = CAP[lay], moe_base[lay]
                with act.Fori(0, LOOPS) as i:
                    for b in range(2):
                        e = i * 2 + b
                        for h in range(2):
                            n = b * NCH + 4 * h + 1
                            act.wait_ge(used[n % RING], i * 3 + (base[n % RING] + n // RING + 1))
                            act.wait_ge(s_hid[lay], e * 2 + (h + 1))
                            fn(sg[0:M, h, :], wide[0:M, 2 * h, :], ACT.Silu).then_inc(s_silu[lay], 1)
                        for h in range(2):
                            act.wait_ge(s_hidtr[lay], e * 2 + (h + 1))
                            fn(hidT[:, h, :, 0:M], turned[:, h, 0:4 * M].rearrange("p (k m) -> p k m", k=4),
                               ACT.Copy).then_inc(s_hidT[lay], 1)

            norm(1)
            affinities(0)
            experts(0)
            norm(2)
            for t in range(TT):
                b = 2 * (t % 2)
                act.wait_ge(s_mz, t + 1)
                if t >= 2:
                    act.wait_ge(s_cqtr, t - 1)
                if t < TLT:
                    fn(cqn[:, t % 2, 0:QL], wide[:, b, 0:QL], ACT.Square, accum_out=mx[:, 0, t:t + 1])
                chain.step(fn(cqn[:, t % 2, QL:QL + KVL], wide[:, b + 1, 0:KVL], ACT.Square, accum_out=mx[:, 1, t:t + 1]))
                if t < TLT:
                    fn(mx[:, 2, t:t + 1], mx[:, 0, t:t + 1], ACT.Sqrt, bias=eps[:, 0:1], scale=1.0 / QL)
                fn(mx[:, 3, t:t + 1], mx[:, 1, t:t + 1], ACT.Sqrt, bias=eps[:, 0:1], scale=1.0 / KVL).then_inc(s_mzs, 1)
            with act.Fori(0, NG) as g:
                for t in range(TLT):
                    act.wait_ge(s_qtr, g * 4 + (t + 1))
                    fn(qT[:, :, t * P:(t + 1) * P], turned[0:QK, 0, :].rearrange("p (h n) -> p h n", h=HG),
                       ACT.Copy, scale=SCALE).then_inc(s_qT, 1)
                for t in range(TT):
                    act.wait_ge(s_ktr, g * 6 + (t + 1))
                    fn(kT[:, :, t * P:(t + 1) * P], turned[0:QK, 1, :].rearrange("p (h n) -> p h n", h=HG),
                       ACT.Copy).then_inc(s_kT, 1)
                for u in range(HG * TLT + 2):
                    if u < HG * TLT:
                        b = 2 * (u % 2)
                        act.wait_ge(s_max, g * 16 + (u + 1))
                        if u >= 2:
                            act.wait_ge(s_ptr, g * 32 + (2 * u - 2))
                        fn(prob[:, u % 2, :], wide[:, b:b + 2, :].rearrange("p a n -> p (a n)")[:, 0:T], ACT.Exp,
                           bias=asum[:, 0, u % 4:u % 4 + 1], accum_out=asum[:, 1, u % 4:u % 4 + 1]).then_inc(s_exp, 1)
                    if u >= 2:
                        h, t = divmod(u - 2, TLT)
                        act.wait_ge(s_ptr, g * 32 + (2 * (u - 2) + 1))
                        if t == 0 and h >= 2:
                            act.wait_ge(s_av, g * 4 + (h - 1))
                        fn(PT[:, h % 2, 0:4, t * P:(t + 1) * P], turned[:, 0, :].rearrange("p (k n) -> p k n", k=4),
                           ACT.Copy).then_inc(s_PTa, 1)
            norm(3)
            affinities(1)
            experts(1)
            for t in range(TLT):
                act.wait_ge(s_x[t], 48)
                chain.step(fn(xo_f[:, t, :], x_f[:, t, :], ACT.Square, accum_out=stat[:, 0, t:t + 1]))
                fn(stat[:, 1, t:t + 1], stat[:, 0, t:t + 1], ACT.Sqrt, bias=eps[:, 0:1], scale=1.0 / D).then_inc(s_rms, 1)

        @block.vector
        def _(dve):
            v = nc.vector
            chain = Chain(dve, s_dve)
            marked = [0]

            def mark(s_, n):
                v.memset(marks[:, marked[0]:marked[0] + 1], 1.0).then_inc(s_, n)
                marked[0] += 1

            def normed_tile(s, t):
                dve.wait_ge(s_rms, N0[s] + t + 1)
                chain.step(v.reciprocal(stat[:, 2, t:t + 1], stat[:, 1, t:t + 1]))
                v.tensor_scalar(stages[s]["xn"][:, t, :], stages[s]["x"][:, t, :], stat[:, 2, t:t + 1], None,
                                ALU.mult).then_inc(s_xn, 1)

            def modulate(s, t):
                a = 2 * s + (0 if t < TLT else 1)
                dve.wait_ge(s_xtr, 2 * (N0[s] + t) + 2)
                for k in range(4, 8):
                    ins = v.tensor_scalar(stages[s]["hT"][:, k, t * P:(t + 1) * P], turned[:, 1, (k - 4) * P:(k - 3) * P],
                                          cols[:, a, k:k + 1], cols[:, 7 + a, k:k + 1], ALU.mult, ALU.add)
                ins.then_inc(s_hTd, 1)

            def norm(s):
                n = stages[s]["n"]
                for step in range(n + 1):
                    if step < n:
                        normed_tile(s, step)
                    if step >= 1:
                        modulate(s, step - 1)

            def ada_read(i):
                name = ("ada", i, KD - 1)
                dve.wait_ge(used[place[name][0]], place[name][1])
                dve.wait_ge(s_bias, 16 * (i + 1))
                v.tensor_tensor(modbias[:], wide[0:2, :, :].rearrange("p a n -> p (a n)"), modbias[:], ALU.add).then_inc(s_modev, 1)

            def columns(a, scale, shift, gain):
                chain.step(v.scalar_tensor_tensor(cols[:, a, :], scale, 1.0, gain, ALU.add, ALU.mult))
                chain.step(v.tensor_copy(cols[:, 7 + a, :], shift))

            def mod_columns(i):
                dve.wait_ge(s_modtr, i + 1)
                n = 32 if i == 0 else 96
                mc = modc[i // 2]
                chain.step(v.tensor_copy(mc[:, 0:n], duo[:, 0, 0:n]))
                for s in ((0,), (1,), (2, 3))[i]:
                    lay, is_ffn = s // 2, s % 2
                    gain = pA[:, 16 + 16 * is_ffn + lay * KD:16 + 16 * is_ffn + (lay + 1) * KD]
                    for st_ in range(1 if s == 3 else 2):
                        at = st_ * 16 if i == 0 else st_ * 48 + (3 * KD if is_ffn else 0)
                        columns(2 * s + st_, mc[:, at + KD:at + 2 * KD], mc[:, at:at + KD], gain)
                mark(s_modcol, 1)

            dve.wait_ge(s_const, NCONST)
            dve.wait_ge(s_partr, 1)
            v.tensor_copy(pA[:], turned[:, 0, 0:48]).then_inc(s_pcol, 1)
            dve.wait_ge(s_partr, 2)
            v.tensor_copy(pB[:, 0:NB], turned[:, 1, 0:NB]).then_inc(s_pcol, 1)
            ada_read(0)
            mod_columns(0)
            norm(0)

            dve.wait_ge(s_pcol, 2)
            lm = pB[:, B_LAM:B_LAM + 16]
            chain.step(v.tensor_scalar(lam[:, 4, :], lm, -1.0, None, ALU.mult))
            v.tensor_tensor(lam[:, 0, :], lm, lam[:, 4, :], ALU.max).then_inc(s_lam, 1)

            for n in range(KD):
                ub = gmix[:, n % 2, :]
                b = 2 * (n % 2)
                dve.wait_ge(s_z, n + 1)
                v.tensor_copy(ub[:, PADL:PADL + TL], wide[:, b, :])
                v.tensor_copy(ub[:, CX + PADL:CX + PADL + TC], wide[:, b + 1, 0:TC]).then_inc(s_ucopy, 1)
                dve.wait_ge(s_ucopy, n + 1)
                tap = lambda j: pB[:, B_CONV + j * KD + n:B_CONV + j * KD + n + 1]
                chain.step(v.tensor_scalar(XC[:, n, 0:W], ub[:, 0:W], tap(0), pB[:, B_CB + n:B_CB + n + 1], ALU.mult, ALU.add))
                for j in range(1, CONV):
                    ins = v.scalar_tensor_tensor(XC[:, n, 0:W], ub[:, j:j + W], tap(j), XC[:, n, 0:W], ALU.mult, ALU.add)
                    if j < CONV - 1:
                        chain.step(ins)
                ins.then_inc(s_xc, 1)

            dve.wait_ge(s_lamE, 1)
            e_, s_, s2, acc = lam[:, 1, :], lam[:, 5, :], lam[:, 6, :], lam[:, 7, :]
            chain.step(v.tensor_scalar(acc, e_, 2.0, None, ALU.add))
            chain.step(v.reciprocal(s2, acc))
            chain.step(v.tensor_tensor(s_, e_, s2, ALU.mult))
            chain.step(v.tensor_tensor(s2, s_, s_, ALU.mult))
            chain.step(v.tensor_scalar(acc, s2, 2.0 / 17, 2.0 / 15, ALU.mult, ALU.add))
            for odd in (13, 11, 9, 7, 5, 3, 1):
                chain.step(v.tensor_tensor(acc, acc, s2, ALU.mult))
                chain.step(v.tensor_scalar(acc, acc, 2.0 / odd, None, ALU.add))
            chain.step(v.tensor_tensor(acc, acc, s_, ALU.mult))
            chain.step(v.scalar_tensor_tensor(acc, lam[:, 4, :], 0.0, acc, ALU.max, ALU.add))
            v.tensor_scalar(lam[:, 2, :], acc, -LRU_C, None, ALU.mult)
            v.tensor_scalar(lam[:, 3, :], acc, LRU_C, None, ALU.mult).then_inc(s_lam, 1)
            v.memset(areaA[:, :, TL:CX], 0.0).then_inc(s_lam, 1)

            for r, (d, half) in enumerate(rounds):
                for jj in range(4):
                    u = 4 * r + jj
                    dve.wait_ge(s_tanh, u + 1)
                    if u:
                        dve.wait_ge(s_v, u)
                    else:
                        dve.wait_ge(s_xc, KD)
                    sq = gmix[:, 0, 0:W]
                    chain.step(v.tensor_tensor(sq, A[:, jj, 0:W], A[:, jj, 0:W], ALU.mult))
                    v.scalar_tensor_tensor(RT[:, jj, 0:W], sq, 1.0, RT[:, jj, 0:W], ALU.add, ALU.mult).then_inc(s_v, 1)
                for jj in range(4):
                    n, u = 4 * half + jj, 4 * r + jj
                    dve.wait_ge(s_sqrt, u + 1)
                    dve.wait_ge(s_ix, u + 1)
                    chain.step(v.tensor_tensor(IT[:, jj, 0:W], RT[:, jj, 0:W], IT[:, jj, 0:W], ALU.mult))
                    dst = Y[:, n, :] if d == 0 else gmix[:, 1, :]
                    a, x_in = A[:, jj, :], IT[:, jj, :]
                    if d == 0:
                        chain.step(v.tensor_tensor_scan(dst[:, CX:W], a[:, CX:W], x_in[:, CX:W], 0.0, ALU.mult, ALU.add))
                        v.tensor_tensor_scan(dst[:, 0:TL], a[:, 0:TL], x_in[:, 0:TL], dst[:, W - 1:W],
                                             ALU.mult, ALU.add).then_inc(s_scan, 1)
                    else:
                        back = lambda ap, i: seg(ap, i)[:, ::-1]
                        chain.step(v.tensor_tensor_scan(back(dst, 1), back(a, 1), back(x_in, 1), 0.0, ALU.mult, ALU.add))
                        v.tensor_tensor_scan(back(dst, 0), back(a, 0), back(x_in, 0), dst[:, CX:CX + 1],
                                             ALU.mult, ALU.add).then_inc(s_scan, 1)
                        dve.wait_ge(s_scan, u + 1)
                        v.tensor_tensor(seg(Y[:, n, :], 0), seg(Y[:, n, :], 0), seg(dst, 0), ALU.add)
                        v.tensor_tensor(seg(Y[:, n, :], 1), seg(Y[:, n, :], 1), seg(dst, 1), ALU.add).then_inc(s_ysum, 1)
                        dve.wait_ge(s_ysum, 4 * half + jj + 1)
                ada_read(r + 1)
            ada_read(5)
            mod_columns(1)
            mod_columns(2)

            def residual(lay, s, t):
                dve.wait_ge(s_o[lay], t + 1)
                if lay == 0:
                    dve.wait_ge(s_x[t], 16)
                if t == 0:
                    dve.wait_ge(s_gmix[lay], 32 if lay == 0 else 16)
                g_ = gmix1[:] if lay else gmix[:, 0 if t < TLT else 1, :]
                b = 2 * (t % 2)
                o = stages[s]["xn"][:, t, :]
                chain.step(v.tensor_tensor(o, wide[:, b:b + 2, :].rearrange("p a n -> p (a n)"), g_, ALU.mult))
                v.tensor_tensor(stages[s]["x"][:, t, :], stages[s]["x"][:, t, :], o, ALU.add).then_inc(s_x1[lay], 1)

            def choose(lay):
                n_t, M = FFT[lay], CAP[lay]
                dve.wait_ge(s_log[lay], n_t)
                lg = duo[:, 0, 0:n_t * E].rearrange("p (t e) -> p t e", e=E)
                af = aff[:, 0:n_t, :]
                over = lambda a: a.unsqueeze(2).to_broadcast([P, n_t, E])
                chain.step(v.tensor_reduce(mx[:, 0, 0:n_t], lg, AX_X, ALU.max))
                v.tensor_tensor(af, lg, over(mx[:, 0, 0:n_t]), ALU.subtract).then_inc(s_sub[lay], 1)
                dve.wait_ge(s_aexp[lay], 1)
                chain.step(v.tensor_reduce(mx[:, 1, 0:n_t], af, AX_X, ALU.add))
                chain.step(v.reciprocal(mx[:, 2, 0:n_t], mx[:, 1, 0:n_t]))
                rs = mx[:, 2, 0:n_t].unsqueeze(2).to_broadcast([P, n_t, E])
                ins = v.tensor_tensor(aff2[:, :, 0:E], aff[:, 0:TLT, :], rs[:, 0:TLT, :], ALU.mult)
                if lay == 0:
                    ins = v.tensor_tensor(aff2[:, 0:TT - TLT, 32:48], aff[:, TLT:TT, :], rs[:, TLT:TT, :], ALU.mult)
                ins.then_inc(s_aff[lay], 1)
                dve.wait_ge(s_afft[lay], 1)
                chain.step(v.tensor_copy(affT[:], turned[0:48, 0, :]))
                for r in range(CAPL // 8):
                    at = slice(8 * r, 8 * r + 8)
                    chain.step(v.max(top_v[:, at], affT[:]))
                    chain.step(v.max_index(top_i[:, at], top_v[:, at], affT[:]))
                    if r < CAPL // 8 - 1:
                        chain.step(v.match_replace(affT[:], top_v[:, at], affT[:], -1.0))
                chain.step(v.tensor_copy(top_f[:], top_i[:]))
                v.tensor_copy(turn_in[:, 0, 0:CAPL], top_f[0:E, :])
                ins = v.tensor_copy(turn_in[:, 1, 0:CAPL], top_v[0:E, :])
                if lay == 0:
                    v.tensor_scalar(turn_in[:, 0, CAPL:M], top_f[32:32 + E, 0:CAPC], float(TL), None, ALU.add)
                    ins = v.tensor_copy(turn_in[:, 1, CAPL:M], top_v[32:32 + E, 0:CAPC])
                ins.then_inc(s_top[lay], 1)
                dve.wait_ge(s_topt[lay], 1)
                v.tensor_copy(idx_t[0:M, :], duo[0:M, 1, 0:E])
                chain.step(v.tensor_copy(gate_t[0:M, :], duo[0:M, 1, E:2 * E]))
                mark(s_sel[lay], 1)

            def experts(lay):
                M, base, s = CAP[lay], moe_base[lay], 2 * lay + 1
                dve.wait_ge(s_st[lay], 16 * FFT[lay])
                dve.wait_ge(s_nst[lay], 16 * FFT[lay])
                parts = [(0, CAPL, 2 * s)] + ([(CAPL, M, 2 * s + 1)] if lay == 0 else [])
                made = []
                for lo, hi, a in parts:
                    for dst, at in ((mod_a, a), (mod_b, 7 + a)):
                        made.append(v.tensor_copy(dst[:, :, lo:hi], cols[:, at, :].unsqueeze(2).to_broadcast([P, KD, hi - lo])))
                made[-1].then_inc(s_hid[lay], 2)
                mark(s_hidT[lay], 2)
                mark(s_ye[lay], 1)
                loop_chain = Chain(dve, s_dloop[lay])
                dve.wait_ge(s_hid[lay], 2)

                def rows(e, b, part):
                    dve.wait_ge(s_xgtr[lay], e * 2 + (part + 1))
                    k = slice(4 * part, 4 * part + 4)
                    loop_chain.step(v.tensor_tensor(xgT[:, b, k, 0:M], turned[:, part, 0:4 * M].rearrange("p (k m) -> p k m", k=4),
                                                    mod_a[:, k, 0:M], ALU.mult))
                    v.tensor_tensor(xgT[:, b, k, 0:M], xgT[:, b, k, 0:M], mod_b[:, k, 0:M], ALU.add).then_inc(s_xgT[lay], 1)

                def body(i, last):
                    loop_chain.n = i * 6 + 2
                    for b in range(2):
                        e = i * 2 + b
                        loop_chain.step(v.tensor_copy(gate_c[0:M, b:b + 1], gate_t[0:M, bass.ds(e, 1)]))
                        for h in range(2):
                            dve.wait_ge(s_silu[lay], e * 2 + (h + 1))
                            n = b * NCH + 4 * h + 3
                            dve.wait_ge(used[n % RING], i * 3 + (base[n % RING] + n // RING + 1))
                            v.tensor_tensor(hid[0:M, h, :], wide[0:M, 2 * h + 1, :], sg[0:M, h, :], ALU.mult).then_inc(s_hid[lay], 1)
                        if not (last and b == 1):
                            rows(e + 1, 1 - b, 0)
                            rows(e + 1, 1 - b, 1)
                        n = b * NCH + NCH - 1
                        dve.wait_ge(used[n % RING], i * 3 + (base[n % RING] + n // RING + 1))
                        dve.wait_ge(s_scat[lay], e * 16 + 16)
                        v.scalar_tensor_tensor(ye[0:M, b, :], duo[0:M, :, :].rearrange("p a n -> p (a n)"), gate_c[0:M, b:b + 1],
                                               gffn[0:M, :], ALU.mult, ALU.mult).then_inc(s_ye[lay], 1)

                rows(0, 0, 0)
                rows(0, 0, 1)
                dve.wait_ge(s_scat[lay], 32)
                with dve.Fori(0, LOOPS - 1) as i:
                    body(i, False)
                body(LOOPS - 1, True)

            def residual_norm(lay):
                s, n = 2 * lay + 1, FFT[lay]
                for step in range(n + 2):
                    if step < n:
                        residual(lay, s, step)
                    if 1 <= step <= n:
                        normed_tile(s, step - 1)
                    if step >= 2:
                        modulate(s, step - 2)

            residual_norm(0)
            choose(0)
            experts(0)

            norm(2)

            def turn_angles(dst, src, n, t):
                x1 = src.rearrange("p n (a h f) -> p n a h f", a=2, h=2)[:, :, :, 0, :]
                x2 = src.rearrange("p n (a h f) -> p n a h f", a=2, h=2)[:, :, :, 1, :]
                o1 = dst.rearrange("p n (a h f) -> p n a h f", a=2, h=2)[:, :, :, 0, :]
                o2 = dst.rearrange("p n (a h f) -> p n a h f", a=2, h=2)[:, :, :, 1, :]
                cos, sin = [ropes[:, t, i, :].rearrange("p (a f) -> p a f", a=2).unsqueeze(1).to_broadcast([P, n, 2, FQ]) for i in range(2)]
                tmp = [rtmp[:, j, 0:n * 2 * FQ].rearrange("p (n a f) -> p n a f", n=n, a=2) for j in range(4)]
                for j, (a_, b_) in enumerate(((x1, cos), (x2, sin), (x1, sin), (x2, cos))):
                    ins = v.tensor_tensor(tmp[j], a_, b_, ALU.mult)
                return ins, [(o1, tmp[0], tmp[1], ALU.subtract), (o2, tmp[2], tmp[3], ALU.add)]

            dve.wait_ge(s_rope, 16)
            for step in range(TT + 1):
                if step < TT:
                    t = step
                    b = 2 * (t % 2)
                    dve.wait_ge(s_mzs, t + 1)
                    if t:
                        dve.wait_ge(s_cqn, t)
                    if t < TLT:
                        v.reciprocal(lam[:, 4, t:t + 1], mx[:, 2, t:t + 1])
                    chain.step(v.reciprocal(lam[:, 5, t:t + 1], mx[:, 3, t:t + 1]))
                    if t < TLT:
                        v.tensor_scalar(cqn[:, t % 2, 0:QL], wide[:, b, 0:QL], lam[:, 4, t:t + 1], None, ALU.mult)
                    v.tensor_scalar(cqn[:, t % 2, QL:QL + KVL], wide[:, b + 1, 0:KVL], lam[:, 5, t:t + 1], None, ALU.mult)
                    kr = wide[:, b + 1, KVL:KVL + ROPE]
                    if t < TLT:
                        chain.step(v.tensor_copy(kraw[:, t % 2, :], kr))
                        ins, rest = turn_angles(krr[:, t:t + 1, :], kraw[:, t % 2:t % 2 + 1, :], 1, t)
                        chain.step(ins)
                        for o, a_, b_, op in rest:
                            ins = v.tensor_tensor(o, a_, b_, op)
                        ins.then_inc(s_cqn, 1)
                    else:
                        v.tensor_copy(krr[:, t, :], kr).then_inc(s_cqn, 1)
                if step >= 1:
                    t = step - 1
                    dve.wait_ge(s_cqtr, t + 1)
                    for k in range(KQ if t < TLT else 0):
                        v.tensor_scalar(cqT[:, k, t * P:(t + 1) * P], duo[:, 0, k * P:(k + 1) * P],
                                        pB[:, B_QN + k:B_QN + k + 1], None, ALU.mult)
                    for k in range(KKV):
                        ins = v.tensor_scalar(ckvT[:, k, t * P:(t + 1) * P], duo[:, 1, k * P:(k + 1) * P],
                                              pB[:, B_KVN + k:B_KVN + k + 1], None, ALU.mult)
                    ins.then_inc(s_cqT, 1)
            dve.wait_ge(s_cqT, TT)
            for s_, n in ((s_qtok, 2), (s_qT, 1), (s_ktok, 2), (s_kT, 1), (s_exp, 2), (s_PTa, 1), (s_PTd, 1), (s_OT, 1)):
                mark(s_, n)
            loop_chain = Chain(dve, s_dloop[2])
            with dve.Fori(0, NG) as g:
                loop_chain.n = g * TLT
                for t in range(TLT):
                    dve.wait_ge(s_q, g * 4 + (t + 1))
                    dve.wait_ge(s_qtok, g * 4 + (t + 2))
                    if t >= 2:
                        dve.wait_ge(s_qtr, g * 4 + (t - 1))
                    q4 = duo[:, t % 2, 0:HG * QK].rearrange("p (h n) -> p h n", h=HG)
                    v.tensor_copy(qtok[:, t % 2, :, 0:NOPE], q4[:, :, 0:NOPE])
                    ins, rest = turn_angles(qtok[:, t % 2, :, NOPE:QK], q4[:, :, NOPE:QK], HG, t)
                    loop_chain.step(ins)
                    for o, a_, b_, op in rest:
                        ins = v.tensor_tensor(o, a_, b_, op)
                    ins.then_inc(s_qtok, 1)
                for t in range(TT):
                    dve.wait_ge(s_kv, g * 6 + (t + 1))
                    if t >= 2:
                        dve.wait_ge(s_ktr, g * 6 + (t - 1))
                    kv4 = duo[:, t % 2, :].rearrange("p (h n) -> p h n", h=HG)
                    v.tensor_copy(ktok[:, t % 2, :, 0:NOPE], kv4[:, :, 0:NOPE])
                    v.tensor_copy(ktok[:, t % 2, :, NOPE:QK], krr[:, t:t + 1, :].to_broadcast([P, HG, ROPE]))
                    v.tensor_copy(V[:, t, :, :], kv4[:, :, NOPE:NOPE + VD]).then_inc(s_ktok, 1)
                U = HG * TLT

                def pair_out(pair):
                    dve.wait_ge(s_av, g * 4 + (2 * pair + 2))
                    v.tensor_copy(OT[:, bass.ds(g * 2 + pair, 1), :], duo[:, 0:1, :]).then_inc(s_OT, 1)

                for u in range(U + 2):
                    if u < U:
                        b = 2 * (u % 2)
                        dve.wait_ge(s_S, g * 16 + (u + 1))
                        v.tensor_reduce(asum[:, 0, u % 4:u % 4 + 1], wide[:, b:b + 2, :].rearrange("p a n -> p (a n)")[:, 0:T],
                                        AX_X, ALU.max, negate=True).then_inc(s_max, 1)
                    if 1 <= u <= U:
                        dve.wait_ge(s_exp, g * 16 + (u + 2))
                        c_ = (u - 1) % 4
                        v.reciprocal(asum[:, 2, c_:c_ + 1], asum[:, 1, c_:c_ + 1]).then_inc(s_rs, 1)
                    if u >= 2:
                        h, t = divmod(u - 2, TLT)
                        dve.wait_ge(s_ptr, g * 32 + (2 * (u - 2) + 2))
                        if t == 0 and h >= 2:
                            dve.wait_ge(s_av, g * 4 + (h - 1))
                        v.tensor_copy(PT[:, h % 2, 4:TT, t * P:(t + 1) * P],
                                      turned[:, 1, 0:2 * P].rearrange("p (k n) -> p k n", k=2)).then_inc(s_PTd, 1)
                        if u - 2 == 3 * TLT - 1:
                            pair_out(0)
                pair_out(1)
            residual_norm(1)
            choose(1)
            experts(1)
            dve.wait_ge(s_nf, 16)
            for t in range(TLT):
                dve.wait_ge(s_rms, N0[4] + t + 1)
                chain.step(v.reciprocal(stat[:, 2, t:t + 1], stat[:, 1, t:t + 1]))
                v.scalar_tensor_tensor(xo_f[:, t, :], x_f[:, t, :], stat[:, 2, t:t + 1], nf[:], ALU.mult, ALU.mult).then_inc(s_fin, 1)

        @block.gpsimd
        def _(pool):
            g_ = nc.gpsimd
            g_.memset(ident[:], 0.0).then_inc(s_const, 1)
            pool.wait_ge(s_const, 1)
            g_.affine_select(out=ident[:], in_=ident[:], compare_op=ALU.not_equal, fill=1.0, base=0,
                             pattern=[[-1, P]], channel_multiplier=1).then_inc(s_const, 1)
            g_.memset(eps[:], EPS).then_inc(s_const, 1)
            g_.memset(aff2[:], -1.0).then_inc(s_const, 1)
            g_.memset(gmix[:], 0.0).then_inc(s_const, 1)
            g_.memset(idx_t[:], 0).then_inc(s_const, 1)
            g_.memset(marks[:], 0.0).then_inc(s_const, 1)
            g_.memset(gate_t[:], 0.0).then_inc(s_const, 1)
            g_.memset(stat[:], 1.0).then_inc(s_const, 1)

            def mod_store(i):
                lay, g = divmod(i, 3)
                pool.wait_ge(s_modev, i + 1)
                pool.dma_start(mods[lay, :, g * MODW:(g + 1) * MODW], modbias[:]).then_inc(s_modst, 16)
                pool.wait_ge(s_modst, 16 * (i + 1))
                if i < 5:
                    lay, g = divmod(i + 1, 3)
                    pool.dma_start(modbias[:], ada_b[lay:lay + 1, g * MODW:(g + 1) * MODW].to_broadcast([2, MODW])).then_inc(s_bias, 16)

            def mod_rows(i):
                lay, n = i // 2, (16 if i == 0 else 48)
                rows = (rows0, rows0, rows1)[i]
                if i == 1:
                    pool.wait_ge(s_modtr, 1)
                for v_ in range(2):
                    pool.dma_start(rows[v_ * n:(v_ + 1) * n, :],
                                   mods[lay, v_, 0:n * P].rearrange("(r q) -> r q", q=P)).then_inc(s_modrow, 16)

            pool.dma_start(modbias[:], ada_b[0:1, 0:MODW].to_broadcast([2, MODW])).then_inc(s_bias, 16)
            mod_store(0)
            mod_rows(0)
            for r, (d, half) in enumerate(rounds):
                for jj in range(4):
                    n, u = 4 * half + jj, 4 * r + jj
                    pool.wait_ge(s_sig, 2 * u + 2)
                    pool.wait_ge(s_xc, n + 1)
                    g_.tensor_tensor(IT[:, jj, 0:W], IT[:, jj, 0:W], XC[:, n, 0:W], ALU.mult).then_inc(s_ix, 1)
                if d == 1:
                    for jj in range(4):
                        n = 4 * half + jj
                        pool.wait_ge(s_ysum, n + 1)
                        g_.tensor_tensor(seg(Y[:, n, :], 0), seg(Y[:, n, :], 0), seg(G[:, n, :], 0), ALU.mult)
                        g_.tensor_tensor(seg(Y[:, n, :], 1), seg(Y[:, n, :], 1), seg(G[:, n, :], 1), ALU.mult).then_inc(s_yg, 1)
                if r == 3:
                    pool.wait_ge(s_ix, 16)
                    pool.wait_ge(s_gmm, 32)
                    for t in range(TT):
                        src = x_d[t * P:(t + 1) * P, :] if t < TLT else ctx_d[(t - TLT) * P:(t - TLT + 1) * P, :]
                        pool.dma_start(stages[1]["x"][:, t, :], src).then_inc(s_x[t], 16)
                    pool.wait_ge(s_ysum, KD)
                    for v_ in range(2):
                        pool.dma_start(gmix[:, v_, :], mods[0, v_:v_ + 1, 2 * D:3 * D].to_broadcast([P, D])).then_inc(s_gmix[0], 16)
                mod_store(r + 1)
                if r == 1:
                    mod_rows(1)
            mod_store(5)
            mod_rows(2)

            def stores(lay):
                s, n = 2 * lay + 1, FFT[lay]
                for step in range(n + 1):
                    if step < n:
                        pool.wait_ge(s_x1[lay], step + 1)
                        pool.dma_start(stream[step * P:(step + 1) * P, :], stages[s]["x"][:, step, :]).then_inc(s_st[lay], 16)
                    if step >= 1:
                        t = step - 1
                        pool.wait_ge(s_xn, N0[s] + t + 1)
                        pool.dma_start(normed[t * P:(t + 1) * P, :], stages[s]["xn"][:, t, :]).then_inc(s_nst[lay], 16)
                pool.wait_ge(s_st[lay], 16 * n)
                pool.wait_ge(s_nst[lay], 16 * n)

            def experts(lay):
                M = CAP[lay]
                pool.wait_ge(s_sel[lay], 1)
                for v_, lo, hi in ((0, 0, CAPL), (1, CAPL, M)) if lay == 0 else ((0, 0, M // 2), (0, M // 2, M)):
                    pool.dma_start(gffn[lo:hi, :], mods[lay, v_:v_ + 1, 5 * D:6 * D].to_broadcast([hi - lo, D])).then_inc(s_scat[lay], 16)

                def gather(e, b):
                    g_.tensor_copy(idx_c[0:M, b:b + 1], idx_t[0:M, e:e + 1]).then_inc(s_idxc[lay], 1)
                    pool.wait_ge(s_idxc[lay], e + 1)
                    pool.indirect_dma_start(out=xg[0:M, b, :], out_offset=None, in_=normed,
                                            in_offset=bass.IndirectOffsetOnAxis(ap=idx_c[0:M, b:b + 1], axis=0)).then_inc(s_gath[lay][b], 16)

                def body(i, last):
                    for b in range(2):
                        e = i * 2 + b
                        if not (last and b == 1):
                            pool.wait_ge(s_scat[lay], e * 16 + 32)
                            gather(e + 1, 1 - b)
                        pool.wait_ge(s_ye[lay], e + 2)
                        pool.wait_ge(s_scat[lay], e * 16 + 32)
                        pool.indirect_dma_start(out=stream, out_offset=bass.IndirectOffsetOnAxis(ap=idx_c[0:M, b:b + 1], axis=0),
                                                in_=ye[0:M, b, :], in_offset=None, compute_op=ALU.add).then_inc(s_scat[lay], 16)

                gather(0, 0)
                for i in range(LOOPS):
                    body(i, i == LOOPS - 1)
                pool.wait_ge(s_scat[lay], 32 + 16 * E)

            stores(0)
            experts(0)
            for t in range(TT):
                pool.dma_start(x_b[:, t, :], stream[t * P:(t + 1) * P, :]).then_inc(s_x[t], 16)
            pool.dma_start(gmix1[:], mods[1, 0:1, 2 * D:3 * D].to_broadcast([P, D])).then_inc(s_gmix[1], 16)
            pool.dma_start(ropes[:], rope.rearrange("(t p) i f -> p t i f", p=P)).then_inc(s_rope, 16)
            with pool.Fori(0, NG) as g:
                for u in range(HG * TLT):
                    pool.wait_ge(s_rs, g * 16 + (u + 1))
                    g_.tensor_tensor(prob[:, u % 2, :], prob[:, u % 2, :], asum[:, 2, u % 4:u % 4 + 1].to_broadcast([P, T]),
                                     ALU.mult).then_inc(s_pn, 1)
            stores(1)
            experts(1)
            for t in range(TLT):
                pool.dma_start(x_f[:, t, :], stream[t * P:(t + 1) * P, :]).then_inc(s_x[t], 16)
            pool.dma_start(nf[:], norm_final.rearrange("(a d) -> a d", a=1).to_broadcast([P, D])).then_inc(s_nf, 16)
            for t in range(TLT):
                pool.wait_ge(s_fin, t + 1)
                pool.dma_start(out_d[t * P:(t + 1) * P, :], xo_f[:, t, :]).then_inc(s_out, 16)
            pool.wait_ge(s_out, 16 * TLT)


INPUTS = ["x", "c", "ctx", "c_ctx", "ada_w", "ada_b", "norm_mix", "norm_ffn", "norm_final", "lru_w_in", "lru_conv_w",
          "lru_conv_b", "lru_gate_w", "lru_gate_b", "lru_lambda", "lru_w_out", "mla_w_in", "mla_q_norm", "mla_kv_norm",
          "mla_w_uq", "mla_w_ukv", "mla_w_o", "moe_router", "moe_w_up", "moe_w_down"]


def rope_table(tokens, freqs):
    freq = np.float32(ROPE_BASE) ** (-np.arange(freqs, dtype=np.float32) / np.float32(freqs))
    pos = np.stack([np.arange(tokens) // GRID_W, np.arange(tokens) % GRID_W], axis=-1).astype(np.float32)
    ang = (pos[:, :, None] * freq).reshape(tokens, 2 * freqs)
    return np.stack([np.cos(ang), np.sin(ang)], axis=1).astype(np.float32)


def kernel(**inputs):
    import concourse.bacc as bacc
    from concourse.bass_utils import run_bass_kernel_spmd

    nc = bacc.Bacc("TRN2", target_bir_lowering=False, num_devices=1)
    arrays = {name: np.ascontiguousarray(inputs[name]) for name in INPUTS}
    arrays["rope"] = rope_table(inputs["x"].shape[1], 8)
    args = [nc.dram_tensor(name, a.shape, mybir.dt.from_np(a.dtype), kind="ExternalInput").ap() for name, a in arrays.items()]
    out = nc.dram_tensor("out", inputs["x"].shape, F32, kind="ExternalOutput").ap()
    build(nc, *args, out)
    result = run_bass_kernel_spmd(nc, [arrays], core_ids=[0])
    return result.results[0]["out"]
```

```python
from contextlib import ExitStack

import numpy as np

import concourse.bass as bass
from concourse import mybir

ALU = mybir.AluOpType
ACT = mybir.ActivationFunctionType
F32 = mybir.dt.float32
F32R = mybir.dt.float32r
U32 = mybir.dt.uint32
AX_X = mybir.AxisListType.X

P = 128
RING = 8
BANK = 512
EPS = 1e-6
LRU_C = 8.0
GRID_W = 64
ROPE_BASE = 10000.0


class Chain:

    def __init__(self, eng, sem):
        self.eng, self.sem, self.n = eng, sem, 0

    def step(self, ins):
        self.n = self.n + 1
        ins.then_inc(self.sem, 1)
        self.eng.wait_ge(self.sem, self.n)


def build(nc, x, c, ctx, c_ctx, ada_w, ada_b, norm_mix, norm_ffn, norm_final, lru_w_in, lru_conv_w, lru_conv_b,
          lru_gate_w, lru_gate_b, lru_lambda, lru_w_out, mla_w_in, mla_q_norm, mla_kv_norm, mla_w_uq, mla_w_ukv,
          mla_w_o, moe_router, moe_w_up, moe_w_down, rope, out):
    TL, D = x.shape[1], x.shape[2]
    TC = ctx.shape[1]
    T = TL + TC
    KD = D // P
    TLT, TT = TL // P, T // P
    L, E = moe_router.shape[0], moe_router.shape[2]
    F = moe_w_down.shape[2]
    CAPL, CAPC = 2 * TL // E, 2 * TC // E
    CAP = [CAPL + CAPC, CAPL]
    FFT = [TT, TLT]
    QL, KVL = mla_q_norm.shape[1], mla_kv_norm.shape[1]
    ROPE = mla_w_in.shape[2] - QL - KVL
    H = 16
    NOPE = mla_w_uq.shape[2] // H - ROPE
    QK = NOPE + ROPE
    VD = mla_w_ukv.shape[2] // H - NOPE
    HG = 4
    NG = H // HG
    KQ, KKV = QL // P, KVL // P
    FQ = ROPE // 4
    SCALE = float(QK) ** -0.5
    CONV = lru_conv_w.shape[1]
    PADL, PADR = CONV // 2, CONV - 1 - CONV // 2
    CX = TL + PADL + PADR
    W = CX + TC
    WP = W + 1
    MODW = 2 * D
    MZ = QL + KVL + ROPE
    MLA_K = [(0, 3), (3, 6), (6, 8)]
    assert (D, TL, TC, T, F) == (1024, 512, 256, 768, 1024) and CAPL % 8 == 0 and CAPC % 8 == 0 and WP == 772

    mods = nc.dram_tensor("mods", [L, 2, 6 * D], F32).ap()
    stream = nc.dram_tensor("stream", [T, D], F32).ap()
    normed = nc.dram_tensor("normed", [T, D], F32).ap()

    chunks, slot_loads = [], [0] * RING
    place = {}

    def chunk(name, slot):
        place[name] = (slot, slot_loads[slot] + 1)
        chunks.append((name, slot, slot_loads[slot]))
        slot_loads[slot] += 1

    free6 = [2, 3, 4, 5, 6, 7]
    turn = 0
    for k in range(KD):
        chunk(("ada", 0, k), k)
    for m in range(KD):
        chunk(("lru_in", (m + KD // 2) % KD), m)
    chunk(("gate", 0), 0)
    chunk(("gate", 1), 1)
    side, group, k = [], 1, 0
    for q in range(2 * KD):
        todo = []
        if k == 0 and group == 2 or group == 3:
            todo.append(("turn", group - 1))
            group += group == 3
        for slot in range(2, (q - 3) // 2 + 1):
            if group > 2:
                break
            chunk(("ada", group, k), slot)
            todo.append(("ada", group, k))
            k += 1
            if k == KD:
                group, k = group + 1, 0
                break
        side.append(todo)
    assert group == 4
    for g in range(3, 6):
        for k in range(KD):
            chunk(("ada", g, k), free6[turn % 6])
            turn += 1
    for j in range(4):
        chunk(("lru_out", j), free6[turn % 6])
        turn += 1
    head_chunks = list(chunks)
    NCH = 12
    USED0, LANDED0 = [None, None], [None, None]
    NS, NW = 8, 4
    USED0[0] = slot_loads + [1] * (NCH - RING)
    LANDED0[0] = slot_loads + [0] * (NCH - RING)
    slot_loads = [n + E for n in slot_loads]
    chunks = []
    for j in range(3):
        chunk(("mla_in", j), j)
    for j in range(KQ):
        chunk(("uq", j), 3 + j)
    for j in range(KKV):
        chunk(("ukv", j), 6 + j)
    for j in range(3):
        chunk(("w_o", j), j)
    chunk(("w_o", 3), 3)
    mla_chunks = list(chunks)
    USED0[1] = slot_loads + [E + 2] * (NCH - RING)
    LANDED0[1] = slot_loads + [E] * (NCH - RING)

    with ExitStack() as es:
        def sb(name, shape, dt=F32, st=es):
            return st.enter_context(nc.sbuf_tensor("sb_" + name, shape, dt))

        def sem(name):
            return es.enter_context(nc.semaphore(name))

        wide = es.enter_context(nc.psum_tensor("wide", [P, 4, BANK], F32))
        duo = es.enter_context(nc.psum_tensor("duo", [P, 2, BANK], F32))
        turned = es.enter_context(nc.psum_tensor("turned", [P, 2, BANK], F32))

        ring = sb("ring", [P, RING, 2048])
        ident = sb("ident", [P, P])
        eps = sb("eps", [P, 1])
        rowsA = sb("rowsA", [P, P])
        rowsB = sb("rowsB", [P, P])
        pA = sb("pA", [P, 48])
        pB = sb("pB", [P, 96])
        modc = [sb("modc0", [P, 96]), sb("modc1", [P, 96])]
        cols = sb("cols", [P, 14, KD])
        router = sb("router", [P, L, KD, E])
        silu_c = sb("silu_c", [P, KD, 2])
        stat = sb("stat", [P, 3, TT])
        lam = sb("lam", [P, 8, 16])
        idx_t = sb("idx_t", [P, E], U32)
        gate_t = sb("gate_t", [P, E])
        mx = sb("mx", [P, 4, TT])
        marks = sb("marks", [P, 32])
        aff = sb("aff", [P, TT, E])
        aff2 = sb("aff2", [P, TLT, 48])
        affT = sb("affT", [48, TL])
        top_v = sb("top_v", [48, CAPL])
        top_i = sb("top_i", [48, CAPL], U32)
        top_f = sb("top_f", [48, CAPL])
        turn_in = sb("turn_in", [E, 2, CAP[0]])

        def phase(*tensors):
            st = ExitStack()
            made = [sb(n, s, d, st) for n, s, d in tensors]
            return st, made

        st, (areaA, areaB, areaC, areaD, areaE, gmix, modbias) = phase(
            ("areaA", [P, 8, WP], F32), ("areaB", [P, 8, WP], F32), ("areaC", [P, 8, WP], F32),
            ("areaD", [P, 8, WP], F32), ("areaE", [P, 4, WP], F32), ("gmix", [P, 2, D], F32),
            ("modbias", [P, 2, BANK], F32))
        st.close()

        def flat(a, n, w):
            return a[:].rearrange("p a b -> p (a b)")[:, 0:n * w].rearrange("p (n w) -> p n w", n=n)

        st, (x_b, gmix1) = phase(("x_b", [P, TT, D], F32), ("gmix1", [P, D], F32))
        mla_keep = ExitStack()
        cqT, ckvT, krr, ropes, cqn, kraw, rtmp = [sb(n, s, F32, mla_keep) for n, s in (
            ("cqT", [P, KQ, TL]), ("ckvT", [P, KKV, T]), ("krr", [P, TT, ROPE]), ("ropes", [P, TLT, 2, 2 * FQ]),
            ("cqn", [P, 2, QL + KVL]), ("kraw", [P, 2, ROPE]), ("rtmp", [P, 4, HG * 2 * FQ]))]
        sub, (xn2, hT2) = phase(("xn2", [P, TT, D], F32), ("hT2", [P, KD, T], F32))
        sub.close()
        sub, (OT, qT, kT, V, qtok, ktok, prob, PT, asum) = phase(
            ("OT", [P, KD, TL], F32), ("qT", [QK, HG, TL], F32), ("kT", [QK, HG, T], F32),
            ("V", [P, TT, HG, VD], F32), ("qtok", [P, 2, HG, QK], F32), ("ktok", [P, 2, HG, QK], F32),
            ("prob", [P, 2, T], F32), ("PT", [P, 2, TT, TL], F32), ("asum", [P, 3, 8], F32))
        sub.close()
        sub, (_, xn3, hT3) = phase(("OTkeep", [P, KD, TL], F32), ("xn3", [P, TLT, D], F32), ("hT3", [P, KD, TL], F32))
        sub.close()
        mla_keep.close()
        st.close()

        st, (xg, h32, xs, sg, lo_rows, hid, hidT, ye, mod_a, mod_b, gffn, idx_c, gate_c, w_hi, w_lo, ring_x) = phase(
            ("xg", [P, D], F32), ("h32", [P, KD, CAP[0]], F32), ("xs", [P, KD, 2 * CAP[0]], F32R),
            ("sg", [P, BANK], F32), ("lo_rows", [CAPL, BANK], F32), ("hid", [P, BANK], F32),
            ("hidT", [P, 2, 4, CAP[0]], F32), ("ye", [P, D], F32), ("mod_a", [P, KD, CAP[0]], F32),
            ("mod_b", [P, KD, CAP[0]], F32), ("gffn", [P, D], F32), ("idx_c", [P, 2], U32), ("gate_c", [P, 2], F32),
            ("w_hi", [P, NW, 2048], F32R), ("w_lo", [P, NW, 2048], F32R), ("ring_x", [P, NCH - RING, 2048], F32))
        st.close()
        st, (x_f, xo_f, nf) = phase(("x_f", [P, TLT, D], F32), ("xo_f", [P, TLT, D], F32), ("nf", [P, D], F32))
        st.close()

        landed = [sem(f"landed{s}") for s in range(NCH)]
        used = [sem(f"used{s}") for s in range(NCH)]
        s_const, s_parA, s_parB, s_rope, s_router = [sem(n) for n in ("s_const", "s_parA", "s_parB", "s_rope", "s_router")]
        s_partr, s_pcol, s_silu_c, s_lam, s_lamE = [sem(n) for n in ("s_partr", "s_pcol", "s_silu_c", "s_lam", "s_lamE")]
        s_modev, s_modst, s_bias, s_modtr, s_modcol = [sem(n) for n in (
            "s_modev", "s_modst", "s_bias", "s_modtr", "s_modcol")]
        s_x0 = [sem(f"s_x0{t}") for t in range(TT)]
        s_x = [sem(f"s_x{t}") for t in range(TT)]
        s_rms, s_xn, s_xtr, s_hTa, s_hTd = [sem(n) for n in ("s_rms", "s_xn", "s_xtr", "s_hTa", "s_hTd")]
        N0 = [0, TT, 2 * TT, 3 * TT, 3 * TT + TLT]
        s_z, s_gelu, s_ucopy, s_xc = [sem(n) for n in ("s_z", "s_gelu", "s_ucopy", "s_xc")]
        s_gmm, s_sig, s_ix, s_tanh, s_v, s_sqrt, s_scan, s_ysum, s_yg = [sem(n) for n in (
            "s_gmm", "s_sig", "s_ix", "s_tanh", "s_v", "s_sqrt", "s_scan", "s_ysum", "s_yg")]
        s_gmix = [sem("s_gmix0"), sem("s_gmix1")]
        s_o = [sem("s_o0"), sem("s_o1")]
        s_x1 = [sem("s_x1_0"), sem("s_x1_1")]
        s_st = [sem("s_st0"), sem("s_st1")]
        s_nst = [sem("s_nst0"), sem("s_nst1")]
        s_log = [sem("s_log0"), sem("s_log1")]
        s_sub, s_aexp, s_aff, s_afft, s_top, s_topt, s_sel = [sem(n) for n in (
            "s_sub", "s_aexp", "s_aff", "s_afft", "s_top", "s_topt", "s_sel")]
        s_idxc = [sem("s_idxc0"), sem("s_idxc1")]
        s_gath = [sem("s_gath0"), sem("s_gath1")]
        s_xgtr = [sem("s_xgtr0"), sem("s_xgtr1")]
        s_xgT = [sem("s_xgT0"), sem("s_xgT1")]
        s_hi = [sem("s_hi0"), sem("s_hi1")]
        s_wdone = [sem("s_wdone0"), sem("s_wdone1")]
        s_lot, s_gs, s_us = sem("s_lot"), sem("s_gs"), sem("s_us")
        s_silu = [sem("s_silu0"), sem("s_silu1")]
        s_hid = [sem("s_hid0"), sem("s_hid1")]
        s_hidtr = [sem("s_hidtr0"), sem("s_hidtr1")]
        s_hidT = [sem("s_hidT0"), sem("s_hidT1")]
        s_ye = [sem("s_ye0"), sem("s_ye1")]
        s_scat = [sem("s_scat0"), sem("s_scat1")]
        s_mz, s_mzs, s_cqn, s_cqtr, s_cqT, s_krr = [sem(n) for n in ("s_mz", "s_mzs", "s_cqn", "s_cqtr", "s_cqT", "s_krr")]
        s_q, s_qtok, s_qtr, s_qT, s_kv, s_V, s_ktok, s_ktr, s_kT = [sem(n) for n in (
            "s_q", "s_qtok", "s_qtr", "s_qT", "s_kv", "s_V", "s_ktok", "s_ktr", "s_kT")]
        s_S, s_max, s_exp, s_pn, s_ptr, s_PTd, s_PTa, s_av, s_OT, s_rs = [sem(n) for n in (
            "s_S", "s_max", "s_exp", "s_pn", "s_ptr", "s_PTd", "s_PTa", "s_av", "s_OT", "s_rs")]
        s_fin, s_out, s_nf = sem("s_fin"), sem("s_out"), sem("s_nf")
        s_dve, s_act, s_pool = sem("s_dve"), sem("s_act"), sem("s_pool")
        s_dloop = [sem("s_dloop0"), sem("s_dloop1"), sem("s_dloop2")]
        NCONST = 10

        def ring_at(name):
            return ring[:, place[name][0], :]

        def chunk_at(j):
            return ring[:, j, :] if j < RING else ring_x[:, j - RING, :]

        def col(layer, v, what, k):
            return v * 48 + what * 8 + k

        B_CONV, B_CB, B_GB, B_LAM = 0, CONV * KD, CONV * KD + KD, CONV * KD + KD + 4 * KD
        B_QN = B_LAM + 2 * KD
        B_KVN = B_QN + KQ
        NB = B_KVN + KKV
        N_COL = [[0, 1], [2, 3], [4, 5], [6, None]]

        x_d = x.rearrange("b t d -> (b t) d")
        ctx_d = ctx.rearrange("b t d -> (b t) d")
        out_d = out.rearrange("b t d -> (b t) d")
        stages = [
            dict(x=flat(areaD, TT, D), xn=flat(areaA, TT, D), hT=flat(areaB, KD, T), n=TT, lay=0, sc=1, sh=0),
            dict(x=flat(areaD, TT, D), xn=flat(areaC, TT, D), hT=flat(areaA, KD, T), n=TT, lay=0, sc=4, sh=3),
            dict(x=x_b[:], xn=xn2[:], hT=hT2[:], n=TT, lay=1, sc=1, sh=0),
            dict(x=x_b[:], xn=xn3[:], hT=hT3[:], n=TLT, lay=1, sc=4, sh=3),
        ]
        XC, G, Y = areaD, areaC, areaB
        RT, IT, A = areaA[:, 0:4, :], areaA[:, 4:8, :], areaE[:]
        rounds = [(0, 0), (1, 0), (0, 1), (1, 1)]

        def mod_banks(i):
            return duo if i <= 2 else wide

        def seg(a, i):
            return a[:, 0:TL] if i == 0 else a[:, CX:CX + TC]

        block = es.enter_context(nc.Block())

        @block.sync
        def _(sp):
            for dst, src in (
                (rowsA[0:8], c.rearrange("b (k q) -> (b k) q", q=P)), (rowsA[8:16], c_ctx.rearrange("(k q) -> k q", q=P)),
                (rowsA[16:32], norm_mix.rearrange("l (k q) -> (l k) q", q=P)),
                (rowsA[32:48], norm_ffn.rearrange("l (k q) -> (l k) q", q=P)),
            ):
                sp.dma_start(dst, src).then_inc(s_parA, 16)
            for t in range(TT):
                src = x_d[t * P:(t + 1) * P, :] if t < TLT else ctx_d[(t - TLT) * P:(t - TLT + 1) * P, :]
                sp.dma_start(stages[0]["x"][:, t, :], src).then_inc(s_x0[t], 16)

            def load(name, slot, before):
                if before >= 1:
                    sp.wait_ge(used[slot], before)
                dst = ring[:, slot, :]
                if name[0] == "ada":
                    lay, g = divmod(name[1], 3)
                    src = ada_w[lay, name[2] * P:(name[2] + 1) * P, g * MODW:(g + 1) * MODW]
                elif name[0] == "lru_in":
                    dst = dst.rearrange("p (k n) -> p k n", k=KD)
                    src = lru_w_in[0].rearrange("(k p) n -> p k n", p=P)[:, :, name[1] * 256:(name[1] + 1) * 256]
                elif name[0] == "gate":
                    dst = dst.rearrange("p (n j) -> p n j", j=P)
                    src = lru_gate_w[0, name[1]].rearrange("g n k j -> k (g n) j")
                elif name[0] in ("lru_out", "w_o"):
                    dst = dst.rearrange("p (k n) -> p k n", k=2)
                    src = (lru_w_out if name[0] == "lru_out" else mla_w_o)[0]
                    src = src.rearrange("(k p) n -> p k n", p=P)[:, 2 * name[1]:2 * name[1] + 2, :]
                elif name[0] == "mla_in":
                    k0, k1 = MLA_K[name[1]]
                    dst = dst[:, 0:(k1 - k0) * MZ].rearrange("p (k n) -> p k n", n=MZ)
                    src = mla_w_in[0].rearrange("(k p) n -> p k n", p=P)[:, k0:k1, :]
                elif name[0] == "uq":
                    dst, src = dst[:, 0:H * QK], mla_w_uq[0, name[1] * P:(name[1] + 1) * P, :]
                elif name[0] == "ukv":
                    src = mla_w_ukv[0, name[1] * P:(name[1] + 1) * P, :]
                sp.dma_start(dst, src).then_inc(landed[slot], 16)

            def experts(lay):
                up = moe_w_up[lay].rearrange("e (k p) (s h n) -> e p k s h n", p=P, s=2, h=2)
                down = moe_w_down[lay].rearrange("e (k p) n -> e p k n", p=P)
                with sp.Fori(0, E) as e:
                    for j in range(NCH):
                        sp.wait_ge(used[j], e + USED0[lay][j])
                        if j < NS:
                            h, s, q = j // 4, j % 4 // 2, j % 2
                            dst = chunk_at(j).rearrange("p (k n) -> p k n", k=4)
                            sp.dma_start(dst, up[e, :, 4 * q:4 * q + 4, s, h, :]).then_inc(landed[j], 16)
                        else:
                            dst = chunk_at(j).rearrange("p (k n) -> p k n", k=2)
                            sp.dma_start(dst, down[e, :, (j - NS) * 2:(j - NS) * 2 + 2, :]).then_inc(landed[j], 16)

            def load_bias(i):
                lay, g = divmod(i, 3)
                if i == 0:
                    sp.wait_ge(s_const, NCONST)
                if i >= 2:
                    sp.wait_ge(s_modst, 32 * (i - 1))
                    sp.wait_ge(s_modtr, i - 1)
                for v_ in range(2):
                    sp.dma_start(modbias[v_:P:32, i % 2, :],
                                 ada_b[lay, g * MODW:(g + 1) * MODW].rearrange("(n f) -> n f", f=BANK)).then_inc(s_bias, 16)

            for n, (name, slot, before) in enumerate(head_chunks):
                if name[0] == "ada" and name[2] == KD - 1:
                    load_bias(name[1])
                load(name, slot, before)
                if n == 7:
                    for dst, src in (
                        (rowsB[B_CONV:B_CB], lru_conv_w.rearrange("a w (k q) -> (a w k) q", q=P)),
                        (rowsB[B_CB:B_GB], lru_conv_b.rearrange("a (k q) -> (a k) q", q=P)),
                        (rowsB[B_GB:B_LAM], lru_gate_b.rearrange("a d g (k q) -> (a d g k) q", q=P)),
                        (rowsB[B_LAM:B_QN], lru_lambda.rearrange("a d (k q) -> (a d k) q", q=P)),
                        (rowsB[B_QN:B_KVN], mla_q_norm.rearrange("a (k q) -> (a k) q", q=P)),
                        (rowsB[B_KVN:NB], mla_kv_norm.rearrange("a (k q) -> (a k) q", q=P)),
                    ):
                        sp.dma_start(dst, src).then_inc(s_parB, 16)
                    for lay in range(L):
                        sp.dma_start(router[:, lay], moe_router[lay].rearrange("(k p) e -> p k e", p=P)).then_inc(s_router, 16)
            experts(0)
            for name, slot, before in mla_chunks:
                load(name, slot, before)
            experts(1)

        @block.tensor
        def _(pe):
            mm = nc.tensor.matmul

            def arrived(name):
                slot, n = place[name]
                pe.wait_ge(landed[slot], 16 * n)

            def turn(dst, src, plain=False):
                n = src.shape[0]
                if plain:
                    return mm(dst, src, ident[0:n, 0:n], start=True, stop=True)
                return nc.tensor.transpose(dst, src, ident[0:n, 0:n])

            def ada_chunk(i, k, owed=None):
                if i >= 1 and k == 0:
                    pe.wait_ge(s_modev, i)
                arrived(("ada", i, k))
                w = ring_at(("ada", i, k))
                for n in range(4):
                    ins = mm(mod_banks(i)[32 * n:32 * n + 2, 0, :], silu_c[:, k, :], w[:, n * BANK:(n + 1) * BANK],
                             start=k == 0, stop=k == KD - 1)
                    if owed and n == 0:
                        ins.then_inc(owed, 1)
                ins.then_inc(used[place[("ada", i, k)][0]], 1)

            def ada(i, owed=None):
                for k in range(KD):
                    ada_chunk(i, k, owed if k == 0 else None)

            def turn_mods(i, owed=None):
                pe.wait_ge(s_modev, i + 1)
                if i >= 1:
                    pe.wait_ge(s_modcol, i)
                for j in range(4):
                    ins = turn(mod_banks(i)[:, 1, j * P:(j + 1) * P], modbias[:, i % 2, j * P:(j + 1) * P])
                    if owed and j == 0:
                        ins.then_inc(owed, 1)
                ins.then_inc(s_modtr, 1)

            def turn_tile(s, t, owed=None):
                pe.wait_ge(s_xn, N0[s] + t + 1)
                for half, s_ev in ((0, s_hTa), (1, s_hTd)):
                    if t >= 1:
                        pe.wait_ge(s_ev, N0[s] + t)
                    for k in range(4):
                        f = (4 * half + k) * P
                        ins = turn(turned[:, half, k * P:(k + 1) * P], stages[s]["xn"][:, t, f:f + P])
                        if owed:
                            ins.then_inc(owed, 1)
                            owed = None
                    ins.then_inc(s_xtr, 1)

            pe.wait_ge(s_const, NCONST)
            pe.wait_ge(s_parA, 64)
            turn(turned[:, 0, 0:48], rowsA[0:48, :]).then_inc(s_partr, 1)
            pe.wait_ge(s_silu_c, 1)
            ada(0)
            turn_mods(0)
            pe.wait_ge(s_parB, 96)
            turn(wide[:, 3, 0:NB], rowsB[0:NB, :]).then_inc(s_partr, 1)
            pe.wait_ge(s_pcol, 1)
            for t in range(TT):
                turn_tile(0, t)

            pe.wait_ge(s_hTa, TT)
            pe.wait_ge(s_hTd, TT)
            hT = stages[0]["hT"]
            owed = None
            for q in range(2 * KD):
                name = ("lru_in", (q // 2 + KD // 2) % KD)
                arrived(name)
                w = ring_at(name).rearrange("p (k n) -> p k n", k=KD)[:, :, (q % 2) * P:(q % 2 + 1) * P]
                if q == 1:
                    pe.wait_ge(s_pcol, 2)
                if q >= 2:
                    if q - 2 < KD:
                        pe.wait_ge(s_ucopy, q - 1)
                    else:
                        pe.wait_ge(s_gelu, q - 1 - KD)
                b = 2 * (q % 2)
                for k in range(KD):
                    first = mm(wide[:, b, :], w[:, k, :], hT[:, k, 0:TL], start=k == 0, stop=k == KD - 1)
                    if owed and k == 0:
                        first.then_inc(owed, 1)
                        owed = None
                    ins = mm(wide[:, b + 1, 0:TC], w[:, k, :], hT[:, k, TL:T], start=k == 0, stop=k == KD - 1)
                ins.then_inc(s_z, 1)
                if q % 2:
                    owed = used[place[name][0]]
                for what, *at in side[q]:
                    (ada_chunk if what == "ada" else turn_mods)(*at, owed=owed)
                    owed = None

            def gates(r, owed=None):
                d, half = rounds[r]
                arrived(("gate", d))
                w = ring_at(("gate", d)).rearrange("p (n j) -> p n j", j=P)
                for jj in range(4):
                    n, u = 4 * half + jj, 4 * r + jj
                    pe.wait_ge(s_xc, n + 1)
                    for g, banks in ((0, turned), (1, duo)):
                        if u >= 1:
                            pe.wait_ge(s_sig, 2 * (u - 1) + g + 1)
                        ins = mm(banks[:, 0, :], w[:, g * KD + n, :], seg(XC[:, n, :], 0), start=True, stop=True)
                        if owed:
                            ins.then_inc(owed, 1)
                            owed = None
                        mm(banks[:, 1, 0:TC], w[:, g * KD + n, :], seg(XC[:, n, :], 1), start=True, stop=True).then_inc(s_gmm, 1)

            pe.wait_ge(s_modev, 3)
            pe.wait_ge(s_modcol, 3)
            gates(0, owed)
            pe.wait_ge(s_gelu, KD)
            ada(3)
            gates(1)
            turn_mods(3)
            ada(4)
            gates(2)
            turn_mods(4, used[place[("gate", 0)][0]])
            ada(5)
            gates(3)
            turn_mods(5, used[place[("gate", 1)][0]])

            def out_project(lay, s, lhs, names):
                n_t = FFT[lay]
                for step in range(n_t + 2):
                    if step < n_t:
                        t = step
                        if t >= 2:
                            pe.wait_ge(s_x1[lay], t - 1)
                        b = 2 * (t % 2)
                        for k in range(KD):
                            if t == 0 and k % 2 == 0:
                                arrived(names[k // 2])
                            w = ring_at(names[k // 2]).rearrange("p (k n) -> p k n", k=2)[:, k % 2, :]
                            for n in range(2):
                                ins = mm(wide[:, b + n, :], lhs(k, t), w[:, n * BANK:(n + 1) * BANK],
                                         start=k == 0, stop=k == KD - 1)
                            if t == n_t - 1 and k % 2 and k < KD - 1:
                                ins.then_inc(used[place[names[k // 2]][0]], 1)
                        ins.then_inc(s_o[lay], 1)
                    if 1 <= step <= n_t:
                        turn_tile(s, step - 1, used[place[names[3]][0]] if step == n_t else None)
                    if step >= 2:
                        t = step - 2
                        pe.wait_ge(s_hTa, N0[s] + t + 1)
                        pe.wait_ge(s_hTd, N0[s] + t + 1)
                        for k in range(KD):
                            ins = mm(duo[:, 0, t * E:(t + 1) * E], stages[s]["hT"][:, k, t * P:(t + 1) * P],
                                     router[:, lay, k, :], start=k == 0, stop=k == KD - 1)
                        ins.then_inc(s_log[lay], 1)

            def turn_choice(lay):
                pe.wait_ge(s_aff, lay + 1)
                for t in range(TLT):
                    ins = turn(turned[0:48, 0, t * P:(t + 1) * P], aff2[:, t, :])
                ins.then_inc(s_afft, 1)
                pe.wait_ge(s_top, lay + 1)
                for i in range(2):
                    ins = turn(duo[0:CAP[lay], 1, i * E:(i + 1) * E], turn_in[:, i, 0:CAP[lay]])
                ins.then_inc(s_topt, 1)

            def experts(lay):
                M = CAP[lay]

                def turn_rows(e, part):
                    if part == 0:
                        pe.wait_ge(s_gath[lay], e * 16 + 16)
                    pe.wait_ge(s_hidT[lay], e * 2 + (1 + part))
                    for k in range(4):
                        ins = turn(turned[:, part, k * M:(k + 1) * M], xg[0:M, (4 * part + k) * P:(4 * part + k + 1) * P],
                                   plain=k == 0 and M <= 64)
                    ins.then_inc(s_xgtr[lay], 1)

                def half(e, h):
                    for s in range(2):
                        if s == 0:
                            pe.wait_ge(s_hid[lay], e * 2 + (h + 1))
                        for q in range(2):
                            j = 4 * h + 2 * s + q
                            pe.wait_ge(used[j], e + (USED0[lay][j] + 1))
                            wh, wl = [w[:, j % NW, :].rearrange("p (k n) -> p k n", k=4) for w in (w_hi, w_lo)]
                            if h == 0 and s == 0:
                                pe.wait_ge(s_xgT[lay], e * 2 + (q + 1))
                            for k in range(4):
                                kk = 4 * q + k
                                first, last_ = kk == 0, kk == KD - 1
                                if lay == 0:
                                    x_hi, x_lo = xs[:, kk, 0:M], xs[:, kk, M:2 * M]
                                    o = wide[0:M, 2 * h + s, :]
                                    mm(o, x_hi, wh[:, k, :], start=first, stop=False)
                                    mm(o, x_hi, wl[:, k, :], start=False, stop=False)
                                    ins = mm(o, x_lo, wh[:, k, :], start=False, stop=last_)
                                else:
                                    both = xs[:, kk, 0:2 * M]
                                    o = wide[0:2 * M, 2 * h + s, :]
                                    mm(o, both, wh[:, k, :], start=first, stop=False)
                                    ins = mm(o, both, wl[:, k, :], start=False, stop=last_)
                            ins.then_inc(s_wdone[lay], 1)
                        if h == 1 and s == 0:
                            turn_hid(e, 0)

                def turn_hid(e, h):
                    pe.wait_ge(s_hid[lay], e * 2 + (h + 3))
                    pe.wait_ge(s_xgT[lay], e * 2 + (h + 1))
                    for k in range(4):
                        ins = turn(turned[:, h, k * M:(k + 1) * M], hid[0:M, k * P:(k + 1) * P], plain=k == 0 and M <= 64)
                    ins.then_inc(s_hidtr[lay], 1)

                def down(e, h):
                    pe.wait_ge(s_hidT[lay], e * 2 + (h + 3))
                    for j in (NS + 2 * h, NS + 1 + 2 * h):
                        pe.wait_ge(landed[j], e * 16 + 16 * (LANDED0[lay][j] + 1))
                        w = chunk_at(j).rearrange("p (k n) -> p k n", k=2)
                        for k in range(2):
                            kk = (j - NS) * 2 + k
                            for n in range(2):
                                ins = mm(duo[0:M, n, :], hidT[:, h, kk % 4, 0:M], w[:, k, n * BANK:(n + 1) * BANK],
                                         start=kk == 0, stop=kk == KD - 1)
                        ins.then_inc(used[j], 1)

                def body(e, last):
                    half(e, 0)
                    half(e, 1)
                    pe.wait_ge(s_ye[lay], e + 1)
                    down(e, 0)
                    turn_hid(e, 1)
                    if not last:
                        turn_rows(e + 1, 0)
                    down(e, 1)
                    if not last:
                        turn_rows(e + 1, 1)

                turn_rows(0, 0)
                turn_rows(0, 1)
                with pe.Fori(0, E - 1) as e:
                    body(e, False)
                body(E - 1, True)

            pe.wait_ge(s_yg, KD)
            pe.wait_ge(s_modev, 6)
            pe.wait_ge(s_modcol, 6)

            def lru_lhs(k, t):
                at = t * P if t < TLT else CX + (t - TLT) * P
                return Y[:, k, at:at + P]

            out_project(0, 1, lru_lhs, [("lru_out", j) for j in range(4)])
            turn_choice(0)
            experts(0)

            for t in range(TT):
                turn_tile(2, t)
            hT = stages[2]["hT"]
            pe.wait_ge(s_hTa, N0[2] + TT)
            pe.wait_ge(s_hTd, N0[2] + TT)
            for j in range(3):
                arrived(("mla_in", j))

            def mla_w(k):
                j = [n for n, (a, b) in enumerate(MLA_K) if a <= k < b][0]
                return ring_at(("mla_in", j))[:, (k - MLA_K[j][0]) * MZ:(k - MLA_K[j][0] + 1) * MZ]

            for step in range(TT + 1):
                if step < TT:
                    t = step
                    if t >= 2:
                        pe.wait_ge(s_cqn, t - 1)
                    else:
                        pe.wait_ge(s_hid[0], 2 * E + 2)
                    b = 2 * (t % 2)
                    for k in range(KD):
                        lhs = hT[:, k, t * P:(t + 1) * P]
                        if t < TLT:
                            mm(wide[:, b, 0:QL], lhs, mla_w(k)[:, 0:QL], start=k == 0, stop=k == KD - 1)
                        ins = mm(wide[:, b + 1, 0:MZ - QL], lhs, mla_w(k)[:, QL:MZ], start=k == 0, stop=k == KD - 1)
                        if t == TT - 1 and k in (2, 5):
                            ins.then_inc(used[place[("mla_in", k // 3)][0]], 1)
                    ins.then_inc(s_mz, 1)
                if step >= 1:
                    t = step - 1
                    pe.wait_ge(s_cqn, t + 1)
                    if t >= 1:
                        pe.wait_ge(s_cqT, t)
                    for k in range(KQ if t < TLT else 0):
                        turn(duo[:, 0, k * P:(k + 1) * P], cqn[:, t % 2, k * P:(k + 1) * P])
                    for k in range(KKV):
                        ins = turn(duo[:, 1, k * P:(k + 1) * P], cqn[:, t % 2, QL + k * P:QL + (k + 1) * P])
                        if step == TT and k == 0:
                            ins.then_inc(used[place[("mla_in", 2)][0]], 1)
                    ins.then_inc(s_cqtr, 1)
            for j in range(KQ):
                arrived(("uq", j))
            for j in range(KKV):
                arrived(("ukv", j))
            pe.wait_ge(s_cqT, TT)
            with pe.Fori(0, NG) as g:
                pe.wait_ge(s_OT, g * 2 + 1)
                for step in range(TLT + 1):
                    if step < TLT:
                        t = step
                        pe.wait_ge(s_qtok, g * 4 + (t + 1))
                        for k in range(KQ):
                            ins = mm(duo[:, t % 2, 0:HG * QK], cqT[:, k, t * P:(t + 1) * P],
                                     ring_at(("uq", k))[:, bass.ds(g * (HG * QK), HG * QK)], start=k == 0, stop=k == KQ - 1)
                        ins.then_inc(s_q, 1)
                    if step >= 1:
                        t = step - 1
                        pe.wait_ge(s_qtok, g * 4 + (t + 3))
                        pe.wait_ge(s_qT, g * 4 + (t + 1))
                        for h in range(HG):
                            ins = turn(turned[0:QK, 0, h * P:(h + 1) * P], qtok[:, t % 2, h, :])
                        ins.then_inc(s_qtr, 1)
                for step in range(TT + 1):
                    if step < TT:
                        t = step
                        pe.wait_ge(s_ktok, g * 6 + (t + 1))
                        if t < 2:
                            pe.wait_ge(s_qtok, g * 4 + (t + 5))
                        for k in range(KKV):
                            ins = mm(duo[:, t % 2, :], ckvT[:, k, t * P:(t + 1) * P],
                                     ring_at(("ukv", k))[:, bass.ds(g * BANK, BANK)], start=k == 0, stop=k == KKV - 1)
                        ins.then_inc(s_kv, 1)
                    if step >= 1:
                        t = step - 1
                        pe.wait_ge(s_ktok, g * 6 + (t + 3))
                        pe.wait_ge(s_kT, g * 6 + (t + 1))
                        for h in range(HG):
                            ins = turn(turned[0:QK, 1, h * P:(h + 1) * P], ktok[:, t % 2, h, :])
                        ins.then_inc(s_ktr, 1)
                pe.wait_ge(s_qT, g * 4 + 5)
                pe.wait_ge(s_kT, g * 6 + 7)

                def scores(u):
                    h, t = divmod(u, TLT)
                    pe.wait_ge(s_exp, g * 16 + (u + 1))
                    b = 2 * (u % 2)
                    q = qT[:, h, t * P:(t + 1) * P]
                    mm(wide[:, b, :], q, kT[:, h, 0:TL], start=True, stop=True)
                    mm(wide[:, b + 1, 0:TC], q, kT[:, h, TL:T], start=True, stop=True).then_inc(s_S, 1)

                def turn_probs(u):
                    h, t = divmod(u, TLT)
                    pe.wait_ge(s_pn, g * 16 + (u + 1))
                    pe.wait_ge(s_PTa, g * 16 + (u + 1))
                    for k in range(4):
                        ins = turn(turned[:, 0, k * P:(k + 1) * P], prob[:, u % 2, k * P:(k + 1) * P])
                    ins.then_inc(s_ptr, 1)
                    pe.wait_ge(s_PTd, g * 16 + (u + 1))
                    for k in range(4, TT):
                        ins = turn(turned[:, 1, (k - 4) * P:(k - 3) * P], prob[:, u % 2, k * P:(k + 1) * P])
                    ins.then_inc(s_ptr, 1)

                def values(h):
                    pe.wait_ge(s_PTa, g * 16 + (4 * h + 5))
                    pe.wait_ge(s_PTd, g * 16 + (4 * h + 5))
                    if h % 2 == 0:
                        pe.wait_ge(s_OT, g * 2 + (h // 2 + 1))
                    r = (h % 2) * VD
                    for k in range(TT):
                        ins = mm(duo[r:r + VD, 0, :], V[:, k, h, :], PT[:, h % 2, k, :], start=k == 0, stop=k == TT - 1)
                    ins.then_inc(s_av, 1)

                U = HG * TLT
                for u in range(U + 2):
                    if u < U:
                        scores(u)
                    if u >= 2:
                        turn_probs(u - 2)
                        if (u - 2) % TLT == TLT - 1 and u - 2 >= TLT:
                            values((u - 2) // TLT - 1)
                values(HG - 1)
            for n, name in enumerate([("uq", j) for j in range(KQ)] + [("ukv", j) for j in range(KKV)]):
                turn(duo[0:32, 1, 32 * n:32 * n + 32], ident[0:32, 0:32]).then_inc(used[place[name][0]], 1)
            pe.wait_ge(s_OT, 2 * NG + 1)
            out_project(1, 3, lambda k, t: OT[:, k, t * P:(t + 1) * P], [("w_o", j) for j in range(4)])
            turn_choice(1)
            experts(1)

        @block.scalar
        def _(act):
            fn = nc.scalar.activation
            chain = Chain(act, s_act)

            def x_ready(eng, s, t):
                if s == 0:
                    eng.wait_ge(s_x0[t], 16)
                elif s == 2:
                    eng.wait_ge(s_x[t], 32)
                else:
                    eng.wait_ge(s_x1[s // 2], t + 1)

            def squares(s, t):
                x_ready(act, s, t)
                chain.step(fn(stages[s]["xn"][:, t, :], stages[s]["x"][:, t, :], ACT.Square, accum_out=stat[:, 0, t:t + 1]))
                fn(stat[:, 1, t:t + 1], stat[:, 0, t:t + 1], ACT.Sqrt, bias=eps[:, 0:1], scale=1.0 / D).then_inc(s_rms, 1)

            def modulate(s, t):
                a = 2 * s + (0 if t < TLT else 1)
                if t == 0:
                    act.wait_ge(s_modcol, (1, 3, 4, 6)[s])
                act.wait_ge(s_xtr, 2 * (N0[s] + t) + 1)
                for k in range(4):
                    ins = fn(stages[s]["hT"][:, k, t * P:(t + 1) * P], turned[:, 0, k * P:(k + 1) * P], ACT.Identity,
                             bias=cols[:, 7 + a, k:k + 1], scale=cols[:, a, k:k + 1])
                ins.then_inc(s_hTa, 1)

            def norm(s):
                n = stages[s]["n"]
                for step in range(n + 1):
                    if step < n:
                        squares(s, step)
                    if step >= 1:
                        modulate(s, step - 1)

            act.wait_ge(s_const, NCONST)
            act.wait_ge(s_pcol, 1)
            fn(silu_c[:].rearrange("p k v -> p v k"), pA[:, 0:16].rearrange("p (v k) -> p v k", v=2), ACT.Silu).then_inc(s_silu_c, 1)
            for t in range(TT):
                squares(0, t)
            for t in range(TT):
                modulate(0, t)
            act.wait_ge(s_lam, 1)
            fn(lam[:, 1, :], lam[:, 0, :], ACT.Exp, scale=-1.0).then_inc(s_lamE, 1)
            for q in range(KD, 2 * KD):
                act.wait_ge(s_z, q + 1)
                b = 2 * (q % 2)
                fn(seg(G[:, q - KD, :], 0), wide[:, b, :], ACT.Gelu_apprx_tanh)
                fn(seg(G[:, q - KD, :], 1), wide[:, b + 1, 0:TC], ACT.Gelu_apprx_tanh).then_inc(s_gelu, 1)
            for r, (d, half) in enumerate(rounds):
                for jj in range(4):
                    n, u = 4 * half + jj, 4 * r + jj
                    if r >= 1:
                        act.wait_ge(s_scan, u - 3)
                    elif jj == 0:
                        act.wait_ge(s_lam, 3)
                    for g, banks, dst in ((0, turned, RT), (1, duo, IT)):
                        act.wait_ge(s_gmm, 2 * u + g + 1)
                        bias = pB[:, B_GB + (2 * d + g) * KD + n:B_GB + (2 * d + g) * KD + n + 1]
                        fn(seg(dst[:, jj, :], 0), banks[:, 0, :], ACT.Sigmoid, bias=bias)
                        fn(seg(dst[:, jj, :], 1), banks[:, 1, 0:TC], ACT.Sigmoid, bias=bias).then_inc(s_sig, 1)
                act.wait_ge(s_lam, 2)
                for jj in range(4):
                    n, u = 4 * half + jj, 4 * r + jj
                    act.wait_ge(s_sig, 2 * u + 2)
                    at = d * KD + n
                    chain.step(fn(A[:, jj, 0:W], RT[:, jj, 0:W], ACT.Exp, scale=lam[:, 2, at:at + 1]))
                    fn(RT[:, jj, 0:W], RT[:, jj, 0:W], ACT.Tanh, scale=lam[:, 3, at:at + 1]).then_inc(s_tanh, 1)
                for jj in range(4):
                    u = 4 * r + jj
                    act.wait_ge(s_v, u + 1)
                    fn(RT[:, jj, 0:W], RT[:, jj, 0:W], ACT.Sqrt).then_inc(s_sqrt, 1)

            def affinities(lay):
                act.wait_ge(s_sub, lay + 1)
                fn(aff[:, 0:FFT[lay], :], aff[:, 0:FFT[lay], :], ACT.Exp).then_inc(s_aexp, 1)

            def experts(lay):
                M = CAP[lay]

                def hi(e, j):
                    act.wait_ge(landed[j], e * 16 + 16 * (LANDED0[lay][j] + 1))
                    act.wait_ge(s_wdone[lay], e * NS + (j + 1))
                    fn(w_hi[:, j % NW, :], chunk_at(j), ACT.Copy).then_inc(s_hi[lay], 1)

                def product(e, j):
                    act.wait_ge(s_wdone[lay], e * NS + (j + 1 + NW))

                def low_rows(e, h, s):
                    product(e, 4 * h + 2 * s + 1)
                    act.wait_ge(s_us if s == 0 else s_gs, e * 2 + (h + (2 if s == 0 else 3)))
                    fn(lo_rows[:], wide[M:2 * M, 2 * h + s, :], ACT.Copy).then_inc(s_lot, 1)

                def silu(e, h):
                    act.wait_ge(s_hid[lay], e * 2 + (h + 2))
                    if lay == 0:
                        product(e, 4 * h + 1)
                        fn(sg[0:M, :], wide[0:M, 2 * h, :], ACT.Silu).then_inc(s_silu[lay], 1)
                    else:
                        act.wait_ge(s_gs, e * 2 + (h + 3))
                        fn(sg[0:M, :], sg[0:M, :], ACT.Silu).then_inc(s_silu[lay], 1)

                def hidden(e, h):
                    act.wait_ge(s_hidtr[lay], e * 2 + (h + 1))
                    fn(hidT[:, h, :, 0:M], turned[:, h, 0:4 * M].rearrange("p (k m) -> p k m", k=4),
                       ACT.Copy).then_inc(s_hidT[lay], 1)

                def body(e, last):
                    hi_next = (lambda j: None) if last else (lambda j: hi(e + 1, j))
                    if lay == 0:
                        hi(e, 4), hi(e, 5), silu(e, 0), hi(e, 6), hi(e, 7)
                        hi_next(0), hi_next(1), silu(e, 1), hidden(e, 0), hi_next(2), hi_next(3), hidden(e, 1)
                    else:
                        hi(e, 4), hi(e, 5), low_rows(e, 0, 0), hi(e, 6), silu(e, 0), hi(e, 7), low_rows(e, 0, 1)
                        hi_next(0), hi_next(1), low_rows(e, 1, 0), hidden(e, 0), hi_next(2), silu(e, 1)
                        hi_next(3), low_rows(e, 1, 1), hidden(e, 1)

                act.wait_ge(s_wdone[lay], NW)
                for j in range(NW):
                    hi(0, j)
                with act.Fori(0, E - 1) as e:
                    body(e, False)
                body(E - 1, True)

            norm(1)
            affinities(0)
            experts(0)
            norm(2)
            for t in range(TT):
                b = 2 * (t % 2)
                act.wait_ge(s_mz, t + 1)
                if t >= 2:
                    act.wait_ge(s_cqtr, t - 1)
                if t < TLT:
                    fn(cqn[:, t % 2, 0:QL], wide[:, b, 0:QL], ACT.Square, accum_out=mx[:, 0, t:t + 1])
                chain.step(fn(cqn[:, t % 2, QL:QL + KVL], wide[:, b + 1, 0:KVL], ACT.Square, accum_out=mx[:, 1, t:t + 1]))
                if t < TLT:
                    fn(mx[:, 2, t:t + 1], mx[:, 0, t:t + 1], ACT.Sqrt, bias=eps[:, 0:1], scale=1.0 / QL)
                fn(mx[:, 3, t:t + 1], mx[:, 1, t:t + 1], ACT.Sqrt, bias=eps[:, 0:1], scale=1.0 / KVL).then_inc(s_mzs, 1)
            with act.Fori(0, NG) as g:
                for t in range(TLT):
                    act.wait_ge(s_qtr, g * 4 + (t + 1))
                    fn(qT[:, :, t * P:(t + 1) * P], turned[0:QK, 0, :].rearrange("p (h n) -> p h n", h=HG),
                       ACT.Copy, scale=SCALE).then_inc(s_qT, 1)
                for t in range(TT):
                    act.wait_ge(s_ktr, g * 6 + (t + 1))
                    fn(kT[:, :, t * P:(t + 1) * P], turned[0:QK, 1, :].rearrange("p (h n) -> p h n", h=HG),
                       ACT.Copy).then_inc(s_kT, 1)
                for u in range(HG * TLT + 2):
                    if u < HG * TLT:
                        b = 2 * (u % 2)
                        act.wait_ge(s_max, g * 16 + (u + 1))
                        if u >= 2:
                            act.wait_ge(s_ptr, g * 32 + (2 * u - 2))
                        fn(prob[:, u % 2, :], wide[:, b:b + 2, :].rearrange("p a n -> p (a n)")[:, 0:T], ACT.Exp,
                           bias=asum[:, 0, u % 4:u % 4 + 1], accum_out=asum[:, 1, u % 4:u % 4 + 1]).then_inc(s_exp, 1)
                    if u >= 2:
                        h, t = divmod(u - 2, TLT)
                        act.wait_ge(s_ptr, g * 32 + (2 * (u - 2) + 1))
                        if t == 0 and h >= 2:
                            act.wait_ge(s_av, g * 4 + (h - 1))
                        fn(PT[:, h % 2, 0:4, t * P:(t + 1) * P], turned[:, 0, :].rearrange("p (k n) -> p k n", k=4),
                           ACT.Copy).then_inc(s_PTa, 1)
            norm(3)
            affinities(1)
            experts(1)
            for t in range(TLT):
                act.wait_ge(s_x[t], 48)
                chain.step(fn(xo_f[:, t, :], x_f[:, t, :], ACT.Square, accum_out=stat[:, 0, t:t + 1]))
                fn(stat[:, 1, t:t + 1], stat[:, 0, t:t + 1], ACT.Sqrt, bias=eps[:, 0:1], scale=1.0 / D).then_inc(s_rms, 1)

        @block.vector
        def _(dve):
            v = nc.vector
            chain = Chain(dve, s_dve)
            marked = [0]

            def mark(s_, n):
                v.memset(marks[:, marked[0]:marked[0] + 1], 1.0).then_inc(s_, n)
                marked[0] += 1

            def normed_tile(s, t):
                dve.wait_ge(s_rms, N0[s] + t + 1)
                chain.step(v.reciprocal(stat[:, 2, t:t + 1], stat[:, 1, t:t + 1]))
                v.tensor_scalar(stages[s]["xn"][:, t, :], stages[s]["x"][:, t, :], stat[:, 2, t:t + 1], None,
                                ALU.mult).then_inc(s_xn, 1)

            def modulate(s, t):
                a = 2 * s + (0 if t < TLT else 1)
                dve.wait_ge(s_xtr, 2 * (N0[s] + t) + 2)
                for k in range(4, 8):
                    ins = v.tensor_scalar(stages[s]["hT"][:, k, t * P:(t + 1) * P], turned[:, 1, (k - 4) * P:(k - 3) * P],
                                          cols[:, a, k:k + 1], cols[:, 7 + a, k:k + 1], ALU.mult, ALU.add)
                ins.then_inc(s_hTd, 1)

            def norm(s):
                n = stages[s]["n"]
                for step in range(n + 1):
                    if step < n:
                        normed_tile(s, step)
                    if step >= 1:
                        modulate(s, step - 1)

            def ada_read(i):
                name = ("ada", i, KD - 1)
                dve.wait_ge(used[place[name][0]], place[name][1])
                dve.wait_ge(s_bias, 32 * (i + 1))
                for n in range(4):
                    rows = slice(32 * n, 32 * n + 2)
                    ins = v.tensor_tensor(modbias[rows, i % 2, :], mod_banks(i)[rows, 0, :], modbias[rows, i % 2, :], ALU.add)
                ins.then_inc(s_modev, 1)

            def columns(a, scale, shift, gain):
                chain.step(v.scalar_tensor_tensor(cols[:, a, :], scale, 1.0, gain, ALU.add, ALU.mult))
                chain.step(v.tensor_copy(cols[:, 7 + a, :], shift))

            def mod_columns(i):
                lay, g = divmod(i, 3)
                dve.wait_ge(s_modtr, i + 1)
                mc = modc[lay]
                for v_ in range(2):
                    at = v_ * 48 + 16 * g
                    chain.step(v.tensor_copy(
                        mc[:, at:at + 16].rearrange("p (n j) -> p n j", n=4),
                        mod_banks(i)[:, 1, :].rearrange("p (j n w) -> p n j w", j=4, n=4)[:, :, :, v_]))
                s = {0: 0, 2: 1, 3: 2, 5: 3}.get(i)
                if s is not None:
                    is_ffn = s % 2
                    gain = pA[:, 16 + 16 * is_ffn + lay * KD:16 + 16 * is_ffn + (lay + 1) * KD]
                    for v_ in range(1 if s == 3 else 2):
                        at = v_ * 48 + (3 * KD if is_ffn else 0)
                        columns(2 * s + v_, mc[:, at + KD:at + 2 * KD], mc[:, at:at + KD], gain)
                mark(s_modcol, 1)

            dve.wait_ge(s_const, NCONST)
            dve.wait_ge(s_partr, 1)
            v.tensor_copy(pA[:], turned[:, 0, 0:48]).then_inc(s_pcol, 1)
            dve.wait_ge(s_pcol, 1)
            for t in range(TT):
                normed_tile(0, t)
            ada_read(0)
            mod_columns(0)
            for t in range(TT):
                modulate(0, t)
            dve.wait_ge(s_partr, 2)
            v.tensor_copy(pB[:, 0:NB], wide[:, 3, 0:NB]).then_inc(s_pcol, 1)

            dve.wait_ge(s_pcol, 2)
            lm = pB[:, B_LAM:B_LAM + 16]
            chain.step(v.tensor_scalar(lam[:, 4, :], lm, -1.0, None, ALU.mult))
            v.tensor_tensor(lam[:, 0, :], lm, lam[:, 4, :], ALU.max).then_inc(s_lam, 1)

            for n in range(KD):
                ub = gmix[:, n % 2, :]
                b = 2 * (n % 2)
                dve.wait_ge(s_z, n + 1)
                v.tensor_copy(ub[:, PADL:PADL + TL], wide[:, b, :])
                v.tensor_copy(ub[:, CX + PADL:CX + PADL + TC], wide[:, b + 1, 0:TC]).then_inc(s_ucopy, 1)
                dve.wait_ge(s_ucopy, n + 1)
                tap = lambda j: pB[:, B_CONV + j * KD + n:B_CONV + j * KD + n + 1]
                chain.step(v.tensor_scalar(XC[:, n, 0:W], ub[:, 0:W], tap(0), pB[:, B_CB + n:B_CB + n + 1], ALU.mult, ALU.add))
                for j in range(1, CONV):
                    ins = v.scalar_tensor_tensor(XC[:, n, 0:W], ub[:, j:j + W], tap(j), XC[:, n, 0:W], ALU.mult, ALU.add)
                    if j < CONV - 1:
                        chain.step(ins)
                ins.then_inc(s_xc, 1)

            dve.wait_ge(s_lamE, 1)
            e_, s_, s2, acc = lam[:, 1, :], lam[:, 5, :], lam[:, 6, :], lam[:, 7, :]
            chain.step(v.tensor_scalar(acc, e_, 2.0, None, ALU.add))
            chain.step(v.reciprocal(s2, acc))
            chain.step(v.tensor_tensor(s_, e_, s2, ALU.mult))
            chain.step(v.tensor_tensor(s2, s_, s_, ALU.mult))
            chain.step(v.tensor_scalar(acc, s2, 2.0 / 17, 2.0 / 15, ALU.mult, ALU.add))
            for odd in (13, 11, 9, 7, 5, 3, 1):
                chain.step(v.tensor_tensor(acc, acc, s2, ALU.mult))
                chain.step(v.tensor_scalar(acc, acc, 2.0 / odd, None, ALU.add))
            chain.step(v.tensor_tensor(acc, acc, s_, ALU.mult))
            chain.step(v.scalar_tensor_tensor(acc, lam[:, 4, :], 0.0, acc, ALU.max, ALU.add))
            v.tensor_scalar(lam[:, 2, :], acc, -LRU_C, None, ALU.mult)
            v.tensor_scalar(lam[:, 3, :], acc, LRU_C, None, ALU.mult).then_inc(s_lam, 1)
            v.memset(areaA[:, :, TL:CX], 0.0).then_inc(s_lam, 1)

            for i in (1, 2):
                ada_read(i)
                mod_columns(i)

            for r, (d, half) in enumerate(rounds):
                for jj in range(4):
                    u = 4 * r + jj
                    dve.wait_ge(s_tanh, u + 1)
                    if u:
                        dve.wait_ge(s_v, u)
                    else:
                        dve.wait_ge(s_xc, KD)
                    sq = gmix[:, 0, 0:W]
                    chain.step(v.tensor_tensor(sq, A[:, jj, 0:W], A[:, jj, 0:W], ALU.mult))
                    v.scalar_tensor_tensor(RT[:, jj, 0:W], sq, 1.0, RT[:, jj, 0:W], ALU.add, ALU.mult).then_inc(s_v, 1)
                for jj in range(4):
                    n, u = 4 * half + jj, 4 * r + jj
                    dve.wait_ge(s_sqrt, u + 1)
                    dve.wait_ge(s_ix, u + 1)
                    chain.step(v.tensor_tensor(IT[:, jj, 0:W], RT[:, jj, 0:W], IT[:, jj, 0:W], ALU.mult))
                    dst = Y[:, n, :] if d == 0 else gmix[:, 1, :]
                    a, x_in = A[:, jj, :], IT[:, jj, :]
                    if d == 0:
                        chain.step(v.tensor_tensor_scan(dst[:, CX:W], a[:, CX:W], x_in[:, CX:W], 0.0, ALU.mult, ALU.add))
                        v.tensor_tensor_scan(dst[:, 0:TL], a[:, 0:TL], x_in[:, 0:TL], dst[:, W - 1:W],
                                             ALU.mult, ALU.add).then_inc(s_scan, 1)
                    else:
                        back = lambda ap, i: seg(ap, i)[:, ::-1]
                        chain.step(v.tensor_tensor_scan(back(dst, 1), back(a, 1), back(x_in, 1), 0.0, ALU.mult, ALU.add))
                        v.tensor_tensor_scan(back(dst, 0), back(a, 0), back(x_in, 0), dst[:, CX:CX + 1],
                                             ALU.mult, ALU.add).then_inc(s_scan, 1)
                        dve.wait_ge(s_scan, u + 1)
                        v.tensor_tensor(seg(Y[:, n, :], 0), seg(Y[:, n, :], 0), seg(dst, 0), ALU.add)
                        v.tensor_tensor(seg(Y[:, n, :], 1), seg(Y[:, n, :], 1), seg(dst, 1), ALU.add).then_inc(s_ysum, 1)
                        dve.wait_ge(s_ysum, 4 * half + jj + 1)
                if r >= 1:
                    mod_columns(r + 2)
                if r <= 2:
                    ada_read(r + 3)

            def residual(lay, s, t):
                dve.wait_ge(s_o[lay], t + 1)
                if lay == 0:
                    dve.wait_ge(s_x[t], 16)
                if t == 0:
                    dve.wait_ge(s_gmix[lay], 32 if lay == 0 else 16)
                g_ = gmix1[:] if lay else gmix[:, 0 if t < TLT else 1, :]
                b = 2 * (t % 2)
                o = stages[s]["xn"][:, t, :]
                chain.step(v.tensor_tensor(o, wide[:, b:b + 2, :].rearrange("p a n -> p (a n)"), g_, ALU.mult))
                v.tensor_tensor(stages[s]["x"][:, t, :], stages[s]["x"][:, t, :], o, ALU.add).then_inc(s_x1[lay], 1)

            def choose(lay):
                n_t, M = FFT[lay], CAP[lay]
                dve.wait_ge(s_log[lay], n_t)
                lg = duo[:, 0, 0:n_t * E].rearrange("p (t e) -> p t e", e=E)
                af = aff[:, 0:n_t, :]
                over = lambda a: a.unsqueeze(2).to_broadcast([P, n_t, E])
                chain.step(v.tensor_reduce(mx[:, 0, 0:n_t], lg, AX_X, ALU.max))
                v.tensor_tensor(af, lg, over(mx[:, 0, 0:n_t]), ALU.subtract).then_inc(s_sub, 1)
                dve.wait_ge(s_aexp, lay + 1)
                chain.step(v.tensor_reduce(mx[:, 1, 0:n_t], af, AX_X, ALU.add))
                chain.step(v.reciprocal(mx[:, 2, 0:n_t], mx[:, 1, 0:n_t]))
                rs = mx[:, 2, 0:n_t].unsqueeze(2).to_broadcast([P, n_t, E])
                ins = v.tensor_tensor(aff2[:, :, 0:E], aff[:, 0:TLT, :], rs[:, 0:TLT, :], ALU.mult)
                if lay == 0:
                    ins = v.tensor_tensor(aff2[:, 0:TT - TLT, 32:48], aff[:, TLT:TT, :], rs[:, TLT:TT, :], ALU.mult)
                ins.then_inc(s_aff, 1)
                dve.wait_ge(s_afft, lay + 1)
                chain.step(v.tensor_copy(affT[:], turned[0:48, 0, :]))
                for r in range(CAPL // 8):
                    at = slice(8 * r, 8 * r + 8)
                    chain.step(v.max(top_v[:, at], affT[:]))
                    chain.step(v.max_index(top_i[:, at], top_v[:, at], affT[:]))
                    if r < CAPL // 8 - 1:
                        chain.step(v.match_replace(affT[:], top_v[:, at], affT[:], -1.0))
                chain.step(v.tensor_copy(top_f[:], top_i[:]))
                v.tensor_copy(turn_in[:, 0, 0:CAPL], top_f[0:E, :])
                ins = v.tensor_copy(turn_in[:, 1, 0:CAPL], top_v[0:E, :])
                if lay == 0:
                    v.tensor_scalar(turn_in[:, 0, CAPL:M], top_f[32:32 + E, 0:CAPC], float(TL), None, ALU.add)
                    ins = v.tensor_copy(turn_in[:, 1, CAPL:M], top_v[32:32 + E, 0:CAPC])
                ins.then_inc(s_top, 1)
                dve.wait_ge(s_topt, lay + 1)
                v.tensor_copy(idx_t[0:M, :], duo[0:M, 1, 0:E])
                chain.step(v.tensor_copy(gate_t[0:M, :], duo[0:M, 1, E:2 * E]))
                mark(s_sel, 1)

            def experts(lay):
                M, s = CAP[lay], 2 * lay + 1
                dve.wait_ge(s_st[lay], 16 * FFT[lay])
                dve.wait_ge(s_nst[lay], 16 * FFT[lay])
                parts = [(0, CAPL, 2 * s)] + ([(CAPL, M, 2 * s + 1)] if lay == 0 else [])
                made = []
                for lo, hi, a in parts:
                    for dst, at in ((mod_a, a), (mod_b, 7 + a)):
                        made.append(v.tensor_copy(dst[:, :, lo:hi], cols[:, at, :].unsqueeze(2).to_broadcast([P, KD, hi - lo])))
                made[-1].then_inc(s_hid[lay], 2)
                mark(s_hidT[lay], 2)
                mark(s_ye[lay], 1)
                if lay == 1:
                    mark(s_gs, 2)
                    mark(s_us, 2)
                for j in range(RING, NCH):
                    mark(used[j], 1)
                mark(s_wdone[lay], NW)
                loop_chain = Chain(dve, s_dloop[lay])
                dve.wait_ge(s_hid[lay], 2)

                def lo(e, j):
                    dve.wait_ge(s_hi[lay], e * NS + (j + 1))
                    v.tensor_tensor(w_lo[:, j % NW, :], chunk_at(j), w_hi[:, j % NW, :].bitcast(F32),
                                    ALU.subtract).then_inc(used[j], 1)

                def rows(e, part):
                    dve.wait_ge(s_xgtr[lay], e * 2 + (part + 1))
                    k = slice(4 * part, 4 * part + 4)
                    hi_, lo_ = xs[:, k, 0:M], xs[:, k, M:2 * M]
                    loop_chain.step(v.tensor_tensor(h32[:, k, 0:M], turned[:, part, 0:4 * M].rearrange("p (k m) -> p k m", k=4),
                                                    mod_a[:, k, 0:M], ALU.mult))
                    loop_chain.step(v.tensor_tensor(h32[:, k, 0:M], h32[:, k, 0:M], mod_b[:, k, 0:M], ALU.add))
                    loop_chain.step(v.tensor_copy(hi_, h32[:, k, 0:M]))
                    v.tensor_tensor(lo_, h32[:, k, 0:M], hi_.bitcast(F32), ALU.subtract).then_inc(s_xgT[lay], 1)

                def gate_sum(e, h):
                    if lay == 1:
                        dve.wait_ge(s_lot, e * 4 + (2 * h + 1))
                        dve.wait_ge(s_hid[lay], e * 2 + (h + 2))
                        v.tensor_tensor(sg[0:M, :], wide[0:M, 2 * h, :], lo_rows[:], ALU.add).then_inc(s_gs, 1)

                def hidden(e, h):
                    up = wide[0:M, 2 * h + 1, :]
                    if h == 1:
                        dve.wait_ge(s_hidtr[lay], e * 2 + 1)
                    if lay == 1:
                        dve.wait_ge(s_lot, e * 4 + (2 * h + 2))
                        v.tensor_tensor(hid[0:M, :], up, lo_rows[:], ALU.add).then_inc(s_us, 1)
                        dve.wait_ge(s_us, e * 2 + (h + 3))
                        up = hid[0:M, :]
                    else:
                        dve.wait_ge(s_wdone[lay], e * NS + (4 * h + 4 + NW))
                    dve.wait_ge(s_silu[lay], e * 2 + (h + 1))
                    v.tensor_tensor(hid[0:M, :], up, sg[0:M, :], ALU.mult).then_inc(s_hid[lay], 1)

                def body(e, last):
                    loop_chain.n = e * 7 + 6
                    lo_next = (lambda j: None) if last else (lambda j: lo(e + 1, j))
                    lo(e, 4), lo(e, 5), gate_sum(e, 0), lo(e, 6), lo(e, 7), hidden(e, 0)
                    dve.wait_ge(s_ye[lay], e + 1)
                    loop_chain.step(v.tensor_copy(gate_c[0:M, 0:1], gate_t[0:M, bass.ds(e, 1)]))
                    lo_next(0), lo_next(1), gate_sum(e, 1), lo_next(2), lo_next(3), hidden(e, 1)
                    if not last:
                        rows(e + 1, 0)
                        rows(e + 1, 1)
                    dve.wait_ge(used[NCH - 1], e + (USED0[lay][NCH - 1] + 1))
                    dve.wait_ge(s_scat[lay], e * 16 + 32)
                    v.scalar_tensor_tensor(ye[0:M, :], duo[0:M, :, :].rearrange("p a n -> p (a n)"), gate_c[0:M, 0:1],
                                           gffn[0:M, :], ALU.mult, ALU.mult).then_inc(s_ye[lay], 1)

                for j in range(NW):
                    lo(0, j)
                rows(0, 0)
                rows(0, 1)
                dve.wait_ge(s_scat[lay], 32)
                with dve.Fori(0, E - 1) as e:
                    body(e, False)
                body(E - 1, True)

            def residual_norm(lay):
                s, n = 2 * lay + 1, FFT[lay]
                for step in range(n + 2):
                    if step < n:
                        residual(lay, s, step)
                    if 1 <= step <= n:
                        normed_tile(s, step - 1)
                    if step >= 2:
                        modulate(s, step - 2)

            residual_norm(0)
            choose(0)
            experts(0)

            norm(2)

            def turn_angles(dst, src, n, t):
                x1 = src.rearrange("p n (a h f) -> p n a h f", a=2, h=2)[:, :, :, 0, :]
                x2 = src.rearrange("p n (a h f) -> p n a h f", a=2, h=2)[:, :, :, 1, :]
                o1 = dst.rearrange("p n (a h f) -> p n a h f", a=2, h=2)[:, :, :, 0, :]
                o2 = dst.rearrange("p n (a h f) -> p n a h f", a=2, h=2)[:, :, :, 1, :]
                cos, sin = [ropes[:, t, i, :].rearrange("p (a f) -> p a f", a=2).unsqueeze(1).to_broadcast([P, n, 2, FQ]) for i in range(2)]
                tmp = [rtmp[:, j, 0:n * 2 * FQ].rearrange("p (n a f) -> p n a f", n=n, a=2) for j in range(4)]
                for j, (a_, b_) in enumerate(((x1, cos), (x2, sin), (x1, sin), (x2, cos))):
                    ins = v.tensor_tensor(tmp[j], a_, b_, ALU.mult)
                return ins, [(o1, tmp[0], tmp[1], ALU.subtract), (o2, tmp[2], tmp[3], ALU.add)]

            dve.wait_ge(s_rope, 16)
            for step in range(TT + 1):
                if step < TT:
                    t = step
                    b = 2 * (t % 2)
                    dve.wait_ge(s_mzs, t + 1)
                    if t:
                        dve.wait_ge(s_cqn, t)
                    if t < TLT:
                        v.reciprocal(lam[:, 4, t:t + 1], mx[:, 2, t:t + 1])
                    chain.step(v.reciprocal(lam[:, 5, t:t + 1], mx[:, 3, t:t + 1]))
                    if t < TLT:
                        v.tensor_scalar(cqn[:, t % 2, 0:QL], wide[:, b, 0:QL], lam[:, 4, t:t + 1], None, ALU.mult)
                    v.tensor_scalar(cqn[:, t % 2, QL:QL + KVL], wide[:, b + 1, 0:KVL], lam[:, 5, t:t + 1], None, ALU.mult)
                    kr = wide[:, b + 1, KVL:KVL + ROPE]
                    if t < TLT:
                        chain.step(v.tensor_copy(kraw[:, t % 2, :], kr))
                        ins, rest = turn_angles(krr[:, t:t + 1, :], kraw[:, t % 2:t % 2 + 1, :], 1, t)
                        chain.step(ins)
                        for o, a_, b_, op in rest:
                            ins = v.tensor_tensor(o, a_, b_, op)
                        ins.then_inc(s_cqn, 1)
                    else:
                        v.tensor_copy(krr[:, t, :], kr).then_inc(s_cqn, 1)
                if step >= 1:
                    t = step - 1
                    dve.wait_ge(s_cqtr, t + 1)
                    for k in range(KQ if t < TLT else 0):
                        v.tensor_scalar(cqT[:, k, t * P:(t + 1) * P], duo[:, 0, k * P:(k + 1) * P],
                                        pB[:, B_QN + k:B_QN + k + 1], None, ALU.mult)
                    for k in range(KKV):
                        ins = v.tensor_scalar(ckvT[:, k, t * P:(t + 1) * P], duo[:, 1, k * P:(k + 1) * P],
                                              pB[:, B_KVN + k:B_KVN + k + 1], None, ALU.mult)
                    ins.then_inc(s_cqT, 1)
            dve.wait_ge(s_cqT, TT)
            for s_, n in ((s_qtok, 2), (s_qT, 1), (s_ktok, 2), (s_kT, 1), (s_exp, 2), (s_PTa, 1), (s_PTd, 1), (s_OT, 1)):
                mark(s_, n)
            loop_chain = Chain(dve, s_dloop[2])
            with dve.Fori(0, NG) as g:
                loop_chain.n = g * TLT
                for t in range(TLT):
                    dve.wait_ge(s_q, g * 4 + (t + 1))
                    dve.wait_ge(s_qtok, g * 4 + (t + 2))
                    if t >= 2:
                        dve.wait_ge(s_qtr, g * 4 + (t - 1))
                    q4 = duo[:, t % 2, 0:HG * QK].rearrange("p (h n) -> p h n", h=HG)
                    v.tensor_copy(qtok[:, t % 2, :, 0:NOPE], q4[:, :, 0:NOPE])
                    ins, rest = turn_angles(qtok[:, t % 2, :, NOPE:QK], q4[:, :, NOPE:QK], HG, t)
                    loop_chain.step(ins)
                    for o, a_, b_, op in rest:
                        ins = v.tensor_tensor(o, a_, b_, op)
                    ins.then_inc(s_qtok, 1)
                for t in range(TT):
                    dve.wait_ge(s_kv, g * 6 + (t + 1))
                    if t >= 2:
                        dve.wait_ge(s_ktr, g * 6 + (t - 1))
                    kv4 = duo[:, t % 2, :].rearrange("p (h n) -> p h n", h=HG)
                    v.tensor_copy(ktok[:, t % 2, :, 0:NOPE], kv4[:, :, 0:NOPE])
                    v.tensor_copy(ktok[:, t % 2, :, NOPE:QK], krr[:, t:t + 1, :].to_broadcast([P, HG, ROPE]))
                    v.tensor_copy(V[:, t, :, :], kv4[:, :, NOPE:NOPE + VD]).then_inc(s_ktok, 1)
                U = HG * TLT

                def pair_out(pair):
                    dve.wait_ge(s_av, g * 4 + (2 * pair + 2))
                    v.tensor_copy(OT[:, bass.ds(g * 2 + pair, 1), :], duo[:, 0:1, :]).then_inc(s_OT, 1)

                for u in range(U + 2):
                    if u < U:
                        b = 2 * (u % 2)
                        dve.wait_ge(s_S, g * 16 + (u + 1))
                        v.tensor_reduce(asum[:, 0, u % 4:u % 4 + 1], wide[:, b:b + 2, :].rearrange("p a n -> p (a n)")[:, 0:T],
                                        AX_X, ALU.max, negate=True).then_inc(s_max, 1)
                    if 1 <= u <= U:
                        dve.wait_ge(s_exp, g * 16 + (u + 2))
                        c_ = (u - 1) % 4
                        v.reciprocal(asum[:, 2, c_:c_ + 1], asum[:, 1, c_:c_ + 1]).then_inc(s_rs, 1)
                    if u >= 2:
                        h, t = divmod(u - 2, TLT)
                        dve.wait_ge(s_ptr, g * 32 + (2 * (u - 2) + 2))
                        if t == 0 and h >= 2:
                            dve.wait_ge(s_av, g * 4 + (h - 1))
                        v.tensor_copy(PT[:, h % 2, 4:TT, t * P:(t + 1) * P],
                                      turned[:, 1, 0:2 * P].rearrange("p (k n) -> p k n", k=2)).then_inc(s_PTd, 1)
                        if u - 2 == 3 * TLT - 1:
                            pair_out(0)
                pair_out(1)
            residual_norm(1)
            choose(1)
            experts(1)
            dve.wait_ge(s_nf, 16)
            for t in range(TLT):
                dve.wait_ge(s_rms, N0[4] + t + 1)
                chain.step(v.reciprocal(stat[:, 2, t:t + 1], stat[:, 1, t:t + 1]))
                v.scalar_tensor_tensor(xo_f[:, t, :], x_f[:, t, :], stat[:, 2, t:t + 1], nf[:], ALU.mult, ALU.mult).then_inc(s_fin, 1)

        @block.gpsimd
        def _(pool):
            g_ = nc.gpsimd
            g_.memset(ident[:], 0.0).then_inc(s_const, 1)
            pool.wait_ge(s_const, 1)
            g_.affine_select(out=ident[:], in_=ident[:], compare_op=ALU.not_equal, fill=1.0, base=0,
                             pattern=[[-1, P]], channel_multiplier=1).then_inc(s_const, 1)
            g_.memset(eps[:], EPS).then_inc(s_const, 1)
            g_.memset(aff2[:], -1.0).then_inc(s_const, 1)
            g_.memset(gmix[:], 0.0).then_inc(s_const, 1)
            g_.memset(idx_t[:], 0).then_inc(s_const, 1)
            g_.memset(marks[:], 0.0).then_inc(s_const, 1)
            g_.memset(gate_t[:], 0.0).then_inc(s_const, 1)
            g_.memset(stat[:], 1.0).then_inc(s_const, 1)
            g_.memset(modbias[:], 0.0).then_inc(s_const, 1)

            def mod_store(i):
                lay, g = divmod(i, 3)
                pool.wait_ge(s_modev, i + 1)
                for v_ in range(2):
                    pool.dma_start(mods[lay, v_, g * MODW:(g + 1) * MODW].rearrange("(n f) -> n f", f=BANK),
                                   modbias[v_:P:32, i % 2, :]).then_inc(s_modst, 16)
                pool.wait_ge(s_modst, 32 * (i + 1))

            for i in range(3):
                mod_store(i)
            for r, (d, half) in enumerate(rounds):
                for jj in range(4):
                    n, u = 4 * half + jj, 4 * r + jj
                    pool.wait_ge(s_sig, 2 * u + 2)
                    pool.wait_ge(s_xc, n + 1)
                    g_.tensor_tensor(IT[:, jj, 0:W], IT[:, jj, 0:W], XC[:, n, 0:W], ALU.mult).then_inc(s_ix, 1)
                if d == 1:
                    for jj in range(4):
                        n = 4 * half + jj
                        pool.wait_ge(s_ysum, n + 1)
                        g_.tensor_tensor(seg(Y[:, n, :], 0), seg(Y[:, n, :], 0), seg(G[:, n, :], 0), ALU.mult)
                        g_.tensor_tensor(seg(Y[:, n, :], 1), seg(Y[:, n, :], 1), seg(G[:, n, :], 1), ALU.mult).then_inc(s_yg, 1)
                if r == 3:
                    pool.wait_ge(s_ix, 16)
                    pool.wait_ge(s_gmm, 32)
                    for t in range(TT):
                        src = x_d[t * P:(t + 1) * P, :] if t < TLT else ctx_d[(t - TLT) * P:(t - TLT + 1) * P, :]
                        pool.dma_start(stages[1]["x"][:, t, :], src).then_inc(s_x[t], 16)
                    pool.wait_ge(s_ysum, KD)
                    for v_ in range(2):
                        pool.dma_start(gmix[:, v_, :], mods[0, v_:v_ + 1, 2 * D:3 * D].to_broadcast([P, D])).then_inc(s_gmix[0], 16)
                if r <= 2:
                    mod_store(r + 3)

            def stores(lay):
                s, n = 2 * lay + 1, FFT[lay]
                for step in range(n + 1):
                    if step < n:
                        pool.wait_ge(s_x1[lay], step + 1)
                        pool.dma_start(stream[step * P:(step + 1) * P, :], stages[s]["x"][:, step, :]).then_inc(s_st[lay], 16)
                    if step >= 1:
                        t = step - 1
                        pool.wait_ge(s_xn, N0[s] + t + 1)
                        pool.dma_start(normed[t * P:(t + 1) * P, :], stages[s]["xn"][:, t, :]).then_inc(s_nst[lay], 16)
                pool.wait_ge(s_st[lay], 16 * n)
                pool.wait_ge(s_nst[lay], 16 * n)

            def experts(lay):
                M = CAP[lay]
                pool.wait_ge(s_sel, lay + 1)
                for v_, lo, hi in ((0, 0, CAPL), (1, CAPL, M)) if lay == 0 else ((0, 0, M // 2), (0, M // 2, M)):
                    pool.dma_start(gffn[lo:hi, :], mods[lay, v_:v_ + 1, 5 * D:6 * D].to_broadcast([hi - lo, D])).then_inc(s_scat[lay], 16)

                def gather(e):
                    b = e % 2
                    g_.tensor_copy(idx_c[0:M, b:b + 1], idx_t[0:M, e:e + 1]).then_inc(s_idxc[lay], 1)
                    pool.wait_ge(s_idxc[lay], e + 1)
                    pool.indirect_dma_start(out=xg[0:M, :], out_offset=None, in_=normed,
                                            in_offset=bass.IndirectOffsetOnAxis(ap=idx_c[0:M, b:b + 1], axis=0)).then_inc(s_gath[lay], 16)

                gather(0)
                for e in range(E):
                    pool.wait_ge(s_scat[lay], e * 16 + 32)
                    if e + 1 < E:
                        pool.wait_ge(s_xgtr[lay], e * 2 + 2)
                        gather(e + 1)
                    pool.wait_ge(s_ye[lay], e + 2)
                    b = e % 2
                    pool.indirect_dma_start(out=stream, out_offset=bass.IndirectOffsetOnAxis(ap=idx_c[0:M, b:b + 1], axis=0),
                                            in_=ye[0:M, :], in_offset=None, compute_op=ALU.add).then_inc(s_scat[lay], 16)
                pool.wait_ge(s_scat[lay], 32 + 16 * E)

            stores(0)
            experts(0)
            for t in range(TT):
                pool.dma_start(x_b[:, t, :], stream[t * P:(t + 1) * P, :]).then_inc(s_x[t], 16)
            pool.dma_start(gmix1[:], mods[1, 0:1, 2 * D:3 * D].to_broadcast([P, D])).then_inc(s_gmix[1], 16)
            pool.dma_start(ropes[:], rope.rearrange("(t p) i f -> p t i f", p=P)).then_inc(s_rope, 16)
            with pool.Fori(0, NG) as g:
                for u in range(HG * TLT):
                    pool.wait_ge(s_rs, g * 16 + (u + 1))
                    g_.tensor_tensor(prob[:, u % 2, :], prob[:, u % 2, :], asum[:, 2, u % 4:u % 4 + 1].to_broadcast([P, T]),
                                     ALU.mult).then_inc(s_pn, 1)
            stores(1)
            experts(1)
            for t in range(TLT):
                pool.dma_start(x_f[:, t, :], stream[t * P:(t + 1) * P, :]).then_inc(s_x[t], 16)
            pool.dma_start(nf[:], norm_final.rearrange("(a d) -> a d", a=1).to_broadcast([P, D])).then_inc(s_nf, 16)
            for t in range(TLT):
                pool.wait_ge(s_fin, t + 1)
                pool.dma_start(out_d[t * P:(t + 1) * P, :], xo_f[:, t, :]).then_inc(s_out, 16)
            pool.wait_ge(s_out, 16 * TLT)


INPUTS = ["x", "c", "ctx", "c_ctx", "ada_w", "ada_b", "norm_mix", "norm_ffn", "norm_final", "lru_w_in", "lru_conv_w",
          "lru_conv_b", "lru_gate_w", "lru_gate_b", "lru_lambda", "lru_w_out", "mla_w_in", "mla_q_norm", "mla_kv_norm",
          "mla_w_uq", "mla_w_ukv", "mla_w_o", "moe_router", "moe_w_up", "moe_w_down"]


def rope_table(tokens, freqs):
    freq = np.float32(ROPE_BASE) ** (-np.arange(freqs, dtype=np.float32) / np.float32(freqs))
    pos = np.stack([np.arange(tokens) // GRID_W, np.arange(tokens) % GRID_W], axis=-1).astype(np.float32)
    ang = (pos[:, :, None] * freq).reshape(tokens, 2 * freqs)
    return np.stack([np.cos(ang), np.sin(ang)], axis=1).astype(np.float32)


def kernel(**inputs):
    import concourse.bacc as bacc
    from concourse.bass_utils import run_bass_kernel_spmd

    nc = bacc.Bacc("TRN2", target_bir_lowering=False, num_devices=1)
    arrays = {name: np.ascontiguousarray(inputs[name]) for name in INPUTS}
    arrays["rope"] = rope_table(inputs["x"].shape[1], 8)
    args = [nc.dram_tensor(name, a.shape, mybir.dt.from_np(a.dtype), kind="ExternalInput").ap() for name, a in arrays.items()]
    out = nc.dram_tensor("out", inputs["x"].shape, F32, kind="ExternalOutput").ap()
    build(nc, *args, out)
    result = run_bass_kernel_spmd(nc, [arrays], core_ids=[0])
    return result.results[0]["out"]
```

```python
from contextlib import ExitStack

import numpy as np

import concourse.bass as bass
from concourse import mybir

ALU = mybir.AluOpType
ACT = mybir.ActivationFunctionType
F32 = mybir.dt.float32
F32R = mybir.dt.float32r
U32 = mybir.dt.uint32
AX_X = mybir.AxisListType.X

P = 128
RING = 8
BANK = 512
EPS = 1e-6
LRU_C = 8.0
GRID_W = 64
ROPE_BASE = 10000.0


class Chain:

    def __init__(self, eng, sem):
        self.eng, self.sem, self.n = eng, sem, 0

    def step(self, ins):
        self.n = self.n + 1
        ins.then_inc(self.sem, 1)
        self.eng.wait_ge(self.sem, self.n)


def build(nc, x, c, ctx, c_ctx, ada_w, ada_b, norm_mix, norm_ffn, norm_final, lru_w_in, lru_conv_w, lru_conv_b,
          lru_gate_w, lru_gate_b, lru_lambda, lru_w_out, mla_w_in, mla_q_norm, mla_kv_norm, mla_w_uq, mla_w_ukv,
          mla_w_o, moe_router, moe_w_up, moe_w_down, rope, out):
    TL, D = x.shape[1], x.shape[2]
    TC = ctx.shape[1]
    T = TL + TC
    KD = D // P
    TLT, TT = TL // P, T // P
    L, E = moe_router.shape[0], moe_router.shape[2]
    F = moe_w_down.shape[2]
    CAPL, CAPC = 2 * TL // E, 2 * TC // E
    CAP = [CAPL + CAPC, CAPL]
    FFT = [TT, TLT]
    QL, KVL = mla_q_norm.shape[1], mla_kv_norm.shape[1]
    ROPE = mla_w_in.shape[2] - QL - KVL
    H = 16
    NOPE = mla_w_uq.shape[2] // H - ROPE
    QK = NOPE + ROPE
    VD = mla_w_ukv.shape[2] // H - NOPE
    HG = 4
    NG = H // HG
    LAG = 3
    KQ, KKV = QL // P, KVL // P
    FQ = ROPE // 4
    SCALE = float(QK) ** -0.5
    CONV = lru_conv_w.shape[1]
    PADL, PADR = CONV // 2, CONV - 1 - CONV // 2
    CX = TL + PADL + PADR
    W = CX + TC
    WP = W + 1
    MODW = 2 * D
    MZ = QL + KVL + ROPE
    MLA_K = [(0, 3), (3, 6), (6, 8)]
    assert (D, TL, TC, T, F) == (1024, 512, 256, 768, 1024) and CAPL % 8 == 0 and CAPC % 8 == 0 and WP == 772

    mods = nc.dram_tensor("mods", [L, 2, 6 * D], F32).ap()
    stream = nc.dram_tensor("stream", [T, D], F32).ap()
    normed = nc.dram_tensor("normed", [T, D], F32).ap()

    chunks, slot_loads = [], [0] * RING
    place = {}

    def chunk(name, slot):
        place[name] = (slot, slot_loads[slot] + 1)
        chunks.append((name, slot, slot_loads[slot]))
        slot_loads[slot] += 1

    spare_slots = [2, 3, 4, 5, 6, 7]
    turn = 0
    for k in range(KD):
        chunk(("ada", 0, k), k)
    for m in range(KD):
        chunk(("lru_in", (m + KD // 2) % KD), m)
    chunk(("gate", 0), 0)
    chunk(("gate", 1), 1)
    side, group, k = [], 1, 0
    for q in range(2 * KD):
        todo = []
        if k == 0 and group == 2 or group == 3:
            todo.append(("turn", group - 1))
            group += group == 3
        for slot in range(2, (q - 3) // 2 + 1):
            if group > 2:
                break
            chunk(("ada", group, k), slot)
            todo.append(("ada", group, k))
            k += 1
            if k == KD:
                group, k = group + 1, 0
                break
        side.append(todo)
    assert group == 4
    for g in range(3, 6):
        for k in range(KD):
            chunk(("ada", g, k), spare_slots[turn % len(spare_slots)])
            turn += 1
    for j in range(4):
        chunk(("lru_out", j), spare_slots[turn % len(spare_slots)])
        turn += 1
    head_chunks = list(chunks)
    NCH = 12
    USED0, LANDED0 = [None, None], [None, None]
    NS, NW = 8, 4
    USED0[0] = slot_loads + [1] * (NCH - RING)
    LANDED0[0] = slot_loads + [0] * (NCH - RING)
    slot_loads = [n + E for n in slot_loads]
    chunks = []
    for j in range(3):
        chunk(("mla_in", j), j)
    for j in range(KQ):
        chunk(("uq", j), 3 + j)
    for j in range(KKV):
        chunk(("ukv", j), 6 + j)
    for j in range(3):
        chunk(("w_o", j), j)
    chunk(("w_o", 3), 3)
    mla_chunks = list(chunks)
    USED0[1] = slot_loads + [E + 2] * (NCH - RING)
    LANDED0[1] = slot_loads + [E] * (NCH - RING)

    with ExitStack() as es:
        def sb(name, shape, dt=F32, st=es):
            return st.enter_context(nc.sbuf_tensor("sb_" + name, shape, dt))

        def sem(name):
            return es.enter_context(nc.semaphore(name))

        wide = es.enter_context(nc.psum_tensor("wide", [P, 4, BANK], F32))
        duo = es.enter_context(nc.psum_tensor("duo", [P, 2, BANK], F32))
        turned = es.enter_context(nc.psum_tensor("turned", [P, 2, BANK], F32))

        ring = sb("ring", [P, RING, 2048])
        ident = sb("ident", [P, P])
        eps = sb("eps", [P, 1])
        rowsA = sb("rowsA", [P, P])
        rowsB = sb("rowsB", [P, P])
        pA = sb("pA", [P, 48])
        pB = sb("pB", [P, 96])
        modc = [sb("modc0", [P, 96]), sb("modc1", [P, 96])]
        cols = sb("cols", [P, 14, KD])
        router = sb("router", [P, L, KD, 2 * E])
        logit_parts = sb("logit_parts", [P, P])
        logits = sb("logits", [P, TT, E])
        silu_c = sb("silu_c", [P, KD, 2])
        stat = sb("stat", [P, 3, TT])
        lam = sb("lam", [P, 8, 16])
        idx_t = sb("idx_t", [P, E], U32)
        gate_t = sb("gate_t", [P, E])
        mx = sb("mx", [P, 4, TT])
        marks = sb("marks", [P, 32])
        aff = sb("aff", [P, TT, E])
        aff2 = sb("aff2", [P, TLT, 48])
        affT = sb("affT", [48, TL])
        top_v = sb("top_v", [48, CAPL])
        top_i = sb("top_i", [48, CAPL], U32)
        top_f = sb("top_f", [48, CAPL])
        turn_in = sb("turn_in", [E, 2, CAP[0]])

        def phase(*tensors):
            st = ExitStack()
            made = [sb(n, s, d, st) for n, s, d in tensors]
            return st, made

        st, (areaA, areaB, areaC, areaD, gmix, modbias, areaE) = phase(
            ("areaA", [P, 8, WP], F32), ("areaB", [P, 8, WP], F32), ("areaC", [P, 8, WP], F32),
            ("areaD", [P, 8, WP], F32), ("gmix", [P, 2, D], F32), ("modbias", [P, 2, BANK], F32),
            ("areaE", [P, 4, WP], F32))
        st.close()
        st, (_, areaB_hi, areaC_lo, _, _, _, w_hi0, w_lo0) = phase(
            ("keepA", [P, 8, WP], F32), ("areaB_hi", [P, 8, WP], F32R), ("areaC_lo", [P, 8, WP], F32R),
            ("keepD", [P, 8, WP], F32), ("keepg", [P, 2, D], F32), ("keepb", [P, 2, BANK], F32),
            ("w_hi0", [P, 2, KD, P], F32R), ("w_lo0", [P, 2, KD, P], F32R))
        st.close()

        def flat(a, n, w):
            return a[:].rearrange("p a b -> p (a b)")[:, 0:n * w].rearrange("p (n w) -> p n w", n=n)

        st, (x_b, gmix1) = phase(("x_b", [P, TT, D], F32), ("gmix1", [P, D], F32))
        mla_keep = ExitStack()
        cqT, ckvT, krr, ropes, rtmp = [sb(n, s, F32, mla_keep) for n, s in (
            ("cqT", [P, KQ, TL]), ("ckvT", [P, KKV, T]), ("krr", [P, TT, ROPE]), ("ropes", [P, TLT, 2, 2 * FQ]),
            ("rtmp", [P, 4, HG * 2 * FQ]))]
        sub, (xn2, hT2, cqn, kraw) = phase(("xn2", [P, TT, D], F32), ("hT2", [P, KD, T], F32),
                                           ("cqn", [P, 2, QL + KVL], F32), ("kraw", [P, 2, ROPE], F32))
        sub.close()
        sub, (OT, q_hi, q_lo, k_hi, k_lo, V, qtok, ktok, prob, PT, asum) = phase(
            ("OT", [P, KD, TL], F32), ("q_hi", [QK, HG, TL], F32R), ("q_lo", [QK, HG, TL], F32R),
            ("k_hi", [QK, HG, T], F32R), ("k_lo", [QK, HG, T], F32R),
            ("V", [P, TT, HG, VD], F32), ("qtok", [P, 2, HG, QK], F32), ("ktok", [P, 2, HG, QK], F32),
            ("prob", [P, LAG, T], F32), ("PT", [P, 2, 2, TT, P], F32), ("asum", [P, 3, 8], F32))
        sub.close()
        sub, (_, xn3, hT3) = phase(("OTkeep", [P, KD, TL], F32), ("xn3", [P, TLT, D], F32), ("hT3", [P, KD, TL], F32))
        sub.close()
        mla_keep.close()
        st.close()

        st, (xg, h32, xs, sg, lo_rows, hid, hidT, ye, mod_a, mod_b, gffn, idx_c, gate_c, w_hi, w_lo, ring_x) = phase(
            ("xg", [P, D], F32), ("h32", [P, KD, CAP[0]], F32), ("xs", [P, KD, 2 * CAP[0]], F32R),
            ("sg", [P, BANK], F32), ("lo_rows", [CAPL, BANK], F32), ("hid", [P, BANK], F32),
            ("hidT", [P, 2, 4, CAP[0]], F32), ("ye", [P, D], F32), ("mod_a", [P, KD, CAP[0]], F32),
            ("mod_b", [P, KD, CAP[0]], F32), ("gffn", [P, D], F32), ("idx_c", [P, 2], U32), ("gate_c", [P, 2], F32),
            ("w_hi", [P, NW, 2048], F32R), ("w_lo", [P, NW, 2048], F32R), ("ring_x", [P, NCH - RING, 2048], F32))
        st.close()
        st, (x_f, xo_f, nf) = phase(("x_f", [P, TLT, D], F32), ("xo_f", [P, TLT, D], F32), ("nf", [P, D], F32))
        st.close()

        landed = [sem(f"landed{s}") for s in range(NCH)]
        used = [sem(f"used{s}") for s in range(NCH)]
        s_const, s_parA, s_parB, s_rope, s_router = [sem(n) for n in ("s_const", "s_parA", "s_parB", "s_rope", "s_router")]
        s_partr, s_pcol, s_silu_c, s_lam, s_lamE = [sem(n) for n in ("s_partr", "s_pcol", "s_silu_c", "s_lam", "s_lamE")]
        s_modev, s_modst, s_bias, s_modtr, s_modcol = [sem(n) for n in (
            "s_modev", "s_modst", "s_bias", "s_modtr", "s_modcol")]
        s_x0 = [sem(f"s_x0{t}") for t in range(TT)]
        s_x = [sem(f"s_x{t}") for t in range(TT)]
        s_rms, s_xn, s_xtr, s_hTa, s_hTd = [sem(n) for n in ("s_rms", "s_xn", "s_xtr", "s_hTa", "s_hTd")]
        N0 = [0, TT, 2 * TT, 3 * TT, 3 * TT + TLT]
        s_hhi, s_hlo, s_whi, s_wlo = [sem(n) for n in ("s_hhi", "s_hlo", "s_whi", "s_wlo")]
        s_z, s_gelu, s_ucopy, s_xc = [sem(n) for n in ("s_z", "s_gelu", "s_ucopy", "s_xc")]
        s_gmm, s_sig, s_ix, s_tanh, s_v, s_sqrt, s_scan, s_ysum, s_yg = [sem(n) for n in (
            "s_gmm", "s_sig", "s_ix", "s_tanh", "s_v", "s_sqrt", "s_scan", "s_ysum", "s_yg")]
        s_gmix = [sem("s_gmix0"), sem("s_gmix1")]
        s_o = [sem("s_o0"), sem("s_o1")]
        s_x1 = [sem("s_x1_0"), sem("s_x1_1")]
        s_st = [sem("s_st0"), sem("s_st1")]
        s_nst = [sem("s_nst0"), sem("s_nst1")]
        s_log, s_logc, s_logt, s_logr = [sem(n) for n in ("s_log", "s_logc", "s_logt", "s_logr")]
        LG0 = [0, TT]
        s_sub, s_aexp, s_aff, s_afft, s_top, s_topt, s_sel = [sem(n) for n in (
            "s_sub", "s_aexp", "s_aff", "s_afft", "s_top", "s_topt", "s_sel")]
        s_idxc = [sem("s_idxc0"), sem("s_idxc1")]
        s_gath = [sem("s_gath0"), sem("s_gath1")]
        s_xgtr = [sem("s_xgtr0"), sem("s_xgtr1")]
        s_xgT = [sem("s_xgT0"), sem("s_xgT1")]
        s_hi = [sem("s_hi0"), sem("s_hi1")]
        s_wdone = [sem("s_wdone0"), sem("s_wdone1")]
        s_lot, s_gs, s_us, s_yhi = [sem(n) for n in ("s_lot", "s_gs", "s_us", "s_yhi")]
        s_silu = [sem("s_silu0"), sem("s_silu1")]
        s_hid = [sem("s_hid0"), sem("s_hid1")]
        s_hidtr = [sem("s_hidtr0"), sem("s_hidtr1")]
        s_hidT = [sem("s_hidT0"), sem("s_hidT1")]
        s_ye = [sem("s_ye0"), sem("s_ye1")]
        s_scat = [sem("s_scat0"), sem("s_scat1")]
        s_mz, s_mzs, s_cqn, s_cqtr, s_cqT, s_qhi, s_khi = [sem(n) for n in (
            "s_mz", "s_mzs", "s_cqn", "s_cqtr", "s_cqT", "s_qhi", "s_khi")]
        s_q, s_qtok, s_qtr, s_qT, s_kv, s_ktok, s_ktr, s_kT = [sem(n) for n in (
            "s_q", "s_qtok", "s_qtr", "s_qT", "s_kv", "s_ktok", "s_ktr", "s_kT")]
        s_S, s_max, s_exp, s_pn, s_ptr, s_PTd, s_PTa, s_av, s_OT, s_rs = [sem(n) for n in (
            "s_S", "s_max", "s_exp", "s_pn", "s_ptr", "s_PTd", "s_PTa", "s_av", "s_OT", "s_rs")]
        s_fin, s_out, s_nf = sem("s_fin"), sem("s_out"), sem("s_nf")
        s_dve, s_act = sem("s_dve"), sem("s_act")
        s_dloop = [sem("s_dloop0"), sem("s_dloop1"), sem("s_dloop2")]
        NCONST = 11

        def ring_at(name):
            return ring[:, place[name][0], :]

        def chunk_at(j):
            return ring[:, j, :] if j < RING else ring_x[:, j - RING, :]

        def col(layer, v, what, k):
            return v * 48 + what * 8 + k

        B_CONV, B_CB, B_GB, B_LAM = 0, CONV * KD, CONV * KD + KD, CONV * KD + KD + 4 * KD
        B_QN = B_LAM + 2 * KD
        B_KVN = B_QN + KQ
        NB = B_KVN + KKV
        N_COL = [[0, 1], [2, 3], [4, 5], [6, None]]

        x_d = x.rearrange("b t d -> (b t) d")
        ctx_d = ctx.rearrange("b t d -> (b t) d")
        out_d = out.rearrange("b t d -> (b t) d")
        stages = [
            dict(x=flat(areaD, TT, D), xn=flat(areaA, TT, D), hT=flat(areaC, KD, T), n=TT, lay=0, sc=1, sh=0),
            dict(x=flat(areaD, TT, D), xn=flat(areaC, TT, D), hT=flat(areaA, KD, T), n=TT, lay=0, sc=4, sh=3),
            dict(x=x_b[:], xn=xn2[:], hT=hT2[:], n=TT, lay=1, sc=1, sh=0),
            dict(x=x_b[:], xn=xn3[:], hT=hT3[:], n=TLT, lay=1, sc=4, sh=3),
        ]
        hT_hi, hT_lo = flat(areaB_hi, KD, T), flat(areaC_lo, KD, T)
        XC, G, Y = areaD, areaA, areaB
        RT, IT, A = areaC[:, 0:4, :], areaC[:, 4:8, :], areaE[:]
        rounds = [(0, 0), (1, 0), (0, 1), (1, 1)]

        def mod_banks(i):
            return duo if i <= 2 else wide

        def unit(u):
            (pair, t), hh = divmod(u // 2, TLT), u % 2
            return 2 * pair + hh, t, pair, hh

        def in_name(q):
            return ("lru_in", (q // 2 + KD // 2) % KD)

        def in_weights(q):
            return ring_at(in_name(q)).rearrange("p (k n) -> p k n", k=KD)[:, :, (q % 2) * P:(q % 2 + 1) * P]

        def seg(a, i):
            return a[:, 0:TL] if i == 0 else a[:, CX:CX + TC]

        block = es.enter_context(nc.Block())

        @block.sync
        def _(sp):
            for dst, src in (
                (rowsA[0:8], c.rearrange("b (k q) -> (b k) q", q=P)), (rowsA[8:16], c_ctx.rearrange("(k q) -> k q", q=P)),
                (rowsA[16:32], norm_mix.rearrange("l (k q) -> (l k) q", q=P)),
                (rowsA[32:48], norm_ffn.rearrange("l (k q) -> (l k) q", q=P)),
            ):
                sp.dma_start(dst, src).then_inc(s_parA, 16)
            for t in range(TT):
                src = x_d[t * P:(t + 1) * P, :] if t < TLT else ctx_d[(t - TLT) * P:(t - TLT + 1) * P, :]
                sp.dma_start(stages[0]["x"][:, t, :], src).then_inc(s_x0[t], 16)

            def load(name, slot, before):
                if before >= 1:
                    sp.wait_ge(used[slot], before)
                dst = ring[:, slot, :]
                if name[0] == "ada":
                    lay, g = divmod(name[1], 3)
                    src = ada_w[lay, name[2] * P:(name[2] + 1) * P, g * MODW:(g + 1) * MODW]
                elif name[0] == "lru_in":
                    dst = dst.rearrange("p (k n) -> p k n", k=KD)
                    src = lru_w_in[0].rearrange("(k p) n -> p k n", p=P)[:, :, name[1] * 256:(name[1] + 1) * 256]
                elif name[0] == "gate":
                    dst = dst.rearrange("p (n j) -> p n j", j=P)
                    src = lru_gate_w[0, name[1]].rearrange("g n k j -> k (g n) j")
                elif name[0] in ("lru_out", "w_o"):
                    dst = dst.rearrange("p (k n) -> p k n", k=2)
                    src = (lru_w_out if name[0] == "lru_out" else mla_w_o)[0]
                    src = src.rearrange("(k p) n -> p k n", p=P)[:, 2 * name[1]:2 * name[1] + 2, :]
                elif name[0] == "mla_in":
                    k0, k1 = MLA_K[name[1]]
                    dst = dst[:, 0:(k1 - k0) * MZ].rearrange("p (k n) -> p k n", n=MZ)
                    src = mla_w_in[0].rearrange("(k p) n -> p k n", p=P)[:, k0:k1, :]
                elif name[0] == "uq":
                    dst, src = dst[:, 0:H * QK], mla_w_uq[0, name[1] * P:(name[1] + 1) * P, :]
                elif name[0] == "ukv":
                    src = mla_w_ukv[0, name[1] * P:(name[1] + 1) * P, :]
                sp.dma_start(dst, src).then_inc(landed[slot], 16)

            def experts(lay):
                up = moe_w_up[lay].rearrange("e (k p) (s h n) -> e p k s h n", p=P, s=2, h=2)
                down = moe_w_down[lay].rearrange("e (k p) n -> e p k n", p=P)
                with sp.Fori(0, E) as e:
                    for j in range(NCH):
                        sp.wait_ge(used[j], e + USED0[lay][j])
                        if j < NS:
                            h, s, q = j // 4, j % 4 // 2, j % 2
                            dst = chunk_at(j).rearrange("p (k n) -> p k n", k=4)
                            sp.dma_start(dst, up[e, :, 4 * q:4 * q + 4, s, h, :]).then_inc(landed[j], 16)
                        else:
                            dst = chunk_at(j).rearrange("p (k n) -> p k n", k=2)
                            sp.dma_start(dst, down[e, :, (j - NS) * 2:(j - NS) * 2 + 2, :]).then_inc(landed[j], 16)

            def load_bias(i):
                lay, g = divmod(i, 3)
                if i == 0:
                    sp.wait_ge(s_const, NCONST)
                if i >= 2:
                    sp.wait_ge(s_modst, 32 * (i - 1))
                    sp.wait_ge(s_modtr, i - 1)
                for v_ in range(2):
                    sp.dma_start(modbias[v_:P:32, i % 2, :],
                                 ada_b[lay, g * MODW:(g + 1) * MODW].rearrange("(n f) -> n f", f=BANK)).then_inc(s_bias, 16)

            for n, (name, slot, before) in enumerate(head_chunks):
                if name[0] == "ada" and name[2] == KD - 1:
                    load_bias(name[1])
                load(name, slot, before)
                if n == 7:
                    for dst, src in (
                        (rowsB[B_CONV:B_CB], lru_conv_w.rearrange("a w (k q) -> (a w k) q", q=P)),
                        (rowsB[B_CB:B_GB], lru_conv_b.rearrange("a (k q) -> (a k) q", q=P)),
                        (rowsB[B_GB:B_LAM], lru_gate_b.rearrange("a d g (k q) -> (a d g k) q", q=P)),
                        (rowsB[B_LAM:B_QN], lru_lambda.rearrange("a d (k q) -> (a d k) q", q=P)),
                        (rowsB[B_QN:B_KVN], mla_q_norm.rearrange("a (k q) -> (a k) q", q=P)),
                        (rowsB[B_KVN:NB], mla_kv_norm.rearrange("a (k q) -> (a k) q", q=P)),
                    ):
                        sp.dma_start(dst, src).then_inc(s_parB, 16)
                    for lay in range(L):
                        sp.dma_start(router[:, lay, :, 0:E], moe_router[lay].rearrange("(k p) e -> p k e", p=P)).then_inc(s_router, 16)
            experts(0)
            for name, slot, before in mla_chunks:
                load(name, slot, before)
            experts(1)

        @block.tensor
        def _(pe):
            mm = nc.tensor.matmul

            def arrived(name):
                slot, n = place[name]
                pe.wait_ge(landed[slot], 16 * n)

            def turn(dst, src, plain=False):
                n = src.shape[0]
                if plain:
                    return mm(dst, src, ident[0:n, 0:n], start=True, stop=True)
                return nc.tensor.transpose(dst, src, ident[0:n, 0:n])

            def ada_chunk(i, k, owed=None):
                if i >= 1 and k == 0:
                    pe.wait_ge(s_modev, i)
                arrived(("ada", i, k))
                w = ring_at(("ada", i, k))
                for n in range(4):
                    ins = mm(mod_banks(i)[32 * n:32 * n + 2, 0, :], silu_c[:, k, :], w[:, n * BANK:(n + 1) * BANK],
                             start=k == 0, stop=k == KD - 1)
                    if owed and n == 0:
                        ins.then_inc(owed, 1)
                ins.then_inc(used[place[("ada", i, k)][0]], 1)

            def ada(i, owed=None):
                for k in range(KD):
                    ada_chunk(i, k, owed if k == 0 else None)

            def turn_mods(i, owed=None):
                pe.wait_ge(s_modev, i + 1)
                if i >= 1:
                    pe.wait_ge(s_modcol, i)
                for j in range(4):
                    ins = turn(mod_banks(i)[:, 1, j * P:(j + 1) * P], modbias[:, i % 2, j * P:(j + 1) * P])
                    if owed and j == 0:
                        ins.then_inc(owed, 1)
                ins.then_inc(s_modtr, 1)

            def turn_tile(s, t, owed=None):
                pe.wait_ge(s_xn, N0[s] + t + 1)
                for half, s_ev in ((0, s_hTa), (1, s_hTd)):
                    if t >= 1:
                        pe.wait_ge(s_ev, N0[s] + t)
                    for k in range(4):
                        f = (4 * half + k) * P
                        ins = turn(turned[:, half, k * P:(k + 1) * P], stages[s]["xn"][:, t, f:f + P])
                        if owed:
                            ins.then_inc(owed, 1)
                            owed = None
                    ins.then_inc(s_xtr, 1)

            pe.wait_ge(s_const, NCONST)
            pe.wait_ge(s_parA, 64)
            turn(turned[:, 0, 0:48], rowsA[0:48, :]).then_inc(s_partr, 1)
            pe.wait_ge(s_silu_c, 1)
            ada(0)
            turn_mods(0)
            pe.wait_ge(s_parB, 96)
            turn(wide[:, 3, 0:NB], rowsB[0:NB, :]).then_inc(s_partr, 1)
            pe.wait_ge(s_pcol, 1)
            for t in range(TT):
                turn_tile(0, t)

            pe.wait_ge(s_hlo, TLT)
            owed = None
            for q in range(2 * KD):
                name = in_name(q)
                pe.wait_ge(s_wlo, q + 1)
                if q == 1:
                    pe.wait_ge(s_pcol, 2)
                if q >= 2:
                    if q - 2 < KD:
                        pe.wait_ge(s_ucopy, q - 1)
                    else:
                        pe.wait_ge(s_gelu, q - 1 - KD)
                b = 2 * (q % 2)
                for part in ((0,), (1,)) if q == 0 else ((0, 1),):
                    if q == 0 and part == (1,):
                        pe.wait_ge(s_hlo, TT)
                    for k in range(KD):
                        for n, (w, h) in enumerate(((w_hi0, hT_hi), (w_hi0, hT_lo), (w_lo0, hT_hi))):
                            for i in part:
                                o, cols_ = (wide[:, b, :], slice(0, TL)) if i == 0 else (wide[:, b + 1, 0:TC], slice(TL, T))
                                ins = mm(o, w[:, q % 2, k, :], h[:, k, cols_],
                                         start=k == 0 and n == 0, stop=k == KD - 1 and n == 2)
                                if owed:
                                    ins.then_inc(owed, 1)
                                    owed = None
                ins.then_inc(s_z, 1)
                if q % 2:
                    owed = used[place[name][0]]
                for what, *at in side[q]:
                    (ada_chunk if what == "ada" else turn_mods)(*at, owed=owed)
                    owed = None

            def gates(r, owed=None):
                d, half = rounds[r]
                arrived(("gate", d))
                w = ring_at(("gate", d)).rearrange("p (n j) -> p n j", j=P)
                for jj in range(4):
                    n, u = 4 * half + jj, 4 * r + jj
                    pe.wait_ge(s_xc, n + 1)
                    for g, banks in ((0, turned), (1, duo)):
                        if u >= 1:
                            pe.wait_ge(s_sig, 2 * (u - 1) + g + 1)
                        ins = mm(banks[:, 0, :], w[:, g * KD + n, :], seg(XC[:, n, :], 0), start=True, stop=True)
                        if owed:
                            ins.then_inc(owed, 1)
                            owed = None
                        mm(banks[:, 1, 0:TC], w[:, g * KD + n, :], seg(XC[:, n, :], 1), start=True, stop=True).then_inc(s_gmm, 1)

            pe.wait_ge(s_modev, 3)
            pe.wait_ge(s_modcol, 3)
            gates(0, owed)
            pe.wait_ge(s_gelu, KD)
            ada(3)
            gates(1)
            turn_mods(3)
            ada(4)
            gates(2)
            turn_mods(4, used[place[("gate", 0)][0]])
            ada(5)
            gates(3)
            turn_mods(5, used[place[("gate", 1)][0]])

            def out_project(lay, s, lhs, names):
                n_t = FFT[lay]
                pe.wait_ge(s_router, 16 * L)
                for step in range(n_t + 3):
                    if step < n_t:
                        t = step
                        if t >= 2:
                            pe.wait_ge(s_x1[lay], t - 1)
                        b = 2 * (t % 2)
                        for k in range(KD):
                            if t == 0 and k % 2 == 0:
                                arrived(names[k // 2])
                            w = ring_at(names[k // 2]).rearrange("p (k n) -> p k n", k=2)[:, k % 2, :]
                            for n in range(2):
                                ins = mm(wide[:, b + n, :], lhs(k, t), w[:, n * BANK:(n + 1) * BANK],
                                         start=k == 0, stop=k == KD - 1)
                            if t == n_t - 1 and k % 2 and k < KD - 1:
                                ins.then_inc(used[place[names[k // 2]][0]], 1)
                        ins.then_inc(s_o[lay], 1)
                    if 1 <= step <= n_t:
                        turn_tile(s, step - 1, used[place[names[3]][0]] if step == n_t else None)
                    if 2 <= step <= n_t + 1:
                        t = step - 2
                        pe.wait_ge(s_hTa, N0[s] + t + 1)
                        pe.wait_ge(s_hTd, N0[s] + t + 1)
                        if LG0[lay] + t:
                            pe.wait_ge(s_logc, LG0[lay] + t)
                        for k in range(KD):
                            j = k % 4
                            ins = mm(duo[32 * j:32 * j + 2 * E, 0, 0:P], router[:, lay, k, :],
                                     stages[s]["hT"][:, k, t * P:(t + 1) * P], start=k < 4, stop=k >= 4)
                        ins.then_inc(s_log, 1)
                    if step >= 3:
                        t = step - 3
                        pe.wait_ge(s_logc, LG0[lay] + t + 1)
                        if LG0[lay] + t:
                            pe.wait_ge(s_logr, LG0[lay] + t)
                        turn(duo[:, 1, 0:P], logit_parts[:]).then_inc(s_logt, 1)

            def turn_choice(lay):
                pe.wait_ge(s_aff, lay + 1)
                for t in range(TLT):
                    ins = turn(turned[0:48, 0, t * P:(t + 1) * P], aff2[:, t, :])
                ins.then_inc(s_afft, 1)
                pe.wait_ge(s_top, lay + 1)
                for i in range(2):
                    ins = turn(duo[0:CAP[lay], 1, i * E:(i + 1) * E], turn_in[:, i, 0:CAP[lay]])
                ins.then_inc(s_topt, 1)

            def experts(lay):
                M = CAP[lay]

                def turn_rows(e, part):
                    if part == 0:
                        pe.wait_ge(s_gath[lay], e * 16 + 16)
                    pe.wait_ge(s_hidT[lay], e * 2 + (1 + part))
                    for k in range(4):
                        ins = turn(turned[:, part, k * M:(k + 1) * M], xg[0:M, (4 * part + k) * P:(4 * part + k + 1) * P],
                                   plain=k == 0 and M <= 64)
                    ins.then_inc(s_xgtr[lay], 1)

                def half(e, h):
                    for s in range(2):
                        if s == 0:
                            pe.wait_ge(s_hid[lay], e * 2 + (h + 1))
                        for q in range(2):
                            j = 4 * h + 2 * s + q
                            pe.wait_ge(used[j], e + (USED0[lay][j] + 1))
                            wh, wl = [w[:, j % NW, :].rearrange("p (k n) -> p k n", k=4) for w in (w_hi, w_lo)]
                            if h == 0 and s == 0:
                                pe.wait_ge(s_xgT[lay], e * 2 + (q + 1))
                            for k in range(4):
                                kk = 4 * q + k
                                first, last_ = kk == 0, kk == KD - 1
                                if lay == 0:
                                    x_hi, x_lo = xs[:, kk, 0:M], xs[:, kk, M:2 * M]
                                    o = wide[0:M, 2 * h + s, :]
                                    mm(o, x_hi, wh[:, k, :], start=first, stop=False)
                                    mm(o, x_hi, wl[:, k, :], start=False, stop=False)
                                    ins = mm(o, x_lo, wh[:, k, :], start=False, stop=last_)
                                else:
                                    both = xs[:, kk, 0:2 * M]
                                    o = wide[0:2 * M, 2 * h + s, :]
                                    mm(o, both, wh[:, k, :], start=first, stop=False)
                                    ins = mm(o, both, wl[:, k, :], start=False, stop=last_)
                            ins.then_inc(s_wdone[lay], 1)
                        if h == 1 and s == 0:
                            turn_hid(e, 0)

                def turn_hid(e, h):
                    pe.wait_ge(s_hid[lay], e * 2 + (h + 3))
                    pe.wait_ge(s_xgT[lay], e * 2 + (h + 1))
                    for k in range(4):
                        ins = turn(turned[:, h, k * M:(k + 1) * M], hid[0:M, k * P:(k + 1) * P], plain=k == 0 and M <= 64)
                    ins.then_inc(s_hidtr[lay], 1)

                def down(e, h):
                    pe.wait_ge(s_hidT[lay], e * 2 + (h + 3))
                    for j in (NS + 2 * h, NS + 1 + 2 * h):
                        pe.wait_ge(landed[j], e * 16 + 16 * (LANDED0[lay][j] + 1))
                        w = chunk_at(j).rearrange("p (k n) -> p k n", k=2)
                        for k in range(2):
                            kk = (j - NS) * 2 + k
                            for n in range(2):
                                o = duo[0:M, n, :] if lay == 0 else duo[n * M:(n + 1) * M, n, :]
                                ins = mm(o, hidT[:, h, kk % 4, 0:M], w[:, k, n * BANK:(n + 1) * BANK],
                                         start=kk == 0, stop=kk == KD - 1)
                        ins.then_inc(used[j], 1)

                def body(e, last):
                    half(e, 0)
                    half(e, 1)
                    pe.wait_ge(s_ye[lay], e + 1)
                    down(e, 0)
                    turn_hid(e, 1)
                    if not last:
                        turn_rows(e + 1, 0)
                    down(e, 1)
                    if not last:
                        turn_rows(e + 1, 1)

                turn_rows(0, 0)
                turn_rows(0, 1)
                with pe.Fori(0, E - 1) as e:
                    body(e, False)
                body(E - 1, True)

            pe.wait_ge(s_yg, KD)
            pe.wait_ge(s_modev, 6)
            pe.wait_ge(s_modcol, 6)

            def lru_lhs(k, t):
                at = t * P if t < TLT else CX + (t - TLT) * P
                return Y[:, k, at:at + P]

            out_project(0, 1, lru_lhs, [("lru_out", j) for j in range(4)])
            turn_choice(0)
            experts(0)

            turn_tile(2, 0)
            turn_tile(2, 1)
            hT = stages[2]["hT"]
            for j in range(3):
                arrived(("mla_in", j))

            def mla_w(k):
                j = [n for n, (a, b) in enumerate(MLA_K) if a <= k < b][0]
                return ring_at(("mla_in", j))[:, (k - MLA_K[j][0]) * MZ:(k - MLA_K[j][0] + 1) * MZ]

            for step in range(TT + 1):
                if step < TT:
                    t = step
                    if t >= 2:
                        pe.wait_ge(s_cqn, t - 1)
                    else:
                        pe.wait_ge(s_hid[0], 2 * E + 2)
                    pe.wait_ge(s_hTa, N0[2] + t + 1)
                    pe.wait_ge(s_hTd, N0[2] + t + 1)
                    b = 2 * (t % 2)
                    for k in range(KD):
                        lhs = hT[:, k, t * P:(t + 1) * P]
                        if t < TLT:
                            mm(wide[:, b, 0:QL], lhs, mla_w(k)[:, 0:QL], start=k == 0, stop=k == KD - 1)
                        ins = mm(wide[:, b + 1, 0:MZ - QL], lhs, mla_w(k)[:, QL:MZ], start=k == 0, stop=k == KD - 1)
                        if t == TT - 1 and k in (2, 5):
                            ins.then_inc(used[place[("mla_in", k // 3)][0]], 1)
                    ins.then_inc(s_mz, 1)
                    for t in {0: (2,), 1: range(3, TT)}.get(step, ()):
                        turn_tile(2, t)
                if step >= 1:
                    t = step - 1
                    pe.wait_ge(s_cqn, t + 1)
                    if t >= 1:
                        pe.wait_ge(s_cqT, t)
                    for k in range(KQ if t < TLT else 0):
                        turn(duo[:, 0, k * P:(k + 1) * P], cqn[:, t % 2, k * P:(k + 1) * P])
                    for k in range(KKV):
                        ins = turn(duo[:, 1, k * P:(k + 1) * P], cqn[:, t % 2, QL + k * P:QL + (k + 1) * P])
                        if step == TT and k == 0:
                            ins.then_inc(used[place[("mla_in", 2)][0]], 1)
                    ins.then_inc(s_cqtr, 1)
            for j in range(KQ):
                arrived(("uq", j))
            for j in range(KKV):
                arrived(("ukv", j))
            pe.wait_ge(s_cqT, TT)
            with pe.Fori(0, NG) as g:
                def kv_project(t):
                    if t < 2:
                        pe.wait_ge(s_OT, g * 2 + (t + 1))
                    pe.wait_ge(s_ktok, g * 6 + (t + 1))
                    for k in range(KKV):
                        ins = mm(duo[:, t % 2, :], ckvT[:, k, t * P:(t + 1) * P],
                                 ring_at(("ukv", k))[:, bass.ds(g * BANK, BANK)], start=k == 0, stop=k == KKV - 1)
                    ins.then_inc(s_kv, 1)

                def turn_keys(t):
                    pe.wait_ge(s_ktok, g * 6 + (t + 3))
                    pe.wait_ge(s_kT, g * 6 + (t + 1))
                    for h in range(HG):
                        ins = turn(turned[0:QK, 1, h * P:(h + 1) * P], ktok[:, t % 2, h, :])
                    ins.then_inc(s_ktr, 1)

                def q_project(t):
                    if t < 2:
                        pe.wait_ge(s_ktok, g * 6 + (t + 7))
                    pe.wait_ge(s_qtok, g * 4 + (t + 1))
                    for k in range(KQ):
                        ins = mm(duo[:, t % 2, 0:HG * QK], cqT[:, k, t * P:(t + 1) * P],
                                 ring_at(("uq", k))[:, bass.ds(g * (HG * QK), HG * QK)], start=k == 0, stop=k == KQ - 1)
                    ins.then_inc(s_q, 1)

                def turn_queries(t):
                    pe.wait_ge(s_qtok, g * 4 + (t + 3))
                    pe.wait_ge(s_qT, g * 4 + (t + 1))
                    for h in range(HG):
                        ins = turn(turned[0:QK, 0, h * P:(h + 1) * P], qtok[:, t % 2, h, :])
                    ins.then_inc(s_qtr, 1)

                kv_project(0)
                for t in range(1, TT):
                    kv_project(t)
                    turn_keys(t - 1)
                q_project(0)
                turn_keys(TT - 1)
                for t in range(1, TLT):
                    q_project(t)
                    turn_queries(t - 1)
                turn_queries(TLT - 1)
                pe.wait_ge(s_kT, g * 6 + 7)

                def scores(u):
                    h, t, _, _ = unit(u)
                    if h == 0:
                        pe.wait_ge(s_qT, g * 4 + (t + 2))
                    pe.wait_ge(s_exp, g * 16 + (u + 1))
                    b = 2 * (u % 2)
                    for n, (q, k_) in enumerate(((q_hi, k_hi), (q_hi, k_lo), (q_lo, k_hi))):
                        q, edge = q[:, h, t * P:(t + 1) * P], dict(start=n == 0, stop=n == 2)
                        mm(wide[:, b, :], q, k_[:, h, 0:TL], **edge)
                        ins = mm(wide[:, b + 1, 0:TC], q, k_[:, h, TL:T], **edge)
                    ins.then_inc(s_S, 1)

                def turn_probs(u):
                    pe.wait_ge(s_pn, g * 16 + (u + 1))
                    pe.wait_ge(s_PTa, g * 16 + (u + 1))
                    for k in range(4):
                        ins = turn(turned[:, 0, k * P:(k + 1) * P], prob[:, u % LAG, k * P:(k + 1) * P])
                    ins.then_inc(s_ptr, 1)
                    pe.wait_ge(s_PTd, g * 16 + (u + 1))
                    for k in range(4, TT):
                        ins = turn(turned[:, 1, (k - 4) * P:(k - 3) * P], prob[:, u % LAG, k * P:(k + 1) * P])
                    ins.then_inc(s_ptr, 1)

                def values(w):
                    pe.wait_ge(s_PTa, g * 16 + (2 * w + 3))
                    pe.wait_ge(s_PTd, g * 16 + (2 * w + 3))
                    _, t, pair, _ = unit(2 * w)
                    for k in range(TT):
                        for hh in range(2):
                            ins = mm(duo[hh * VD:(hh + 1) * VD, pair, t * P:(t + 1) * P], V[:, k, 2 * pair + hh, :],
                                     PT[:, w % 2, hh, k, :], start=k == 0, stop=k == TT - 1)
                    ins.then_inc(s_av, 1)

                U = HG * TLT
                for u in range(U + LAG):
                    if u < U:
                        scores(u)
                    if u >= LAG:
                        turn_probs(u - LAG)
                        if (u - LAG) % 2 and u - LAG >= 3:
                            values((u - LAG) // 2 - 1)
                values(U // 2 - 1)
            pe.wait_ge(s_OT, 2 * NG + 2)
            for n, name in enumerate([("uq", j) for j in range(KQ)] + [("ukv", j) for j in range(KKV)]):
                turn(duo[0:32, 1, 32 * n:32 * n + 32], ident[0:32, 0:32]).then_inc(used[place[name][0]], 1)
            out_project(1, 3, lambda k, t: OT[:, k, t * P:(t + 1) * P], [("w_o", j) for j in range(4)])
            turn_choice(1)
            experts(1)

        @block.scalar
        def _(act):
            fn = nc.scalar.activation
            chain = Chain(act, s_act)

            def x_ready(eng, s, t):
                if s == 0:
                    eng.wait_ge(s_x0[t], 16)
                elif s == 2:
                    eng.wait_ge(s_x[t], 32)
                else:
                    eng.wait_ge(s_x1[s // 2], t + 1)

            def squares(s, t):
                x_ready(act, s, t)
                chain.step(fn(stages[s]["xn"][:, t, :], stages[s]["x"][:, t, :], ACT.Square, accum_out=stat[:, 0, t:t + 1]))
                fn(stat[:, 1, t:t + 1], stat[:, 0, t:t + 1], ACT.Sqrt, bias=eps[:, 0:1], scale=1.0 / D).then_inc(s_rms, 1)

            def modulate(s, t):
                a = 2 * s + (0 if t < TLT else 1)
                if t == 0:
                    act.wait_ge(s_modcol, (1, 3, 4, 6)[s])
                act.wait_ge(s_xtr, 2 * (N0[s] + t) + 1)
                for k in range(4):
                    ins = fn(stages[s]["hT"][:, k, t * P:(t + 1) * P], turned[:, 0, k * P:(k + 1) * P], ACT.Identity,
                             bias=cols[:, 7 + a, k:k + 1], scale=cols[:, a, k:k + 1])
                ins.then_inc(s_hTa, 1)

            def norm(s):
                n = stages[s]["n"]
                for step in range(n + 1):
                    if step < n:
                        squares(s, step)
                    if step >= 1:
                        modulate(s, step - 1)

            act.wait_ge(s_const, NCONST)
            act.wait_ge(s_pcol, 1)
            fn(silu_c[:].rearrange("p k v -> p v k"), pA[:, 0:16].rearrange("p (v k) -> p v k", v=2), ACT.Silu).then_inc(s_silu_c, 1)
            for t in range(TT):
                squares(0, t)

            def in_hi(q):
                slot, n = place[in_name(q)]
                act.wait_ge(landed[slot], 16 * n)
                if q >= 2:
                    act.wait_ge(s_z, q - 1)
                fn(w_hi0[:, q % 2], in_weights(q), ACT.Copy).then_inc(s_whi, 1)

            in_hi(0)
            for step in range(TT + 1):
                if step < TT:
                    modulate(0, step)
                if step >= 1:
                    act.wait_ge(s_hTa, step)
                    act.wait_ge(s_hTd, step)
                    cols_ = slice((step - 1) * P, step * P)
                    fn(hT_hi[:, :, cols_], stages[0]["hT"][:, :, cols_], ACT.Copy).then_inc(s_hhi, 1)
            in_hi(1)
            act.wait_ge(s_lam, 1)
            fn(lam[:, 1, :], lam[:, 0, :], ACT.Exp, scale=-1.0).then_inc(s_lamE, 1)
            for q in range(2 * KD):
                if q >= 1 and q + 1 < 2 * KD:
                    in_hi(q + 1)
                if q < KD:
                    continue
                act.wait_ge(s_z, q + 1)
                b = 2 * (q % 2)
                fn(seg(G[:, q - KD, :], 0), wide[:, b, :], ACT.Gelu_apprx_tanh)
                fn(seg(G[:, q - KD, :], 1), wide[:, b + 1, 0:TC], ACT.Gelu_apprx_tanh).then_inc(s_gelu, 1)
            for r, (d, half) in enumerate(rounds):
                for jj in range(4):
                    n, u = 4 * half + jj, 4 * r + jj
                    if r >= 1:
                        act.wait_ge(s_scan, u - 3)
                    elif jj == 0:
                        act.wait_ge(s_lam, 3)
                    for g, banks, dst in ((0, turned, RT), (1, duo, IT)):
                        act.wait_ge(s_gmm, 2 * u + g + 1)
                        bias = pB[:, B_GB + (2 * d + g) * KD + n:B_GB + (2 * d + g) * KD + n + 1]
                        fn(seg(dst[:, jj, :], 0), banks[:, 0, :], ACT.Sigmoid, bias=bias)
                        fn(seg(dst[:, jj, :], 1), banks[:, 1, 0:TC], ACT.Sigmoid, bias=bias).then_inc(s_sig, 1)
                act.wait_ge(s_lam, 2)
                for jj in range(4):
                    n, u = 4 * half + jj, 4 * r + jj
                    act.wait_ge(s_sig, 2 * u + 2)
                    at = d * KD + n
                    chain.step(fn(A[:, jj, 0:W], RT[:, jj, 0:W], ACT.Exp, scale=lam[:, 2, at:at + 1]))
                    fn(RT[:, jj, 0:W], RT[:, jj, 0:W], ACT.Tanh, scale=lam[:, 3, at:at + 1]).then_inc(s_tanh, 1)
                for jj in range(4):
                    u = 4 * r + jj
                    act.wait_ge(s_v, u + 1)
                    fn(RT[:, jj, 0:W], RT[:, jj, 0:W], ACT.Sqrt).then_inc(s_sqrt, 1)

            def norm_and_logits(lay):
                s, n = 2 * lay + 1, FFT[lay]
                for step in range(n + 2):
                    if step < n:
                        squares(s, step)
                    if 1 <= step <= n:
                        modulate(s, step - 1)
                    if step >= 2:
                        t = step - 2
                        act.wait_ge(s_log, LG0[lay] + t + 1)
                        if LG0[lay] + t:
                            act.wait_ge(s_logt, LG0[lay] + t)
                        fn(logit_parts[:], duo[:, 0, 0:P], ACT.Copy).then_inc(s_logc, 1)

            def affinities(lay):
                act.wait_ge(s_sub, lay + 1)
                fn(aff[:, 0:FFT[lay], :], aff[:, 0:FFT[lay], :], ACT.Exp).then_inc(s_aexp, 1)

            def experts(lay):
                M = CAP[lay]

                def hi(e, j):
                    act.wait_ge(landed[j], e * 16 + 16 * (LANDED0[lay][j] + 1))
                    act.wait_ge(s_wdone[lay], e * NS + (j + 1))
                    fn(w_hi[:, j % NW, :], chunk_at(j), ACT.Copy).then_inc(s_hi[lay], 1)

                def product(e, j):
                    act.wait_ge(s_wdone[lay], e * NS + (j + 1 + NW))

                def low_rows(e, h, s):
                    product(e, 4 * h + 2 * s + 1)
                    act.wait_ge(s_us if s == 0 else s_gs, e * 2 + (h + (2 if s == 0 else 3)))
                    fn(lo_rows[:], wide[M:2 * M, 2 * h + s, :], ACT.Copy).then_inc(s_lot, 1)

                def silu(e, h):
                    act.wait_ge(s_hid[lay], e * 2 + (h + 2))
                    if lay == 0:
                        product(e, 4 * h + 1)
                        fn(sg[0:M, :], wide[0:M, 2 * h, :], ACT.Silu).then_inc(s_silu[lay], 1)
                    else:
                        act.wait_ge(s_gs, e * 2 + (h + 3))
                        fn(sg[0:M, :], sg[0:M, :], ACT.Silu).then_inc(s_silu[lay], 1)

                def hidden(e, h):
                    act.wait_ge(s_hidtr[lay], e * 2 + (h + 1))
                    fn(hidT[:, h, :, 0:M], turned[:, h, 0:4 * M].rearrange("p (k m) -> p k m", k=4),
                       ACT.Copy).then_inc(s_hidT[lay], 1)

                def output_rows(e):
                    if lay == 0:
                        return
                    act.wait_ge(used[NCH - 1], e + (USED0[lay][NCH - 1] + 1))
                    act.wait_ge(s_scat[lay], e * 16 + 32)
                    fn(ye[0:M, BANK:D], duo[M:2 * M, 1, :], ACT.Copy).then_inc(s_yhi, 1)

                def body(e, last):
                    hi_next = (lambda j: None) if last else (lambda j: hi(e + 1, j))
                    if lay == 0:
                        hi(e, 4), hi(e, 5), silu(e, 0), hi(e, 6), hi(e, 7)
                        hi_next(0), hi_next(1), silu(e, 1), hidden(e, 0), hi_next(2), hi_next(3), hidden(e, 1)
                    else:
                        hi(e, 4), hi(e, 5), low_rows(e, 0, 0), hi(e, 6), silu(e, 0), hi(e, 7), low_rows(e, 0, 1)
                        hi_next(0), hi_next(1), low_rows(e, 1, 0), hidden(e, 0), hi_next(2), silu(e, 1)
                        hi_next(3), low_rows(e, 1, 1), hidden(e, 1), output_rows(e)

                act.wait_ge(s_wdone[lay], NW)
                for j in range(NW):
                    hi(0, j)
                with act.Fori(0, E - 1) as e:
                    body(e, False)
                body(E - 1, True)

            norm_and_logits(0)
            affinities(0)
            experts(0)
            norm(2)
            for t in range(TT):
                b = 2 * (t % 2)
                act.wait_ge(s_mz, t + 1)
                if t >= 2:
                    act.wait_ge(s_cqtr, t - 1)
                if t < TLT:
                    fn(cqn[:, t % 2, 0:QL], wide[:, b, 0:QL], ACT.Square, accum_out=mx[:, 0, t:t + 1])
                chain.step(fn(cqn[:, t % 2, QL:QL + KVL], wide[:, b + 1, 0:KVL], ACT.Square, accum_out=mx[:, 1, t:t + 1]))
                if t < TLT:
                    fn(mx[:, 2, t:t + 1], mx[:, 0, t:t + 1], ACT.Sqrt, bias=eps[:, 0:1], scale=1.0 / QL)
                fn(mx[:, 3, t:t + 1], mx[:, 1, t:t + 1], ACT.Sqrt, bias=eps[:, 0:1], scale=1.0 / KVL).then_inc(s_mzs, 1)
            with act.Fori(0, NG) as g:
                for t in range(TT):
                    act.wait_ge(s_ktr, g * 6 + (t + 1))
                    fn(k_hi[:, :, t * P:(t + 1) * P], turned[0:QK, 1, :].rearrange("p (h n) -> p h n", h=HG),
                       ACT.Copy).then_inc(s_khi, 1)
                for t in range(TLT):
                    act.wait_ge(s_qtr, g * 4 + (t + 1))
                    fn(q_hi[:, :, t * P:(t + 1) * P], turned[0:QK, 0, :].rearrange("p (h n) -> p h n", h=HG),
                       ACT.Copy, scale=SCALE).then_inc(s_qhi, 1)
                for u in range(HG * TLT + LAG):
                    if u >= LAG:
                        w, hh = divmod(u - LAG, 2)
                        act.wait_ge(s_ptr, g * 32 + (2 * (u - LAG) + 1))
                        if hh == 0 and w >= 2:
                            act.wait_ge(s_av, g * 8 + (w - 1))
                        fn(PT[:, w % 2, hh, 0:4, :], turned[:, 0, :].rearrange("p (k n) -> p k n", k=4),
                           ACT.Copy).then_inc(s_PTa, 1)
                    if u < HG * TLT:
                        b = 2 * (u % 2)
                        act.wait_ge(s_max, g * 16 + (u + 1))
                        if u >= LAG:
                            act.wait_ge(s_ptr, g * 32 + (2 * (u - LAG) + 2))
                        fn(prob[:, u % LAG, :], wide[:, b:b + 2, :].rearrange("p a n -> p (a n)")[:, 0:T], ACT.Exp,
                           bias=asum[:, 0, u % 4:u % 4 + 1], accum_out=asum[:, 1, u % 4:u % 4 + 1]).then_inc(s_exp, 1)
            norm_and_logits(1)
            affinities(1)
            experts(1)
            for t in range(TLT):
                act.wait_ge(s_x[t], 48)
                chain.step(fn(xo_f[:, t, :], x_f[:, t, :], ACT.Square, accum_out=stat[:, 0, t:t + 1]))
                fn(stat[:, 1, t:t + 1], stat[:, 0, t:t + 1], ACT.Sqrt, bias=eps[:, 0:1], scale=1.0 / D).then_inc(s_rms, 1)

        @block.vector
        def _(dve):
            v = nc.vector
            chain = Chain(dve, s_dve)
            marked = [0]

            def mark(s_, n):
                v.memset(marks[:, marked[0]:marked[0] + 1], 1.0).then_inc(s_, n)
                marked[0] += 1

            def normed_tile(s, t):
                dve.wait_ge(s_rms, N0[s] + t + 1)
                chain.step(v.reciprocal(stat[:, 2, t:t + 1], stat[:, 1, t:t + 1]))
                v.tensor_scalar(stages[s]["xn"][:, t, :], stages[s]["x"][:, t, :], stat[:, 2, t:t + 1], None,
                                ALU.mult).then_inc(s_xn, 1)

            def modulate(s, t):
                a = 2 * s + (0 if t < TLT else 1)
                dve.wait_ge(s_xtr, 2 * (N0[s] + t) + 2)
                for k in range(4, 8):
                    ins = v.tensor_scalar(stages[s]["hT"][:, k, t * P:(t + 1) * P], turned[:, 1, (k - 4) * P:(k - 3) * P],
                                          cols[:, a, k:k + 1], cols[:, 7 + a, k:k + 1], ALU.mult, ALU.add)
                ins.then_inc(s_hTd, 1)

            def norm(s):
                n = stages[s]["n"]
                for step in range(n + 1):
                    if step < n:
                        normed_tile(s, step)
                    if step >= 1:
                        modulate(s, step - 1)

            def ada_read(i):
                name = ("ada", i, KD - 1)
                dve.wait_ge(used[place[name][0]], place[name][1])
                dve.wait_ge(s_bias, 32 * (i + 1))
                for n in range(4):
                    rows = slice(32 * n, 32 * n + 2)
                    ins = v.tensor_tensor(modbias[rows, i % 2, :], mod_banks(i)[rows, 0, :], modbias[rows, i % 2, :], ALU.add)
                ins.then_inc(s_modev, 1)

            def columns(a, scale, shift, gain):
                chain.step(v.scalar_tensor_tensor(cols[:, a, :], scale, 1.0, gain, ALU.add, ALU.mult))
                chain.step(v.tensor_copy(cols[:, 7 + a, :], shift))

            def mod_columns(i):
                lay, g = divmod(i, 3)
                dve.wait_ge(s_modtr, i + 1)
                mc = modc[lay]
                for v_ in range(2):
                    at = v_ * 48 + 16 * g
                    chain.step(v.tensor_copy(
                        mc[:, at:at + 16].rearrange("p (n j) -> p n j", n=4),
                        mod_banks(i)[:, 1, :].rearrange("p (j n w) -> p n j w", j=4, n=4)[:, :, :, v_]))
                s = {0: 0, 2: 1, 3: 2, 5: 3}.get(i)
                if s is not None:
                    is_ffn = s % 2
                    gain = pA[:, 16 + 16 * is_ffn + lay * KD:16 + 16 * is_ffn + (lay + 1) * KD]
                    for v_ in range(1 if s == 3 else 2):
                        at = v_ * 48 + (3 * KD if is_ffn else 0)
                        columns(2 * s + v_, mc[:, at + KD:at + 2 * KD], mc[:, at:at + KD], gain)
                mark(s_modcol, 1)

            dve.wait_ge(s_const, NCONST)
            dve.wait_ge(s_partr, 1)
            v.tensor_copy(pA[:], turned[:, 0, 0:48]).then_inc(s_pcol, 1)
            dve.wait_ge(s_pcol, 1)
            for t in range(TT):
                normed_tile(0, t)
            ada_read(0)
            mod_columns(0)

            def in_lo(q):
                dve.wait_ge(s_whi, q + 1)
                v.tensor_tensor(w_lo0[:, q % 2], in_weights(q), w_hi0[:, q % 2].bitcast(F32), ALU.subtract).then_inc(s_wlo, 1)

            for step in range(TT + 1):
                if step < TT:
                    modulate(0, step)
                if step == 1:
                    in_lo(0)
                if step >= 1:
                    dve.wait_ge(s_hhi, step)
                    cols_ = slice((step - 1) * P, step * P)
                    v.tensor_tensor(hT_lo[:, :, cols_], stages[0]["hT"][:, :, cols_], hT_hi[:, :, cols_].bitcast(F32),
                                    ALU.subtract).then_inc(s_hlo, 1)
            dve.wait_ge(s_partr, 2)
            v.tensor_copy(pB[:, 0:NB], wide[:, 3, 0:NB]).then_inc(s_pcol, 1)

            dve.wait_ge(s_pcol, 2)
            lm = pB[:, B_LAM:B_LAM + 16]
            chain.step(v.tensor_scalar(lam[:, 4, :], lm, -1.0, None, ALU.mult))
            v.tensor_tensor(lam[:, 0, :], lm, lam[:, 4, :], ALU.max).then_inc(s_lam, 1)

            def convolve(n):
                ub = gmix[:, n % 2, :]
                b = 2 * (n % 2)
                dve.wait_ge(s_z, n + 1)
                v.tensor_copy(ub[:, PADL:PADL + TL], wide[:, b, :])
                v.tensor_copy(ub[:, CX + PADL:CX + PADL + TC], wide[:, b + 1, 0:TC]).then_inc(s_ucopy, 1)
                dve.wait_ge(s_ucopy, n + 1)
                tap = lambda j: pB[:, B_CONV + j * KD + n:B_CONV + j * KD + n + 1]
                chain.step(v.tensor_scalar(XC[:, n, 0:W], ub[:, 0:W], tap(0), pB[:, B_CB + n:B_CB + n + 1], ALU.mult, ALU.add))
                for j in range(1, CONV):
                    ins = v.scalar_tensor_tensor(XC[:, n, 0:W], ub[:, j:j + W], tap(j), XC[:, n, 0:W], ALU.mult, ALU.add)
                    if j < CONV - 1:
                        chain.step(ins)
                ins.then_inc(s_xc, 1)

            for q in range(KD):
                in_lo(q + 1)
                convolve(q)
            dve.wait_ge(s_lamE, 1)
            e_, s_, s2, acc = lam[:, 1, :], lam[:, 5, :], lam[:, 6, :], lam[:, 7, :]
            chain.step(v.tensor_scalar(acc, e_, 2.0, None, ALU.add))
            chain.step(v.reciprocal(s2, acc))
            chain.step(v.tensor_tensor(s_, e_, s2, ALU.mult))
            chain.step(v.tensor_tensor(s2, s_, s_, ALU.mult))
            chain.step(v.tensor_scalar(acc, s2, 2.0 / 17, 2.0 / 15, ALU.mult, ALU.add))
            for odd in (13, 11, 9, 7, 5, 3, 1):
                chain.step(v.tensor_tensor(acc, acc, s2, ALU.mult))
                chain.step(v.tensor_scalar(acc, acc, 2.0 / odd, None, ALU.add))
            chain.step(v.tensor_tensor(acc, acc, s_, ALU.mult))
            chain.step(v.scalar_tensor_tensor(acc, lam[:, 4, :], 0.0, acc, ALU.max, ALU.add))
            v.tensor_scalar(lam[:, 2, :], acc, -LRU_C, None, ALU.mult)
            v.tensor_scalar(lam[:, 3, :], acc, LRU_C, None, ALU.mult).then_inc(s_lam, 1)
            for q in range(KD, 2 * KD):
                if q + 1 < 2 * KD:
                    in_lo(q + 1)
                for what, *at in side[q - 1]:
                    if what == "ada" and at[1] == KD - 1:
                        ada_read(at[0])
                        mod_columns(at[0])
            dve.wait_ge(s_z, 2 * KD)
            v.memset(areaC[:, :, TL:CX], 0.0).then_inc(s_lam, 1)

            for r, (d, half) in enumerate(rounds):
                for jj in range(4):
                    u = 4 * r + jj
                    dve.wait_ge(s_tanh, u + 1)
                    if u:
                        dve.wait_ge(s_v, u)
                    else:
                        dve.wait_ge(s_xc, KD)
                    sq = gmix[:, 0, 0:W]
                    chain.step(v.tensor_tensor(sq, A[:, jj, 0:W], A[:, jj, 0:W], ALU.mult))
                    v.scalar_tensor_tensor(RT[:, jj, 0:W], sq, 1.0, RT[:, jj, 0:W], ALU.add, ALU.mult).then_inc(s_v, 1)
                for jj in range(4):
                    n, u = 4 * half + jj, 4 * r + jj
                    dve.wait_ge(s_sqrt, u + 1)
                    dve.wait_ge(s_ix, u + 1)
                    chain.step(v.tensor_tensor(IT[:, jj, 0:W], RT[:, jj, 0:W], IT[:, jj, 0:W], ALU.mult))
                    dst = Y[:, n, :] if d == 0 else gmix[:, 1, :]
                    a, x_in = A[:, jj, :], IT[:, jj, :]
                    if d == 0:
                        chain.step(v.tensor_tensor_scan(dst[:, CX:W], a[:, CX:W], x_in[:, CX:W], 0.0, ALU.mult, ALU.add))
                        v.tensor_tensor_scan(dst[:, 0:TL], a[:, 0:TL], x_in[:, 0:TL], dst[:, W - 1:W],
                                             ALU.mult, ALU.add).then_inc(s_scan, 1)
                    else:
                        back = lambda ap, i: seg(ap, i)[:, ::-1]
                        chain.step(v.tensor_tensor_scan(back(dst, 1), back(a, 1), back(x_in, 1), 0.0, ALU.mult, ALU.add))
                        v.tensor_tensor_scan(back(dst, 0), back(a, 0), back(x_in, 0), dst[:, CX:CX + 1],
                                             ALU.mult, ALU.add).then_inc(s_scan, 1)
                        dve.wait_ge(s_scan, u + 1)
                        v.tensor_tensor(seg(Y[:, n, :], 0), seg(Y[:, n, :], 0), seg(dst, 0), ALU.add)
                        v.tensor_tensor(seg(Y[:, n, :], 1), seg(Y[:, n, :], 1), seg(dst, 1), ALU.add).then_inc(s_ysum, 1)
                        dve.wait_ge(s_ysum, 4 * half + jj + 1)
                if r >= 1:
                    mod_columns(r + 2)
                if r <= 2:
                    ada_read(r + 3)

            def residual(lay, s, t):
                dve.wait_ge(s_o[lay], t + 1)
                if lay == 0:
                    dve.wait_ge(s_x[t], 16)
                if t == 0:
                    dve.wait_ge(s_gmix[lay], 32 if lay == 0 else 16)
                g_ = gmix1[:] if lay else gmix[:, 0 if t < TLT else 1, :]
                b = 2 * (t % 2)
                o = stages[s]["xn"][:, t, :]
                chain.step(v.tensor_tensor(o, wide[:, b:b + 2, :].rearrange("p a n -> p (a n)"), g_, ALU.mult))
                v.tensor_tensor(stages[s]["x"][:, t, :], stages[s]["x"][:, t, :], o, ALU.add).then_inc(s_x1[lay], 1)

            def open_experts(lay):
                M, s = CAP[lay], 2 * lay + 1
                dve.wait_ge(s_st[lay], 16 * FFT[lay])
                dve.wait_ge(s_nst[lay], 16 * FFT[lay])
                parts = [(0, CAPL, 2 * s)] + ([(CAPL, M, 2 * s + 1)] if lay == 0 else [])
                made = []
                for lo, hi, a in parts:
                    for dst, at in ((mod_a, a), (mod_b, 7 + a)):
                        made.append(v.tensor_copy(dst[:, :, lo:hi], cols[:, at, :].unsqueeze(2).to_broadcast([P, KD, hi - lo])))
                made[-1].then_inc(s_hid[lay], 2)
                mark(s_hidT[lay], 2)
                mark(s_ye[lay], 1)
                if lay == 1:
                    mark(s_gs, 2)
                    mark(s_us, 2)
                for j in range(RING, NCH):
                    mark(used[j], 1)
                mark(s_wdone[lay], NW)

            def choose(lay):
                n_t, M = FFT[lay], CAP[lay]
                dve.wait_ge(s_logr, LG0[lay] + n_t)
                lg = logits[:, 0:n_t, :]
                af = aff[:, 0:n_t, :]
                over = lambda a: a.unsqueeze(2).to_broadcast([P, n_t, E])
                chain.step(v.tensor_reduce(mx[:, 0, 0:n_t], lg, AX_X, ALU.max))
                v.tensor_tensor(af, lg, over(mx[:, 0, 0:n_t]), ALU.subtract).then_inc(s_sub, 1)
                dve.wait_ge(s_aexp, lay + 1)
                chain.step(v.tensor_reduce(mx[:, 1, 0:n_t], af, AX_X, ALU.add))
                chain.step(v.reciprocal(mx[:, 2, 0:n_t], mx[:, 1, 0:n_t]))
                rs = mx[:, 2, 0:n_t].unsqueeze(2).to_broadcast([P, n_t, E])
                ins = v.tensor_tensor(aff2[:, :, 0:E], aff[:, 0:TLT, :], rs[:, 0:TLT, :], ALU.mult)
                if lay == 0:
                    ins = v.tensor_tensor(aff2[:, 0:TT - TLT, 32:48], aff[:, TLT:TT, :], rs[:, TLT:TT, :], ALU.mult)
                ins.then_inc(s_aff, 1)
                open_experts(lay)
                dve.wait_ge(s_afft, lay + 1)
                chain.step(v.tensor_copy(affT[:], turned[0:48, 0, :]))
                for r in range(CAPL // 8):
                    at = slice(8 * r, 8 * r + 8)
                    chain.step(v.max(top_v[:, at], affT[:]))
                    chain.step(v.max_index(top_i[:, at], top_v[:, at], affT[:]))
                    if r < CAPL // 8 - 1:
                        chain.step(v.match_replace(affT[:], top_v[:, at], affT[:], -1.0))
                chain.step(v.tensor_copy(top_f[:], top_i[:]))
                v.tensor_copy(turn_in[:, 0, 0:CAPL], top_f[0:E, :])
                ins = v.tensor_copy(turn_in[:, 1, 0:CAPL], top_v[0:E, :])
                if lay == 0:
                    v.tensor_scalar(turn_in[:, 0, CAPL:M], top_f[32:32 + E, 0:CAPC], float(TL), None, ALU.add)
                    ins = v.tensor_copy(turn_in[:, 1, CAPL:M], top_v[32:32 + E, 0:CAPC])
                ins.then_inc(s_top, 1)
                dve.wait_ge(s_topt, lay + 1)
                v.tensor_copy(idx_t[0:M, :], duo[0:M, 1, 0:E])
                chain.step(v.tensor_copy(gate_t[0:M, :], duo[0:M, 1, E:2 * E]))
                mark(s_sel, 1)

            def experts(lay):
                M = CAP[lay]
                loop_chain = Chain(dve, s_dloop[lay])
                dve.wait_ge(s_hid[lay], 2)

                def lo(e, j):
                    dve.wait_ge(s_hi[lay], e * NS + (j + 1))
                    v.tensor_tensor(w_lo[:, j % NW, :], chunk_at(j), w_hi[:, j % NW, :].bitcast(F32),
                                    ALU.subtract).then_inc(used[j], 1)

                def rows(e, part):
                    dve.wait_ge(s_xgtr[lay], e * 2 + (part + 1))
                    k = slice(4 * part, 4 * part + 4)
                    hi_, lo_ = xs[:, k, 0:M], xs[:, k, M:2 * M]
                    loop_chain.step(v.tensor_tensor(h32[:, k, 0:M], turned[:, part, 0:4 * M].rearrange("p (k m) -> p k m", k=4),
                                                    mod_a[:, k, 0:M], ALU.mult))
                    loop_chain.step(v.tensor_tensor(h32[:, k, 0:M], h32[:, k, 0:M], mod_b[:, k, 0:M], ALU.add))
                    loop_chain.step(v.tensor_copy(hi_, h32[:, k, 0:M]))
                    v.tensor_tensor(lo_, h32[:, k, 0:M], hi_.bitcast(F32), ALU.subtract).then_inc(s_xgT[lay], 1)

                def gate_sum(e, h):
                    if lay == 1:
                        dve.wait_ge(s_lot, e * 4 + (2 * h + 1))
                        dve.wait_ge(s_hid[lay], e * 2 + (h + 2))
                        v.tensor_tensor(sg[0:M, :], wide[0:M, 2 * h, :], lo_rows[:], ALU.add).then_inc(s_gs, 1)

                def hidden(e, h):
                    up = wide[0:M, 2 * h + 1, :]
                    if h == 1:
                        dve.wait_ge(s_hidtr[lay], e * 2 + 1)
                    if lay == 1:
                        dve.wait_ge(s_lot, e * 4 + (2 * h + 2))
                        v.tensor_tensor(hid[0:M, :], up, lo_rows[:], ALU.add).then_inc(s_us, 1)
                        dve.wait_ge(s_us, e * 2 + (h + 3))
                        up = hid[0:M, :]
                    else:
                        dve.wait_ge(s_wdone[lay], e * NS + (4 * h + 4 + NW))
                    dve.wait_ge(s_silu[lay], e * 2 + (h + 1))
                    v.tensor_tensor(hid[0:M, :], up, sg[0:M, :], ALU.mult).then_inc(s_hid[lay], 1)

                def body(e, last):
                    loop_chain.n = e * 7 + 6
                    lo_next = (lambda j: None) if last else (lambda j: lo(e + 1, j))
                    lo(e, 4), lo(e, 5), gate_sum(e, 0), lo(e, 6), lo(e, 7), hidden(e, 0)
                    dve.wait_ge(s_ye[lay], e + 1)
                    loop_chain.step(v.tensor_copy(gate_c[0:M, 0:1], gate_t[0:M, bass.ds(e, 1)]))
                    lo_next(0), lo_next(1), gate_sum(e, 1), lo_next(2), lo_next(3), hidden(e, 1)
                    if not last:
                        rows(e + 1, 0)
                        rows(e + 1, 1)
                    dve.wait_ge(used[NCH - 1], e + (USED0[lay][NCH - 1] + 1))
                    dve.wait_ge(s_scat[lay], e * 16 + 32)
                    if lay == 0:
                        v.scalar_tensor_tensor(ye[0:M, :], duo[0:M, :, :].rearrange("p a n -> p (a n)"), gate_c[0:M, 0:1],
                                               gffn[0:M, :], ALU.mult, ALU.mult).then_inc(s_ye[lay], 1)
                    else:
                        v.scalar_tensor_tensor(ye[0:M, 0:BANK], duo[0:M, 0, :], gate_c[0:M, 0:1], gffn[0:M, 0:BANK],
                                               ALU.mult, ALU.mult)
                        dve.wait_ge(s_yhi, e + 1)
                        v.scalar_tensor_tensor(ye[0:M, BANK:D], ye[0:M, BANK:D], gate_c[0:M, 0:1], gffn[0:M, BANK:D],
                                               ALU.mult, ALU.mult).then_inc(s_ye[lay], 1)

                lo(0, 0), lo(0, 1), lo(0, 2), rows(0, 0), rows(0, 1), lo(0, 3)
                dve.wait_ge(s_scat[lay], 32)
                with dve.Fori(0, E - 1) as e:
                    body(e, False)
                body(E - 1, True)

            def residual_norm(lay):
                s, n = 2 * lay + 1, FFT[lay]
                for step in range(n + 3):
                    if step < n:
                        residual(lay, s, step)
                        normed_tile(s, step)
                    if 1 <= step <= n:
                        modulate(s, step - 1)
                    if step >= 3:
                        t = step - 3
                        dve.wait_ge(s_logt, LG0[lay] + t + 1)
                        v.tensor_reduce(logits[:, t, :], duo[:, 1, 0:P].rearrange("p (j e) -> p e j", j=4)[:, 0:E, :],
                                        AX_X, ALU.add).then_inc(s_logr, 1)

            residual_norm(0)
            choose(0)
            experts(0)

            norm(2)

            def turn_angles(dst, src, n, t):
                x1 = src.rearrange("p n (a h f) -> p n a h f", a=2, h=2)[:, :, :, 0, :]
                x2 = src.rearrange("p n (a h f) -> p n a h f", a=2, h=2)[:, :, :, 1, :]
                o1 = dst.rearrange("p n (a h f) -> p n a h f", a=2, h=2)[:, :, :, 0, :]
                o2 = dst.rearrange("p n (a h f) -> p n a h f", a=2, h=2)[:, :, :, 1, :]
                cos, sin = [ropes[:, t, i, :].rearrange("p (a f) -> p a f", a=2).unsqueeze(1).to_broadcast([P, n, 2, FQ]) for i in range(2)]
                tmp = [rtmp[:, j, 0:n * 2 * FQ].rearrange("p (n a f) -> p n a f", n=n, a=2) for j in range(4)]
                for j, (a_, b_) in enumerate(((x1, cos), (x2, sin), (x1, sin), (x2, cos))):
                    ins = v.tensor_tensor(tmp[j], a_, b_, ALU.mult)
                return ins, [(o1, tmp[0], tmp[1], ALU.subtract), (o2, tmp[2], tmp[3], ALU.add)]

            dve.wait_ge(s_rope, 16)
            for step in range(TT + 1):
                if step < TT:
                    t = step
                    b = 2 * (t % 2)
                    dve.wait_ge(s_mzs, t + 1)
                    if t:
                        dve.wait_ge(s_cqn, t)
                    if t < TLT:
                        v.reciprocal(lam[:, 4, t:t + 1], mx[:, 2, t:t + 1])
                    chain.step(v.reciprocal(lam[:, 5, t:t + 1], mx[:, 3, t:t + 1]))
                    if t < TLT:
                        v.tensor_scalar(cqn[:, t % 2, 0:QL], wide[:, b, 0:QL], lam[:, 4, t:t + 1], None, ALU.mult)
                    v.tensor_scalar(cqn[:, t % 2, QL:QL + KVL], wide[:, b + 1, 0:KVL], lam[:, 5, t:t + 1], None, ALU.mult)
                    kr = wide[:, b + 1, KVL:KVL + ROPE]
                    if t < TLT:
                        chain.step(v.tensor_copy(kraw[:, t % 2, :], kr))
                        ins, rest = turn_angles(krr[:, t:t + 1, :], kraw[:, t % 2:t % 2 + 1, :], 1, t)
                        chain.step(ins)
                        for o, a_, b_, op in rest:
                            ins = v.tensor_tensor(o, a_, b_, op)
                        ins.then_inc(s_cqn, 1)
                    else:
                        v.tensor_copy(krr[:, t, :], kr).then_inc(s_cqn, 1)
                if step >= 1:
                    t = step - 1
                    dve.wait_ge(s_cqtr, t + 1)
                    for k in range(KQ if t < TLT else 0):
                        v.tensor_scalar(cqT[:, k, t * P:(t + 1) * P], duo[:, 0, k * P:(k + 1) * P],
                                        pB[:, B_QN + k:B_QN + k + 1], None, ALU.mult)
                    for k in range(KKV):
                        ins = v.tensor_scalar(ckvT[:, k, t * P:(t + 1) * P], duo[:, 1, k * P:(k + 1) * P],
                                              pB[:, B_KVN + k:B_KVN + k + 1], None, ALU.mult)
                    ins.then_inc(s_cqT, 1)
            dve.wait_ge(s_cqT, TT)
            for s_, n in ((s_qtok, 2), (s_qT, 1), (s_ktok, 2), (s_kT, 1), (s_exp, 2), (s_PTa, 1), (s_PTd, 1), (s_OT, 2)):
                mark(s_, n)
            loop_chain = Chain(dve, s_dloop[2])
            with dve.Fori(0, NG) as g:
                loop_chain.n = g * TLT
                for step in range(TT + 1):
                    if step < TT:
                        t = step
                        dve.wait_ge(s_kv, g * 6 + (t + 1))
                        if t >= 2:
                            dve.wait_ge(s_ktr, g * 6 + (t - 1))
                        kv4 = duo[:, t % 2, :].rearrange("p (h n) -> p h n", h=HG)
                        v.tensor_copy(ktok[:, t % 2, :, 0:NOPE], kv4[:, :, 0:NOPE])
                        v.tensor_copy(ktok[:, t % 2, :, NOPE:QK], krr[:, t:t + 1, :].to_broadcast([P, HG, ROPE]))
                        v.tensor_copy(V[:, t, :, :], kv4[:, :, NOPE:NOPE + VD]).then_inc(s_ktok, 1)
                    if step >= 1:
                        cols_ = slice((step - 1) * P, step * P)
                        dve.wait_ge(s_khi, g * 6 + step)
                        v.tensor_tensor(k_lo[:, :, cols_], turned[0:QK, 1, :].rearrange("p (h n) -> p h n", h=HG),
                                        k_hi[:, :, cols_].bitcast(F32), ALU.subtract).then_inc(s_kT, 1)
                for step in range(TLT + 1):
                    if step < TLT:
                        t = step
                        dve.wait_ge(s_q, g * 4 + (t + 1))
                        dve.wait_ge(s_qtok, g * 4 + (t + 2))
                        if t >= 2:
                            dve.wait_ge(s_qtr, g * 4 + (t - 1))
                        q4 = duo[:, t % 2, 0:HG * QK].rearrange("p (h n) -> p h n", h=HG)
                        v.tensor_copy(qtok[:, t % 2, :, 0:NOPE], q4[:, :, 0:NOPE])
                        ins, rest = turn_angles(qtok[:, t % 2, :, NOPE:QK], q4[:, :, NOPE:QK], HG, t)
                        loop_chain.step(ins)
                        for o, a_, b_, op in rest:
                            ins = v.tensor_tensor(o, a_, b_, op)
                        ins.then_inc(s_qtok, 1)
                    if step >= 1:
                        cols_ = slice((step - 1) * P, step * P)
                        dve.wait_ge(s_qhi, g * 4 + step)
                        v.scalar_tensor_tensor(q_lo[:, :, cols_], turned[0:QK, 0, :].rearrange("p (h n) -> p h n", h=HG), SCALE,
                                               q_hi[:, :, cols_].bitcast(F32), ALU.mult, ALU.subtract).then_inc(s_qT, 1)
                U = HG * TLT

                def pair_out(pair):
                    dve.wait_ge(s_av, g * 8 + (4 * pair + 4))
                    v.tensor_copy(OT[:, bass.ds(g * 2 + pair, 1), :], duo[:, pair:pair + 1, :]).then_inc(s_OT, 1)

                for u in range(U + LAG):
                    if 1 <= u <= U:
                        dve.wait_ge(s_exp, g * 16 + (u + 2))
                        c_ = (u - 1) % 4
                        v.reciprocal(asum[:, 2, c_:c_ + 1], asum[:, 1, c_:c_ + 1]).then_inc(s_rs, 1)
                    if u < U:
                        b = 2 * (u % 2)
                        dve.wait_ge(s_S, g * 16 + (u + 1))
                        v.tensor_reduce(asum[:, 0, u % 4:u % 4 + 1], wide[:, b:b + 2, :].rearrange("p a n -> p (a n)")[:, 0:T],
                                        AX_X, ALU.max, negate=True).then_inc(s_max, 1)
                    if u >= LAG:
                        w, hh = divmod(u - LAG, 2)
                        dve.wait_ge(s_ptr, g * 32 + (2 * (u - LAG) + 2))
                        if hh == 0 and w >= 2:
                            dve.wait_ge(s_av, g * 8 + (w - 1))
                        v.tensor_copy(PT[:, w % 2, hh, 4:TT, :],
                                      turned[:, 1, 0:2 * P].rearrange("p (k n) -> p k n", k=2)).then_inc(s_PTd, 1)
                        if u - LAG == 3 * TLT - 1:
                            pair_out(0)
                pair_out(1)
            residual_norm(1)
            choose(1)
            experts(1)
            dve.wait_ge(s_nf, 16)
            for t in range(TLT):
                dve.wait_ge(s_rms, N0[4] + t + 1)
                chain.step(v.reciprocal(stat[:, 2, t:t + 1], stat[:, 1, t:t + 1]))
                v.scalar_tensor_tensor(xo_f[:, t, :], x_f[:, t, :], stat[:, 2, t:t + 1], nf[:], ALU.mult, ALU.mult).then_inc(s_fin, 1)

        @block.gpsimd
        def _(pool):
            g_ = nc.gpsimd
            g_.memset(ident[:], 0.0).then_inc(s_const, 1)
            pool.wait_ge(s_const, 1)
            g_.affine_select(out=ident[:], in_=ident[:], compare_op=ALU.not_equal, fill=1.0, base=0,
                             pattern=[[-1, P]], channel_multiplier=1).then_inc(s_const, 1)
            g_.memset(eps[:], EPS).then_inc(s_const, 1)
            g_.memset(aff2[:], -1.0).then_inc(s_const, 1)
            g_.memset(gmix[:], 0.0).then_inc(s_const, 1)
            g_.memset(idx_t[:], 0).then_inc(s_const, 1)
            g_.memset(marks[:], 0.0).then_inc(s_const, 1)
            g_.memset(gate_t[:], 0.0).then_inc(s_const, 1)
            g_.memset(stat[:], 1.0).then_inc(s_const, 1)
            g_.memset(modbias[:], 0.0).then_inc(s_const, 1)
            g_.memset(router[:], 0.0).then_inc(s_const, 1)

            def mod_store(i):
                lay, g = divmod(i, 3)
                pool.wait_ge(s_modev, i + 1)
                for v_ in range(2):
                    pool.dma_start(mods[lay, v_, g * MODW:(g + 1) * MODW].rearrange("(n f) -> n f", f=BANK),
                                   modbias[v_:P:32, i % 2, :]).then_inc(s_modst, 16)
                pool.wait_ge(s_modst, 32 * (i + 1))

            mod_store(0)
            mod_store(1)
            mod_store(2)
            for r, (d, half) in enumerate(rounds):
                for jj in range(4):
                    n, u = 4 * half + jj, 4 * r + jj
                    pool.wait_ge(s_sig, 2 * u + 2)
                    pool.wait_ge(s_xc, n + 1)
                    g_.tensor_tensor(IT[:, jj, 0:W], IT[:, jj, 0:W], XC[:, n, 0:W], ALU.mult).then_inc(s_ix, 1)
                if d == 1:
                    for jj in range(4):
                        n = 4 * half + jj
                        pool.wait_ge(s_ysum, n + 1)
                        g_.tensor_tensor(seg(Y[:, n, :], 0), seg(Y[:, n, :], 0), seg(G[:, n, :], 0), ALU.mult)
                        g_.tensor_tensor(seg(Y[:, n, :], 1), seg(Y[:, n, :], 1), seg(G[:, n, :], 1), ALU.mult).then_inc(s_yg, 1)
                if r == 3:
                    pool.wait_ge(s_ix, 16)
                    pool.wait_ge(s_gmm, 32)
                    for t in range(TT):
                        src = x_d[t * P:(t + 1) * P, :] if t < TLT else ctx_d[(t - TLT) * P:(t - TLT + 1) * P, :]
                        pool.dma_start(stages[1]["x"][:, t, :], src).then_inc(s_x[t], 16)
                    pool.wait_ge(s_ysum, KD)
                    for v_ in range(2):
                        pool.dma_start(gmix[:, v_, :], mods[0, v_:v_ + 1, 2 * D:3 * D].to_broadcast([P, D])).then_inc(s_gmix[0], 16)
                if r <= 2:
                    mod_store(r + 3)

            def stores(lay):
                s, n = 2 * lay + 1, FFT[lay]
                for step in range(n + 1):
                    if step < n:
                        pool.wait_ge(s_x1[lay], step + 1)
                        pool.dma_start(stream[step * P:(step + 1) * P, :], stages[s]["x"][:, step, :]).then_inc(s_st[lay], 16)
                    if step >= 1:
                        t = step - 1
                        pool.wait_ge(s_xn, N0[s] + t + 1)
                        pool.dma_start(normed[t * P:(t + 1) * P, :], stages[s]["xn"][:, t, :]).then_inc(s_nst[lay], 16)
                pool.wait_ge(s_st[lay], 16 * n)
                pool.wait_ge(s_nst[lay], 16 * n)

            def experts(lay):
                M = CAP[lay]
                pool.wait_ge(s_aff, lay + 1)
                for v_, lo, hi in ((0, 0, CAPL), (1, CAPL, M)) if lay == 0 else ((0, 0, M // 2), (0, M // 2, M)):
                    pool.dma_start(gffn[lo:hi, :], mods[lay, v_:v_ + 1, 5 * D:6 * D].to_broadcast([hi - lo, D])).then_inc(s_scat[lay], 16)

                def gather(e):
                    b = e % 2
                    g_.tensor_copy(idx_c[0:M, b:b + 1], idx_t[0:M, e:e + 1]).then_inc(s_idxc[lay], 1)
                    pool.wait_ge(s_idxc[lay], e + 1)
                    pool.indirect_dma_start(out=xg[0:M, :], out_offset=None, in_=normed,
                                            in_offset=bass.IndirectOffsetOnAxis(ap=idx_c[0:M, b:b + 1], axis=0)).then_inc(s_gath[lay], 16)

                pool.wait_ge(s_sel, lay + 1)
                gather(0)
                for e in range(E):
                    pool.wait_ge(s_scat[lay], e * 16 + 32)
                    if e + 1 < E:
                        pool.wait_ge(s_xgtr[lay], e * 2 + 2)
                        gather(e + 1)
                    pool.wait_ge(s_ye[lay], e + 2)
                    b = e % 2
                    pool.indirect_dma_start(out=stream, out_offset=bass.IndirectOffsetOnAxis(ap=idx_c[0:M, b:b + 1], axis=0),
                                            in_=ye[0:M, :], in_offset=None, compute_op=ALU.add).then_inc(s_scat[lay], 16)
                pool.wait_ge(s_scat[lay], 32 + 16 * E)

            stores(0)
            experts(0)
            for t in range(TT):
                pool.dma_start(x_b[:, t, :], stream[t * P:(t + 1) * P, :]).then_inc(s_x[t], 16)
            pool.dma_start(gmix1[:], mods[1, 0:1, 2 * D:3 * D].to_broadcast([P, D])).then_inc(s_gmix[1], 16)
            pool.dma_start(ropes[:], rope.rearrange("(t p) i f -> p t i f", p=P)).then_inc(s_rope, 16)
            with pool.Fori(0, NG) as g:
                for u in range(HG * TLT):
                    pool.wait_ge(s_rs, g * 16 + (u + 1))
                    g_.tensor_tensor(prob[:, u % LAG, :], prob[:, u % LAG, :], asum[:, 2, u % 4:u % 4 + 1].to_broadcast([P, T]),
                                     ALU.mult).then_inc(s_pn, 1)
            stores(1)
            experts(1)
            for t in range(TLT):
                pool.dma_start(x_f[:, t, :], stream[t * P:(t + 1) * P, :]).then_inc(s_x[t], 16)
            pool.dma_start(nf[:], norm_final.rearrange("(a d) -> a d", a=1).to_broadcast([P, D])).then_inc(s_nf, 16)
            for t in range(TLT):
                pool.wait_ge(s_fin, t + 1)
                pool.dma_start(out_d[t * P:(t + 1) * P, :], xo_f[:, t, :]).then_inc(s_out, 16)
            pool.wait_ge(s_out, 16 * TLT)


INPUTS = ["x", "c", "ctx", "c_ctx", "ada_w", "ada_b", "norm_mix", "norm_ffn", "norm_final", "lru_w_in", "lru_conv_w",
          "lru_conv_b", "lru_gate_w", "lru_gate_b", "lru_lambda", "lru_w_out", "mla_w_in", "mla_q_norm", "mla_kv_norm",
          "mla_w_uq", "mla_w_ukv", "mla_w_o", "moe_router", "moe_w_up", "moe_w_down"]


def rope_table(tokens, freqs):
    freq = np.float32(ROPE_BASE) ** (-np.arange(freqs, dtype=np.float32) / np.float32(freqs))
    pos = np.stack([np.arange(tokens) // GRID_W, np.arange(tokens) % GRID_W], axis=-1).astype(np.float32)
    ang = (pos[:, :, None] * freq).reshape(tokens, 2 * freqs)
    return np.stack([np.cos(ang), np.sin(ang)], axis=1).astype(np.float32)


def kernel(**inputs):
    import concourse.bacc as bacc
    from concourse.bass_utils import run_bass_kernel_spmd

    nc = bacc.Bacc("TRN2", target_bir_lowering=False, num_devices=1)
    arrays = {name: np.ascontiguousarray(inputs[name]) for name in INPUTS}
    arrays["rope"] = rope_table(inputs["x"].shape[1], 8)
    args = [nc.dram_tensor(name, a.shape, mybir.dt.from_np(a.dtype), kind="ExternalInput").ap() for name, a in arrays.items()]
    out = nc.dram_tensor("out", inputs["x"].shape, F32, kind="ExternalOutput").ap()
    build(nc, *args, out)
    result = run_bass_kernel_spmd(nc, [arrays], core_ids=[0])
    return result.results[0]["out"]
```
